# Optimizing a Trainium2 kernel written in Bass

```python
import jax, jax.numpy as jnp
from jax import lax
import numpy as np

D_MODEL = 1024
BATCH = 1
SEQ = 512
DEPTH = 2
DEC_BATCH = 8
DEC_SEQ = 4
PAST_LEN = 256
PAGE_SIZE = 128

N_EVEN = (DEPTH + 1) // 2
N_ODD = DEPTH // 2
A_WIDTH = D_MODEL // 4
A_KERNEL = 3
DIL_GROUPS = ((128, 1), (512, 4), (2048, 16))
N_GROUPS_B = len(DIL_GROUPS)
HEADS_PER_GROUP = 4
HEAD_DIM = 64
B_QKV = N_GROUPS_B * HEADS_PER_GROUP * HEAD_DIM
B_OUT = HEADS_PER_GROUP * HEAD_DIM
IN_COLS = 3 * A_WIDTH + 3 * B_QKV
MIX_OUT = A_WIDTH + B_OUT
C_WIDTH = D_MODEL
C_KERNEL = 31
N_EXPERT_GROUPS = 4
EXPERTS_PER_GROUP = 8
N_EXPERTS = N_EXPERT_GROUPS * EXPERTS_PER_GROUP
TOP_K_IN_GROUP = 2
D_EXPERT = D_MODEL // 4
RMS_EPS = 1e-6
LN_EPS = 1e-5
NEG_INF = -1e30

kernel_name = "hybrid_shortconv_dilated_conformer_hmoe_step"

def rms_norm(x, g):
    xf = x.astype(jnp.float32)
    y = xf * lax.rsqrt(jnp.mean(xf * xf, axis=-1, keepdims=True) + RMS_EPS)
    return (y * g.astype(jnp.float32)).astype(x.dtype)

def layer_norm(x, g, b):
    xf = x.astype(jnp.float32)
    mu = jnp.mean(xf, axis=-1, keepdims=True)
    var = jnp.mean(jnp.square(xf - mu), axis=-1, keepdims=True)
    y = (xf - mu) * lax.rsqrt(var + LN_EPS) * g.astype(jnp.float32) + b.astype(jnp.float32)
    return y.astype(x.dtype)

def causal_dwconv(x_ext, w):
    c = x_ext.shape[-1]
    return lax.conv_general_dilated(
        x_ext, w[:, None, :].astype(x_ext.dtype), window_strides=(1,), padding='VALID',
        dimension_numbers=('NWC', 'WIO', 'NWC'), feature_group_count=c)

def dilated_attn_prompt(q, k, v, window, dil):
    n, s_len, h, dh = q.shape
    nk = window // dil
    sub_len = s_len // dil
    nb = -(-sub_len // nk)
    lp = nb * nk

    def to_sub(t):
        t = t.reshape(n, sub_len, dil, h, dh).transpose(0, 2, 1, 3, 4)
        t = jnp.pad(t, ((0, 0), (0, 0), (0, lp - sub_len), (0, 0), (0, 0)))
        return t.reshape(n, dil, nb, nk, h, dh)

    def with_prev(t):
        prev = jnp.pad(t, ((0, 0), (0, 0), (1, 0), (0, 0), (0, 0), (0, 0)))[:, :, :-1]
        return jnp.concatenate([prev, t], axis=3)

    qb = to_sub(q)
    kk = with_prev(to_sub(k))
    vv = with_prev(to_sub(v))
    sc = jnp.einsum('brnqhd,brnkhd->brnhqk', qb, kk).astype(jnp.float32) * (HEAD_DIM ** -0.5)
    qi = jnp.arange(nk)[:, None]
    kc = jnp.arange(2 * nk)[None, :]
    band = (kc >= qi) & (kc <= qi + nk)
    blk = jnp.arange(nb)[:, None, None]
    mask = band[None] & ((blk > 0) | (kc[None] >= nk))
    sc = jnp.where(mask[:, None], sc, NEG_INF)
    lse = jax.nn.logsumexp(sc, axis=-1)
    p = jnp.exp(sc - lse[..., None])
    o = jnp.einsum('brnhqk,brnkhd->brnqhd', p.astype(v.dtype), vv)
    o = o.reshape(n, dil, lp, h, dh)[:, :, :sub_len].transpose(0, 2, 1, 3, 4).reshape(n, s_len, h, dh)
    lse = lse.transpose(0, 1, 2, 4, 3).reshape(n, dil, lp, h)[:, :, :sub_len]
    lse = lse.transpose(0, 2, 1, 3).reshape(n, s_len, h)
    return o, lse

def dilated_attn_sample(q, kv_new, kv_buf, window, dil):
    lbuf = kv_buf.shape[1]
    t_len = q.shape[1]
    nk = window // dil
    ext = jnp.concatenate([kv_buf, kv_new.astype(kv_buf.dtype)], axis=1)
    qi = jnp.arange(t_len)[:, None]
    kj = jnp.arange(nk + 1)[None, :]
    idx = lbuf + qi - dil * kj
    valid = (PAST_LEN + qi - dil * kj) >= 0
    g = ext[:, jnp.clip(idx, 0, None)]
    sc = jnp.einsum('nthd,ntkhd->nthk', q, g[:, :, :, 0].astype(q.dtype)).astype(jnp.float32) * (HEAD_DIM ** -0.5)
    sc = jnp.where(valid[None, :, None, :], sc, NEG_INF)
    lse = jax.nn.logsumexp(sc, axis=-1)
    p = jnp.exp(sc - lse[..., None])
    o = jnp.einsum('nthk,ntkhd->nthd', p.astype(q.dtype), g[:, :, :, 1].astype(q.dtype))
    return o, lse

def even_mixer(h, w_in, conv_a_w, w_out, conv_buf, kv_bufs):
    n, t_len, _ = h.shape
    proj = h @ w_in
    cuts = [A_WIDTH, 2 * A_WIDTH, 3 * A_WIDTH, 3 * A_WIDTH + B_QKV, 3 * A_WIDTH + 2 * B_QKV]
    gate_b, gate_c, a_in, q, k, v = jnp.split(proj, cuts, axis=-1)
    u = gate_c * a_in
    ctx = jnp.zeros((n, A_KERNEL - 1, A_WIDTH), u.dtype) if conv_buf is None else conv_buf.astype(u.dtype)
    u_ext = jnp.concatenate([ctx, u], axis=1)
    y_a = gate_b * causal_dwconv(u_ext, conv_a_w)
    new_conv = u_ext[:, -(A_KERNEL - 1):]
    q = q.reshape(n, t_len, N_GROUPS_B, HEADS_PER_GROUP, HEAD_DIM)
    kv = jnp.stack([k, v], axis=2).reshape(n, t_len, 2, N_GROUPS_B, HEADS_PER_GROUP, HEAD_DIM)
    outs, lses, new_kv = [], [], []
    for gi, (window, dil) in enumerate(DIL_GROUPS):
        kv_g = kv[:, :, :, gi]
        if kv_bufs is None:
            o, lse = dilated_attn_prompt(q[:, :, gi], kv_g[:, :, 0], kv_g[:, :, 1], window, dil)
            new_kv.append(kv_g[:, t_len - min(window, t_len):])
        else:
            o, lse = dilated_attn_sample(q[:, :, gi], kv_g, kv_bufs[gi], window, dil)
            new_kv.append(kv_g)
        outs.append(o)
        lses.append(lse)
    alpha = jax.nn.softmax(jnp.stack(lses, axis=0), axis=0)
    y_b = jnp.sum(jnp.stack(outs, axis=0).astype(jnp.float32) * alpha[..., None], axis=0)
    y_b = y_b.astype(h.dtype).reshape(n, t_len, B_OUT)
    y = jnp.concatenate([y_a, y_b], axis=-1) @ w_out
    return y, new_conv, new_kv

def odd_mixer(h, w_pw1, b_pw1, dw_w, dw_b, ln_g, ln_b, w_pw2, b_pw2, conv_buf):
    n = h.shape[0]
    z = h @ w_pw1 + b_pw1
    za, zg = jnp.split(z, 2, axis=-1)
    u = za * jax.nn.sigmoid(zg)
    ctx = jnp.zeros((n, C_KERNEL - 1, C_WIDTH), u.dtype) if conv_buf is None else conv_buf.astype(u.dtype)
    u_ext = jnp.concatenate([ctx, u], axis=1)
    c = causal_dwconv(u_ext, dw_w) + dw_b
    c = jax.nn.silu(layer_norm(c, ln_g, ln_b))
    return c @ w_pw2 + b_pw2, u_ext[:, -(C_KERNEL - 1):]

def hier_moe(h, w_rg, b_rg, w_re, b_re, w_gate, w_up, w_down):
    n, t_len, d = h.shape
    x = h.reshape(-1, d)
    gp = jax.nn.softmax((x @ w_rg + b_rg).astype(jnp.float32), axis=-1)
    g_val, g_idx = lax.top_k(gp, 1)
    el = (x @ w_re + b_re).astype(jnp.float32).reshape(-1, N_EXPERT_GROUPS, EXPERTS_PER_GROUP)
    el_sel = jnp.take_along_axis(el, g_idx[:, :, None], axis=1)[:, 0]
    e_val, e_idx = lax.top_k(jax.nn.softmax(el_sel, axis=-1), TOP_K_IN_GROUP)
    e_w = e_val / jnp.sum(e_val, axis=-1, keepdims=True) * g_val
    expert_id = g_idx * EXPERTS_PER_GROUP + e_idx
    combine = jnp.sum(jax.nn.one_hot(expert_id, N_EXPERTS, dtype=jnp.float32) * e_w[..., None], axis=1)
    hg = jnp.einsum('md,edf->mef', x, w_gate)
    hu = jnp.einsum('md,edf->mef', x, w_up)
    act = jax.nn.silu(hg) * hu * combine[..., None].astype(x.dtype)
    y = jnp.einsum('mef,efd->md', act, w_down)
    return y.reshape(n, t_len, d)

def run_trunk(x, states, p):
    new_a, new_c = [], []
    new_kv = [[] for _ in DIL_GROUPS]
    for layer in range(DEPTH):
        j = layer // 2
        h = rms_norm(x, p['g_mix'][layer])
        if layer % 2 == 0:
            conv_buf = None if states is None else states[0][j]
            kv_bufs = None if states is None else [c[j] for c in states[1]]
            y, a_state, kv_state = even_mixer(h, p['w_in'][j], p['conv_a_w'][j], p['w_out'][j], conv_buf, kv_bufs)
            new_a.append(a_state)
            for gi in range(N_GROUPS_B):
                new_kv[gi].append(kv_state[gi])
        else:
            conv_buf = None if states is None else states[2][j]
            y, c_state = odd_mixer(h, p['w_pw1'][j], p['b_pw1'][j], p['dw_w'][j], p['dw_b'][j],
                                   p['ln_g'][j], p['ln_b'][j], p['w_pw2'][j], p['b_pw2'][j], conv_buf)
            new_c.append(c_state)
        x = x + y
        x = x + hier_moe(rms_norm(x, p['g_ffn'][layer]), p['w_router_group'][layer], p['b_router_group'][layer],
                         p['w_router_expert'][layer], p['b_router_expert'][layer],
                         p['w_gate'][layer], p['w_up'][layer], p['w_down'][layer])
    y = rms_norm(x, p['g_final'])
    return (y, jnp.stack(new_a), jnp.stack(new_kv[0]), jnp.stack(new_kv[1]), jnp.stack(new_kv[2]), jnp.stack(new_c))

def setup_inputs(seed: int = 0) -> dict:
    key = jax.random.key(seed)
    ks = jax.random.split(key, 32)
    f32 = jnp.float32

    def nrm(k, shape, scale):
        return jax.random.normal(k, shape, f32) * scale

    kv_shape = lambda w: (N_EVEN, DEC_BATCH, min(w, PAST_LEN), 2, HEADS_PER_GROUP, HEAD_DIM)
    return {
        'x_prompt': nrm(ks[0], (BATCH, SEQ, D_MODEL), 1.0),
        'x_sample': nrm(ks[1], (DEC_BATCH, DEC_SEQ, D_MODEL), 1.0),
        'state_shortconv': nrm(ks[2], (N_EVEN, DEC_BATCH, A_KERNEL - 1, A_WIDTH), 1.0),
        'cache_kv_w128': nrm(ks[3], kv_shape(DIL_GROUPS[0][0]), 1.0),
        'cache_kv_w512': nrm(ks[4], kv_shape(DIL_GROUPS[1][0]), 1.0),
        'cache_kv_w2048': nrm(ks[5], kv_shape(DIL_GROUPS[2][0]), 1.0),
        'state_conformer': nrm(ks[6], (N_ODD, DEC_BATCH, C_KERNEL - 1, C_WIDTH), 0.5),
        'g_mix': 1.0 + nrm(ks[7], (DEPTH, D_MODEL), 0.02),
        'g_ffn': 1.0 + nrm(ks[8], (DEPTH, D_MODEL), 0.02),
        'g_final': 1.0 + nrm(ks[9], (D_MODEL,), 0.02),
        'w_in': nrm(ks[10], (N_EVEN, D_MODEL, IN_COLS), D_MODEL ** -0.5),
        'conv_a_w': nrm(ks[11], (N_EVEN, A_KERNEL, A_WIDTH), A_KERNEL ** -0.5),
        'w_out': nrm(ks[12], (N_EVEN, MIX_OUT, D_MODEL), MIX_OUT ** -0.5),
        'w_pw1': nrm(ks[13], (N_ODD, D_MODEL, 2 * C_WIDTH), D_MODEL ** -0.5),
        'b_pw1': nrm(ks[14], (N_ODD, 2 * C_WIDTH), 0.02),
        'dw_w': nrm(ks[15], (N_ODD, C_KERNEL, C_WIDTH), C_KERNEL ** -0.5),
        'dw_b': nrm(ks[16], (N_ODD, C_WIDTH), 0.02),
        'ln_g': 1.0 + nrm(ks[17], (N_ODD, C_WIDTH), 0.02),
        'ln_b': nrm(ks[18], (N_ODD, C_WIDTH), 0.02),
        'w_pw2': nrm(ks[19], (N_ODD, C_WIDTH, D_MODEL), C_WIDTH ** -0.5),
        'b_pw2': nrm(ks[20], (N_ODD, D_MODEL), 0.02),
        'w_router_group': nrm(ks[21], (DEPTH, D_MODEL, N_EXPERT_GROUPS), D_MODEL ** -0.5),
        'b_router_group': nrm(ks[22], (DEPTH, N_EXPERT_GROUPS), 0.01),
        'w_router_expert': nrm(ks[23], (DEPTH, D_MODEL, N_EXPERTS), D_MODEL ** -0.5),
        'b_router_expert': nrm(ks[24], (DEPTH, N_EXPERTS), 0.01),
        'w_gate': nrm(ks[25], (DEPTH, N_EXPERTS, D_MODEL, D_EXPERT), D_MODEL ** -0.5),
        'w_up': nrm(ks[26], (DEPTH, N_EXPERTS, D_MODEL, D_EXPERT), D_MODEL ** -0.5),
        'w_down': nrm(ks[27], (DEPTH, N_EXPERTS, D_EXPERT, D_MODEL), D_EXPERT ** -0.5),
    }

def reference(x_prompt, x_sample, state_shortconv, cache_kv_w128, cache_kv_w512, cache_kv_w2048, state_conformer,
              g_mix, g_ffn, g_final, w_in, conv_a_w, w_out, w_pw1, b_pw1, dw_w, dw_b, ln_g, ln_b, w_pw2, b_pw2,
              w_router_group, b_router_group, w_router_expert, b_router_expert, w_gate, w_up, w_down):
    p = {'g_mix': g_mix, 'g_ffn': g_ffn, 'g_final': g_final, 'w_in': w_in, 'conv_a_w': conv_a_w, 'w_out': w_out,
         'w_pw1': w_pw1, 'b_pw1': b_pw1, 'dw_w': dw_w, 'dw_b': dw_b, 'ln_g': ln_g, 'ln_b': ln_b,
         'w_pw2': w_pw2, 'b_pw2': b_pw2, 'w_router_group': w_router_group, 'b_router_group': b_router_group,
         'w_router_expert': w_router_expert, 'b_router_expert': b_router_expert,
         'w_gate': w_gate, 'w_up': w_up, 'w_down': w_down}
    y_prompt, p_sc, p_kv0, p_kv1, p_kv2, p_cf = run_trunk(x_prompt, None, p)
    sample_states = (state_shortconv, [cache_kv_w128, cache_kv_w512, cache_kv_w2048], state_conformer)
    y_sample, s_sc, s_kv0, s_kv1, s_kv2, s_cf = run_trunk(x_sample, sample_states, p)
    return (y_prompt, y_sample, p_sc, p_kv0, p_kv1, p_kv2, p_cf, s_sc, s_kv0, s_kv1, s_kv2, s_cf)


_drawn_inputs = setup_inputs


def setup_inputs(seed=0):
    import zlib

    import numpy as np

    out = dict(_drawn_inputs(seed))
    spreads = {}
    factors = {'g_final': 8.071, 'ln_g': 2.867, 'ln_b': 3.669, 'b_pw2': 4.178, 'b_router_expert': 3.167}
    for name, (base, spread) in spreads.items():
        noise = np.random.default_rng([zlib.crc32(name.encode()), seed]).standard_normal(out[name].shape)
        drawn = base * np.exp(spread * noise) if base else spread * noise
        out[name] = __import__('jax').numpy.asarray(drawn.astype(out[name].dtype))
    for name, factor in factors.items():
        out[name] = (out[name] * factor).astype(out[name].dtype)
    return out
```

```python
from contextlib import ExitStack

import concourse.bass as bass
import numpy as np
from concourse import mybir

F32 = mybir.dt.float32
I32 = mybir.dt.int32
ALU = mybir.AluOpType
ACT = mybir.ActivationFunctionType
AX = mybir.AxisListType

P = 128
D = 1024
KD = D // P
SEQ = 512
DEC_B, DEC_T = 8, 4
SAMPLES = DEC_B * DEC_T
TOK = SEQ + SAMPLES
TILES = 5
HALF = TOK // 2
ROWS = [P, P, P, P, SAMPLES]
GROUPS = 3
HD = 64
SCALE = HD ** -0.5
NEG = -1e30
EXPERTS = 32
EGROUPS = 4
FE = 256
JOB = 64
ASSIGNED = 2 * TOK
XCOLS = ASSIGNED + JOB
MAX_ITERS = 12
MAX_JOBS = 4 * MAX_ITERS
SLOT = 6144
SLOTS = 4
CK = 31
UP = SEQ + CK - 1
US = DEC_T + CK - 1
KEYS = [128, 256, 64]
KOFF = [0, 128, 384]
CACHED = 448
KV = 2 * CACHED + 4 * 256
C_ID, C_TRI, C_ONE, C_MEAN = 0, 128, 256, 384
C_M = [512, 768, 1280]
C_SM = 1792
C_SMALL = C_SM + CACHED + 3 * SAMPLES
(C_IOTA, C_IOTAP, C_E64, C_THR, C_THJ, C_JM, C_JLO, C_HI, C_HI1, C_VALID, C_GI, C_GIP) = (
    C_SMALL, C_SMALL + 32, C_SMALL + 64, C_SMALL + 96, C_SMALL + 104, C_SMALL + 108, C_SMALL + 109,
    C_SMALL + 110, C_SMALL + 111, C_SMALL + 112, C_SMALL + 117, C_SMALL + 121)
C_END = C_SMALL + 125
V_GAIN = 0
V_GPK = 32
V_BP1, V_DWB, V_LNG, V_LNB, V_CA, V_DW = 48, 64, 72, 80, 88, 94
V_RB = V_DW + KD * CK
V_RW = V_RB + 72
V_END = V_RW + 2 * KD * 36
A_HT = 0
A_QK = A_HT + KD * TOK
A_V = A_QK + 12 * TOK
A_GB = A_V + TILES * 768
A_U = A_GB + 2 * TOK
A_YT = A_U + 2 * 514 + 2 * 48
A_QZ = [3840, A_YT + 4 * TOK]
A_AIN = A_YT + 2 * TOK
A_XN0 = A_QK
A_SC = 0
A_PT = 2560
A_QBD = 0
A_PS = 1536
A_PTC = A_PS + 544
A_PTN = A_PTC + 512
B_U = KD * TOK
B_US = B_U + KD * UP
B_C = B_US + KD * DEC_B * US
B_SIG = B_C + KD * TOK
B_WIN = B_SIG + 2 * TOK
B_STD = B_WIN + SAMPLES * CK
M_XN = 0
M_HT = TILES * D
M_XS = 0
M_STG = 9472
M_XJ = M_STG + 2 * D
M_SG = M_XJ + 2 * KD * JOB
M_ACT = M_SG + 2 * P
M_AT = M_ACT + 2 * P
M_Y = M_AT + 2 * P
M_YG = M_Y + 2 * 512
M_R = M_YG
A_BC = M_YG + 4 * D
ARENA = max(A_BC + D, A_QZ[1] + 384)


def program(nc, x_in, w_mix0, kv_in, w_out, w_pw1, w_pw2, w_moe, smalls, consts, rows, st_a, st_c,
            y_out, k_out, v_out, ua_p_out, ua_s_out, uc_p_out, uc_s_out):
    ctx = ExitStack()
    with ctx:
        def sb(name, shape, dt=F32):
            return ctx.enter_context(nc.sbuf_tensor(name, shape, dt))

        def sem(name):
            return ctx.enter_context(nc.semaphore(name))

        xs_dram = nc.dram_tensor("rows_by_expert", (ASSIGNED, D), F32, kind="Internal").ap()
        ys_dram = nc.dram_tensor("expert_outputs", (MAX_JOBS * JOB, D), F32, kind="Internal").ap()
        ring = sb("ring", [P, SLOTS, SLOT])
        X = sb("X", [P, TILES, D])
        cst = sb("cst", [P, C_END])
        sv = sb("sv", [P, V_END])
        ar = sb("ar", [P, ARENA])
        stat = sb("stat", [P, 3, 8])
        vec = sb("vec", [P, 64])
        eps = sb("eps", [P, 2])
        cw = sb("cw", [P, TILES, 2])
        ix = sb("ix", [P, TILES, 4], I32)
        jt = sb("jt", [1, 2 * 64 + 2], I32)
        psum = ctx.enter_context(nc.psum_tensor("psum", [P, 8, 512], F32))

        def view(off, n, pat=None, parts=P, **dims):
            a = ar[0:parts, off:off + n]
            return a.rearrange(pat, **dims) if pat else a

        ident = cst[:, C_ID:C_ID + P]
        ones = cst[:, C_ONE:C_ONE + P]

        def bcast(ap, shape):
            return ap.to_broadcast(shape)

        x_in_done = sem("x_in_done")
        consts_in = sem("consts_in")
        smalls_in = sem("smalls_in")
        proj_w = [sem(f"proj_w{c}") for c in range(4)]
        kv_w = [sem(f"kv_w{c}") for c in range(3)]
        wout_w = sem("wout_w")
        pw1_w = [sem(f"pw1_w{c}") for c in range(4)]
        pw2_w = [sem(f"pw2_w{c}") for c in range(2)]
        state_a_in = sem("state_a_in")
        state_c_in = sem("state_c_in")
        row_in = sem("row_in")
        zeros_made = sem("zeros_made")
        zeros_out = sem("zeros_out")
        outs_done = sem("outs_done")
        dve_link = sem("dve_link")
        act_link = sem("act_link")
        pool_link = sem("pool_link")
        stats_set = sem("stats_set")
        root_ready = sem("root_ready")
        inv_ready = sem("inv_ready")
        xn_dve = sem("xn_dve")
        xn_act = sem("xn_act")
        turned = sem("turned")
        hT_ready = sem("hT_ready")
        proj_done = sem("proj_done")
        proj_kept = sem("proj_kept")
        u_made = sem("u_made")
        ya_made = sem("ya_made")
        qbd_made = sem("qbd_made")
        ss_done = sem("ss_done")
        ss_max = sem("ss_max")
        ss_exp = sem("ss_exp")
        ss_norm = sem("ss_norm")
        ss_turned = sem("ss_turned")
        ss_kept = sem("ss_kept")
        so_done = sem("so_done")
        so_kept = sem("so_kept")
        qz_zero = sem("qz_zero")
        qz_ready = sem("qz_ready")
        s_done = sem("s_done")
        max_ready = sem("max_ready")
        exp_done = sem("exp_done")
        p_ready = sem("p_ready")
        pt_done = sem("pt_done")
        pt_kept = sem("pt_kept")
        o_done = sem("o_done")
        o_kept = sem("o_kept")
        wo_done = sem("wo_done")
        x_updated = sem("x_updated")
        z_done = sem("z_done")
        sig_ready = sem("sig_ready")
        u_ready = sem("u_ready")
        conv_done = sem("conv_done")
        mean_done = sem("mean_done")
        centred = sem("centred")
        squared = sem("squared")
        var_done = sem("var_done")
        std_ready = sem("std_ready")
        scaled = sem("scaled")
        swish_done = sem("swish_done")
        pw2_done = sem("pw2_done")
        y_ready = sem("y_ready")

        class Moe:
            def __init__(self, n):
                self.logits = sem(f"logits{n}")
                self.gshift = sem(f"gshift{n}")
                self.gexp = sem(f"gexp{n}")
                self.eshift = sem(f"eshift{n}")
                self.eexp = sem(f"eexp{n}")
                self.picks = sem(f"picks{n}")
                self.ranks = sem(f"ranks{n}")
                self.table = sem(f"table{n}")
                self.rowed = sem(f"rowed{n}")
                self.places = sem(f"places{n}")
                self.jobs = sem(f"jobs{n}")
                self.scattered = sem(f"scattered{n}")
                self.staged = [sem(f"staged{n}_{b}") for b in range(2)]
                self.st_turned = sem(f"st_turned{n}")
                self.xs_kept = sem(f"xs_kept{n}")
                self.xs_tail = sem(f"xs_tail{n}")
                self.w_in = [sem(f"w_in{n}_{u}") for u in range(SLOTS)]
                self.xj_ready = sem(f"xj_ready{n}")
                self.gu_done = sem(f"gu_done{n}")
                self.sg_ready = sem(f"sg_ready{n}")
                self.act_ready = sem(f"act_ready{n}")
                self.at_done = sem(f"at_done{n}")
                self.at_kept = sem(f"at_kept{n}")
                self.down_done = sem(f"down_done{n}")
                self.y_kept = sem(f"y_kept{n}")
                self.y_out = [sem(f"y_out{n}_{b}") for b in range(2)]
                self.gathered = [sem(f"gathered{n}_{b}") for b in range(4)]
                self.all_out = sem(f"all_out{n}")
                self.combined = sem(f"combined{n}")

        moe = [Moe(0), Moe(1)]
        block = ctx.enter_context(nc.Block())

        qkT = view(A_QK, 12 * TOK, "p (m t) -> p m t", m=12)
        vS = view(A_V, TILES * 768, "p (i c) -> p i c", i=TILES)
        gB = view(A_GB, 2 * TOK, "p (m t) -> p m t", m=2)
        aIn = view(A_AIN, 2 * TOK, "p (m t) -> p m t", m=2)
        uP = view(A_U, 2 * 514, "p (m t) -> p m t", m=2)
        uS = view(A_U + 2 * 514, 96, "p (m b t) -> p m b t", m=2, b=DEC_B)
        yT = view(A_YT, 4 * TOK, "p (m t) -> p m t", m=4)
        qz = [view(A_QZ[h], 384, "p (g t) -> p g t", g=3) for h in range(2)]
        qbd = view(A_QBD, 1536, "p (g r b c) -> p g r b c", g=3, r=2, b=DEC_B)
        cu = view(B_U, KD * UP, "p (k t) -> p k t", k=KD)
        cs = view(B_US, KD * DEC_B * US, "p (k b t) -> p k b t", k=KD, b=DEC_B)
        cT = view(B_C, KD * TOK, "p (k t) -> p k t", k=KD)
        sigm = view(B_SIG, 2 * TOK, "p (h t) -> p h t", h=2)
        std = view(B_STD, TOK)
        brow = view(A_BC, D)
        xsT = view(M_XS, KD * XCOLS, "p (k t) -> p k t", k=KD)
        stg = [view(M_STG + D * b, D) for b in range(2)]
        xj = [view(M_XJ + 512 * b, 512, "p (k t) -> p k t", k=KD) for b in range(2)]
        sg = [view(M_SG + P * b, P) for b in range(2)]
        av = [view(M_ACT + P * b, P) for b in range(2)]
        aT = [view(M_AT + P * b, P) for b in range(2)]
        yj = [view(M_Y + 512 * b, 512) for b in range(2)]
        yg = [view(M_YG + D * b, D) for b in range(4)]

        def hT_of(call):
            return view(M_HT if call % 2 else A_HT, KD * TOK, "p (k t) -> p k t", k=KD)

        def xn_of(call):
            return view(M_XN if call % 2 else A_XN0, TILES * D, "p (i c) -> p i c", i=TILES)

        def wait_residual(eng, call):
            if call == 0:
                eng.wait_ge(x_in_done, 16 * TILES)
            else:
                eng.wait_ge(x_updated, TILES * call)

        def kt_of(b):
            return ring[:, b // 3, KV * (b % 3):KV * (b % 3) + 2 * CACHED].rearrange("p (r t) -> p r t", r=2)

        def v_of(b):
            o = KV * (b % 3) + 2 * CACHED
            return ring[:, b // 3, o:o + 1024].rearrange("p (t c) -> p t c", t=4)

        VT = [(P, 0), (P, 1), (P, 1), (64, 2)]

        @block.sync
        def _(sp):
            sp.dma_start(cst[:, :], consts).then_inc(consts_in, 16)
            sp.dma_start(ring[:, 0, :], w_mix0[0]).then_inc(proj_w[0], 16)
            sp.dma_start(ring[:, 1, :], w_mix0[1]).then_inc(proj_w[1], 16)
            sp.dma_start(ring[:, 2, :], w_mix0[2]).then_inc(proj_w[2], 16)
            sp.wait_ge(zeros_out, 16 * 8)
            sp.dma_start(ring[:, 3, :], w_mix0[3]).then_inc(proj_w[3], 16)
            for c, m in enumerate((6, 12, 17)):
                n = KV * (3 if c < 2 else 2)
                sp.wait_ge(proj_done, m)
                sp.dma_start(ring[:, c, 0:n], kv_in[c, :, 0:n]).then_inc(kv_w[c], 16)
            sp.wait_ge(proj_done, 23)
            sp.dma_start(ring[:, 3, 0:4096], w_out).then_inc(wout_w, 16)

            def experts(n):
                m = moe[n]
                for u in (2, 0, 1, 3) if n == 0 else (2, 3, 0, 1):
                    if n == 0:
                        if u < 3:
                            sp.wait_ge(so_done, 1)
                        else:
                            sp.wait_ge(wo_done, TILES)
                    elif u >= 2:
                        sp.wait_ge(z_done, 2 * KD)
                    else:
                        sp.wait_ge(pw2_done, TILES)
                    sp.dma_start(ring[:, u, :], w_moe[n, u]).then_inc(m.w_in[u], 16)
                sp.wait_ge(m.scattered, 160)
                for t in range(9):
                    if t >= 2:
                        sp.wait_ge(m.st_turned, 2 * (t - 1))
                    r = min(P, ASSIGNED - P * t)
                    sp.dma_start(stg[t % 2][0:r, :], xs_dram[P * t:P * t + r, :]).then_inc(m.staged[t % 2], 16)
                sp.wait_ge(m.jobs, 1)
                iters = sp.value_load(jt[0:1, 128:129], min_val=8, max_val=MAX_ITERS)
                with sp.Fori(1, iters) as it:
                    for u in range(SLOTS):
                        e = sp.value_load(jt[0:1, bass.ds(4 * it + u, 1)], min_val=0, max_val=EXPERTS - 1)
                        sp.wait_ge(m.down_done, 4 * it + (u - 3))
                        sp.dma_start(ring[:, u, :], w_moe[n, bass.ds(e, 1), :, :].rearrange("a p c -> (a p) c")
                                     ).then_inc(m.w_in[u], 16)

            experts(0)
            sp.wait_ge(x_updated, 2 * TILES)
            for c in range(4):
                sp.dma_start(ring[:, c, 0:4096], w_pw1[c]).then_inc(pw1_w[c], 16)
            for c in range(2):
                sp.wait_ge(z_done, 4 * (c + 1))
                sp.dma_start(ring[:, c, 0:4096], w_pw2[c]).then_inc(pw2_w[c], 16)
            experts(1)
            for i in range(TILES):
                sp.wait_ge(y_ready, i + 1)
                sp.dma_start(y_out[P * i:P * i + ROWS[i], :], view(D * i, D, parts=ROWS[i])).then_inc(outs_done, 16)
            sp.wait_ge(outs_done, 16 * (TILES + 7))

        @block.gpsimd
        def _(pool):
            nc.gpsimd.memset(ring[:, 3, 0:D], 0.0).then_inc(zeros_made, 1)
            pool.wait_ge(zeros_made, 1)
            for t in range(8):
                o = EXPERTS * JOB + P * t
                pool.dma_start(ys_dram[o:o + P, :], ring[:, 3, 0:D]).then_inc(zeros_out, 16)
            nc.gpsimd.memset(uP[:, :, 0:2], 0.0).then_inc(pool_link, 1)
            pool.dma_start(uS[:, :, :, 0:2], st_a).then_inc(state_a_in, 16)
            pool.wait_ge(proj_kept, 21)
            pool.wait_ge(proj_done, 23)
            for h in range(2):
                nc.gpsimd.memset(qz[h][64 * (1 - h):64 * (1 - h) + 64, :, :], 0.0).then_inc(qz_zero, 1)
                pool.wait_ge(qz_zero, h + 1)
            nc.gpsimd.memset(view(A_QBD, 1536), 0.0).then_inc(pool_link, 1)
            pool.wait_ge(pool_link, 2)
            made = 0
            for g in range(GROUPS):
                for r in range(2):
                    for hh in range(2):
                        for bb in range(2):
                            src = qkT[64 * hh:64 * hh + 64, 2 * g + r, SEQ:TOK].rearrange(
                                "p (q b i) -> p q b i", q=4, b=2)[:, :, bb, :]
                            c = 16 * bb + 4 * (2 * r + hh)
                            dst = qbd[64 * hh:64 * hh + 64, g, r, :, :].rearrange(
                                "p (q b) c -> p q b c", b=2)[:, :, bb, c:c + 4]
                            nc.gpsimd.tensor_copy(dst, src).then_inc(qbd_made, 1)
                            made += 1
                            pool.wait_ge(qbd_made, made)
            for n in range(16):
                i, h = n // 4, n % 4
                hh = h % 2
                if n >= 2:
                    pool.wait_ge(s_done, n - 1)
                if n:
                    pool.wait_ge(qz_ready, n)
                nc.gpsimd.tensor_copy(
                    qz[hh][64 * hh:64 * hh + 64, :, :],
                    qkT[64 * hh:64 * hh + 64, h // 2:6:2, P * i:P * i + P]).then_inc(qz_ready, 1)

            def experts(n):
                m = moe[n]
                pool.wait_ge(m.places, 1)
                for i in range(TILES):
                    for k in range(2):
                        pool.indirect_dma_start(
                            xs_dram, bass.IndirectOffsetOnAxis(ix[0:ROWS[i], i, k:k + 1], 0),
                            xn_of(2 * n + 1)[0:ROWS[i], i, :], None).then_inc(m.scattered, 16)
                pool.wait_ge(m.xs_tail, 1)
                pool.wait_ge(m.jobs, 1)
                iters = pool.value_load(jt[0:1, 128:129], min_val=8, max_val=MAX_ITERS)

                def job_rows(it, first):
                    for u in range(SLOTS):
                        at = pool.value_load(jt[0:1, bass.ds(4 * it + (64 + u), 1)], min_val=0, max_val=ASSIGNED)
                        if not first or u >= 2:
                            pool.wait_ge(m.gu_done, 4 * it + (u - 1))
                        nc.gpsimd.tensor_copy(xj[u % 2], xsT[:, :, bass.ds(at, JOB)]).then_inc(m.xj_ready, 1)

                job_rows(0, True)
                with pool.Fori(1, iters) as it:
                    job_rows(it, False)
                pool.wait_ge(m.all_out, 1)
                for q in range(2 * TILES):
                    i, k = q // 2, q % 2
                    if q >= 4:
                        if k:
                            pool.wait_ge(x_updated, TILES * (2 * n + 1) + i - 1)
                        else:
                            pool.wait_ge(m.combined, i - 1)
                    pool.indirect_dma_start(
                        yg[q % 4][0:ROWS[i], :], None, ys_dram,
                        bass.IndirectOffsetOnAxis(ix[0:ROWS[i], i, 2 + k:3 + k], 0)).then_inc(m.gathered[q % 4], 16)

            experts(0)
            pool.wait_ge(hT_ready, 30)
            nc.gpsimd.memset(cu[:, :, 0:CK - 1], 0.0).then_inc(pool_link, 1)
            pool.dma_start(cs[:, :, :, 0:CK - 1], st_c).then_inc(state_c_in, 16)
            experts(1)

        @block.scalar
        def _(act):
            for i in range(TILES):
                act.dma_start(X[0:ROWS[i], i, :], x_in[P * i:P * i + ROWS[i], :]).then_inc(x_in_done, 16)
            act.dma_start(sv[:, :], smalls).then_inc(smalls_in, 16)
            links = [0]

            def link(ins):
                links[0] += 1
                ins.then_inc(act_link, 1)
                act.wait_ge(act_link, links[0])

            def norm(call):
                wait_residual(act, call)
                act.wait_ge(stats_set, 1)
                junk = psum[:, 6:8, :].rearrange("p b c -> p (b c)")
                for i in range(TILES):
                    r = ROWS[i]
                    link(nc.scalar.activation(junk[0:r, :], X[0:r, i, :], ACT.Square,
                                              accum_out=stat[0:r, 0, i:i + 1]))
                nc.scalar.activation(stat[:, 1, 0:TILES], stat[:, 0, 0:TILES], ACT.Sqrt, scale=1.0 / D,
                                     bias=eps[:, 0:1]).then_inc(root_ready, 1)
                if call < 4:
                    act.wait_ge(inv_ready, call + 1)
                    for i in (1, 3):
                        nc.scalar.activation(xn_of(call)[:, i, :], X[:, i, :], ACT.Copy,
                                             scale=stat[:, 2, i:i + 1]).then_inc(xn_act, 1)

            norm(0)
            for m in range(23):
                b = 2 * (m % 3)
                if 19 <= m <= 20:
                    continue
                act.wait_ge(proj_done, m + 1)
                if 12 <= m < 17:
                    r = ROWS[m - 12]
                    nc.scalar.activation(vS[0:r, m - 12, :].rearrange("p (h c) -> p h c", h=2),
                                         psum[0:r, b:b + 2, 0:384], ACT.Copy).then_inc(proj_kept, 1)
                    continue
                dst = qkT[:, m, :] if m < 12 else (aIn[:, m - 17, :] if m < 19 else gB[:, m - 21, :])
                nc.scalar.activation(dst.rearrange("p (h t) -> p h t", h=2), psum[:, b:b + 2, 0:HALF],
                                     ACT.Copy).then_inc(proj_kept, 1)
                if m == 11:
                    act.wait_ge(proj_kept, 12)
                    act.dma_start(k_out, qkT[:, 6:12, :]).then_inc(outs_done, 16)
                if m == 17:
                    act.wait_ge(proj_kept, 17)
                    act.dma_start(v_out[0:SEQ, :].rearrange("(i p) c -> p i c", p=P), vS[:, 0:4, :]
                                  ).then_inc(outs_done, 16)
                    act.dma_start(v_out[SEQ:TOK, :], vS[0:SAMPLES, 4, :]).then_inc(outs_done, 16)
            act.wait_ge(u_made, 6)
            act.dma_start(ua_p_out, uP[:, :, SEQ:SEQ + 2]).then_inc(outs_done, 16)
            act.dma_start(ua_s_out, uS[:, :, :, 4:6]).then_inc(outs_done, 16)

            act.wait_ge(ss_max, 1)
            nc.scalar.activation(view(A_PS, 544), view(A_PS, 544), ACT.Exp, bias=vec[:, 0:1],
                                 accum_out=vec[:, 1:2]).then_inc(ss_exp, 1)
            act.wait_ge(ss_turned, 1)
            nc.scalar.activation(view(A_PTC, 512), psum[:, 2, :], ACT.Copy).then_inc(ss_kept, 1)
            nc.scalar.activation(view(A_PTN, 384, parts=32), psum[0:32, 3, 0:384], ACT.Copy).then_inc(ss_kept, 1)

            for n in range(16):
                i, h = n // 4, n % 4
                tiles = 2 * (i + 1) + (2 if i else 1)
                w = P * tiles
                sc = view(A_SC + 1280 * (n % 2), w)
                act.wait_ge(max_ready, n + 1)
                nc.scalar.activation(sc, sc, ACT.Exp, bias=vec[:, 4 + n % 2:5 + n % 2],
                                     accum_out=vec[:, 6 + n % 2:7 + n % 2]).then_inc(exp_done, 1)
                act.wait_ge(pt_done, n + 1)
                if n >= 1:
                    act.wait_ge(o_done, n)
                nc.scalar.activation(view(A_PT, w), psum[:, 3:6, :].rearrange("p b c -> p (b c)")[:, 0:w],
                                     ACT.Copy).then_inc(pt_kept, 1)
                act.wait_ge(o_done, n + 1)
                hh = h % 2
                nc.scalar.activation(yT[64 * hh:64 * hh + 64, 2 + h // 2, P * i:P * i + P],
                                     psum[64 * hh:64 * hh + 64, 6 + (n // 2) % 2, 0:P], ACT.Copy
                                     ).then_inc(o_kept, 1)

            def experts(n):
                m = moe[n]
                act.wait_ge(m.gshift, 1)
                g4 = view(M_R + 180, 20)
                nc.scalar.activation(g4, g4, ACT.Exp).then_inc(m.gexp, 1)
                act.wait_ge(m.eshift, 1)
                nc.scalar.activation(vec[:, 30:35], vec[:, 25:30], ACT.Exp).then_inc(m.eexp, 1)
                act.wait_ge(m.jobs, 1)
                iters = act.value_load(jt[0:1, 128:129], min_val=8, max_val=MAX_ITERS)

                def silu(it, u, first):
                    act.wait_ge(m.gu_done, 4 * it + (u + 1))
                    if not first or u >= 2:
                        act.wait_ge(m.act_ready, 4 * it + (u - 1))
                    nc.scalar.activation(sg[u % 2], psum[:, u % 2, 0:P], ACT.Silu).then_inc(m.sg_ready, 1)

                def keep_y(it, u, first):
                    b = u % 2
                    act.wait_ge(m.down_done, 4 * it + (u + 1))
                    if not first or u >= 2:
                        act.wait_ge(m.y_out[b], 64 * it + 32 * (u // 2))
                    nc.scalar.activation(yj[b], psum[:, 4 + b, :], ACT.Copy).then_inc(m.y_kept, 1)
                    act.wait_ge(m.y_kept, 4 * it + (u + 1))
                    rows = ys_dram.rearrange("(j r) c -> j r c", r=JOB)[bass.ds(4 * it + u, 1), :, :].rearrange(
                        "a r c -> (a r) c")
                    for q in range(2):
                        act.dma_start(rows[:, 512 * q:512 * q + 512], yj[b][64 * q:64 * q + 64, :]
                                      ).then_inc(m.y_out[b], 16)

                def body(it, first):
                    for u in range(SLOTS + 1):
                        if u < SLOTS:
                            silu(it, u, first)
                        if u:
                            keep_y(it, u - 1, first)

                body(0, True)
                with act.Fori(1, iters) as it:
                    body(it, False)
                for b in range(2):
                    act.wait_ge(m.y_out[b], 64 * iters)
                act.sem_inc(m.all_out, 1)

            act.wait_ge(outs_done, 16 * 5)
            norm(1)
            experts(0)

            wait_residual(act, 2)
            act.dma_start(brow, rows[0:1, :].to_broadcast([P, D])).then_inc(row_in, 16)
            norm(2)
            for c in range(KD):
                b = 2 * ((2 * c) % 3)
                act.wait_ge(z_done, 2 * c + 1)
                if c >= 2:
                    act.wait_ge(u_ready, c - 1)
                nc.scalar.activation(sigm[:, c % 2, :].rearrange("p (h t) -> p h t", h=2), psum[:, b:b + 2, 0:HALF],
                                     ACT.Sigmoid, bias=sv[:, V_BP1 + 8 + c:V_BP1 + 9 + c]).then_inc(sig_ready, 1)
            act.wait_ge(u_ready, KD)
            act.wait_ge(state_c_in, 16)
            act.dma_start(uc_p_out, cu[:, :, SEQ:UP]).then_inc(outs_done, 16)
            act.dma_start(uc_s_out, cs[:, :, :, DEC_T:US]).then_inc(outs_done, 16)
            sq = hT_of(2)
            for k in range(KD):
                act.wait_ge(centred, k + 1)
                nc.scalar.activation(sq[:, k, :], cT[:, k, :], ACT.Square).then_inc(squared, 1)
            act.wait_ge(var_done, 1)
            nc.scalar.activation(std.rearrange("p (h t) -> p h t", h=2), psum[:, 2:4, 0:HALF], ACT.Sqrt,
                                 bias=eps[:, 1:2]).then_inc(std_ready, 1)
            for k in range(KD):
                act.wait_ge(scaled, k + 1)
                nc.scalar.activation(cT[:, k, :], cT[:, k, :], ACT.Silu, scale=sv[:, V_LNG + k:V_LNG + k + 1],
                                     bias=sv[:, V_LNB + k:V_LNB + k + 1]).then_inc(swish_done, 1)
            act.wait_ge(outs_done, 16 * 7)
            norm(3)
            act.dma_start(brow, rows[1:2, :].to_broadcast([P, D])).then_inc(row_in, 16)
            experts(1)
            norm(4)

        @block.vector
        def _(dve):
            links = [0]

            def link(ins):
                links[0] += 1
                ins.then_inc(dve_link, 1)
                dve.wait_ge(dve_link, links[0])

            nc.vector.memset(eps[:, 0:1], 1e-6).then_inc(dve_link, 1)
            nc.vector.memset(eps[:, 1:2], 1e-5).then_inc(dve_link, 1)
            links[0] = 2
            dve.wait_ge(dve_link, 2)
            nc.vector.memset(stat[:, :, :], 1.0).then_inc(stats_set, 1)
            dve.wait_ge(consts_in, 16)
            dve.wait_ge(smalls_in, 16)

            def norm(call):
                wait_residual(dve, call)
                dve.wait_ge(root_ready, call + 1)
                nc.vector.reciprocal(stat[:, 2, 0:TILES], stat[:, 1, 0:TILES]).then_inc(inv_ready, 1)
                dve.wait_ge(inv_ready, call + 1)
                xn, hT = xn_of(call), hT_of(call)
                for i in (0, 2, 4):
                    r = ROWS[i]
                    nc.vector.tensor_scalar(xn[0:r, i, :], X[0:r, i, :], stat[0:r, 2, i:i + 1], None,
                                            ALU.mult).then_inc(xn_dve, 1)
                for i in range(TILES):
                    r = ROWS[i]
                    for h in range(2):
                        n = 2 * i + h
                        dve.wait_ge(turned, 10 * call + n + 1)
                        g = sv[:, V_GAIN + 8 * call + 4 * h:V_GAIN + 8 * call + 4 * h + 4]
                        nc.vector.tensor_tensor(
                            hT[:, 4 * h:4 * h + 4, P * i:P * i + r],
                            psum[:, n % 4, :].rearrange("p (k t) -> p k t", k=4)[:, :, 0:r],
                            bcast(g[:, :, None], [P, 4, r]), ALU.mult).then_inc(hT_ready, 1)

            norm(0)
            for c in range(2):
                b = 2 * ((19 + c) % 3)
                dve.wait_ge(proj_done, 20 + c)
                dve.wait_ge(proj_kept, 18 + c)
                if c == 0:
                    dve.wait_ge(state_a_in, 16)
                    dve.wait_ge(pool_link, 1)
                nc.vector.tensor_tensor(uP[:, c, 2:2 + HALF], psum[:, b, 0:HALF], aIn[:, c, 0:HALF],
                                        ALU.mult).then_inc(u_made, 1)
                nc.vector.tensor_tensor(uP[:, c, 2 + HALF:2 + SEQ], psum[:, b + 1, 0:SEQ - HALF],
                                        aIn[:, c, HALF:SEQ], ALU.mult).then_inc(u_made, 1)
                nc.vector.tensor_tensor(
                    uS[:, c, :, 2:6], psum[:, b + 1, SEQ - HALF:HALF].rearrange("p (b t) -> p b t", b=DEC_B),
                    aIn[:, c, SEQ:TOK].rearrange("p (b t) -> p b t", b=DEC_B), ALU.mult).then_inc(u_made, 1)
            dve.wait_ge(u_made, 6)
            dve.wait_ge(proj_kept, 21)
            for c in range(2):
                yp = yT[:, c, 0:SEQ]
                ys = yT[:, c, SEQ:TOK].rearrange("p (b t) -> p b t", b=DEC_B)
                for j in range(3):
                    w = sv[:, V_CA + 3 * c + j:V_CA + 3 * c + j + 1]
                    for dst, src in ((yp, uP[:, c, j:j + SEQ]), (ys, uS[:, c, :, j:j + 4])):
                        if j == 0:
                            link(nc.vector.tensor_scalar(dst, src, w, None, ALU.mult))
                        else:
                            link(nc.vector.scalar_tensor_tensor(out=dst, in0=src, scalar=w, in1=dst,
                                                                op0=ALU.mult, op1=ALU.add))
                nc.vector.tensor_tensor(yT[:, c, :], yT[:, c, :], gB[:, c, :], ALU.mult).then_inc(ya_made, 1)

            ps = view(A_PS, 544)
            dve.wait_ge(ss_done, 1)
            link(nc.vector.scalar_tensor_tensor(out=ps[:, 0:CACHED], in0=psum[:, 0, 0:CACHED], scalar=SCALE,
                                                in1=cst[:, C_SM:C_SM + CACHED], op0=ALU.mult, op1=ALU.add))
            link(nc.vector.scalar_tensor_tensor(out=ps[:, CACHED:544], in0=psum[:, 1, 0:96], scalar=SCALE,
                                                in1=cst[:, C_SM + CACHED:C_SM + 544], op0=ALU.mult, op1=ALU.add))
            nc.vector.tensor_reduce(vec[:, 0:1], ps, AX.X, ALU.max, negate=True).then_inc(ss_max, 1)
            dve.wait_ge(ss_exp, 1)
            link(nc.vector.reciprocal(vec[:, 2:3], vec[:, 1:2]))
            nc.vector.tensor_scalar(ps, ps, vec[:, 2:3], None, ALU.mult).then_inc(ss_norm, 1)
            dve.wait_ge(so_done, 1)
            for r in range(2):
                for hh in range(2):
                    src = psum[64 * hh:64 * hh + 64, 4, P * r:P * r + P].rearrange(
                        "p (b c) -> p b c", b=DEC_B)[:, :, 4 * (2 * r + hh):4 * (2 * r + hh) + 4]
                    nc.vector.tensor_copy(yT[64 * hh:64 * hh + 64, 2 + r, SEQ:TOK].rearrange(
                        "p (b t) -> p b t", b=DEC_B), src).then_inc(so_kept, 1)

            def scores(n):
                i = n // 4
                full = P * (i + 1)
                w0 = 2 * P if i else P
                sc = view(A_SC + 1280 * (n % 2), w0 + 2 * full)
                dve.wait_ge(s_done, n + 1)
                if n == 0:
                    dve.wait_ge(so_kept, 4)
                if n >= 2:
                    dve.wait_ge(pt_done, n - 1)
                at = 0
                for g, (w, width) in enumerate(((w0, 256), (full, 512), (full, 512))):
                    link(nc.vector.scalar_tensor_tensor(
                        out=sc[:, at:at + w], in0=psum[:, g, 0:w], scalar=SCALE,
                        in1=cst[:, C_M[g] + width - w:C_M[g] + width], op0=ALU.mult, op1=ALU.add))
                    at += w
                nc.vector.tensor_reduce(vec[:, 4 + n % 2:5 + n % 2], sc, AX.X, ALU.max, negate=True
                                        ).then_inc(max_ready, 1)

            def normalise(n):
                i = n // 4
                sc = view(A_SC + 1280 * (n % 2), P * (2 * (i + 1) + (2 if i else 1)))
                dve.wait_ge(exp_done, n + 1)
                link(nc.vector.reciprocal(vec[:, 8 + n % 2:9 + n % 2], vec[:, 6 + n % 2:7 + n % 2]))
                nc.vector.tensor_scalar(sc, sc, vec[:, 8 + n % 2:9 + n % 2], None, ALU.mult).then_inc(p_ready, 1)

            scores(0)
            for n in range(16):
                if n < 15:
                    scores(n + 1)
                normalise(n)

            def add_from_psum(done, first):
                for i in range(TILES):
                    r, b = ROWS[i], 2 * (i % 3)
                    dve.wait_ge(done, i + 1)
                    nc.vector.tensor_tensor(X[0:r, i, :], X[0:r, i, :],
                                            psum[0:r, b:b + 2, :].rearrange("p b c -> p (b c)"), ALU.add
                                            ).then_inc(x_updated, 1)

            add_from_psum(wo_done, 0)

            def experts(n):
                m = moe[n]
                o = [M_R]

                def new(k, pat=None, **dims):
                    o[0] += k
                    return view(o[0] - k, k, pat, **dims)

                def const(c, k):
                    return cst[:, c:c + k]

                S5 = [P, TILES, EXPERTS]
                L = new(180, "p (i e) -> p i e", i=TILES)
                g4 = new(20, "p (i e) -> p i e", i=TILES)
                t4 = new(20, "p (i e) -> p i e", i=TILES)
                em = new(160, "p (i e) -> p i e", i=TILES)
                tt = new(160, "p (i e) -> p i e", i=TILES)
                o1 = new(160, "p (i e) -> p i e", i=TILES)
                o2 = new(160, "p (i e) -> p i e", i=TILES)
                mk = new(160, "p (i e) -> p i e", i=TILES)
                rank = new(160, "p (i e) -> p i e", i=TILES)
                base = new(192, "p (i e) -> p i e", i=6)
                bigger = new(256, "p (e m) -> p e m", m=8)
                one = new(32)
                off = new(32)
                extra = new(32)
                inc = new(32)
                xb = new(32)
                d64 = new(32)
                joh = new(32)
                gmax, gsum, gval, gidx = vec[:, 0:5], vec[:, 5:10], vec[:, 10:15], vec[:, 15:20]
                m1, m2, eidx = vec[:, 20:25], vec[:, 25:30], vec[:, 35:40]
                place = vec[:, 40:60].rearrange("p (i k) -> p i k", i=TILES)
                tab = vec[:, 60:64]

                def tt_(out, a, b, op):
                    link(nc.vector.tensor_tensor(out, a, b, op))

                def ts_(out, a, s1, s2, op0, op1=ALU.bypass):
                    link(nc.vector.tensor_scalar(out, a, s1, s2, op0, op1))

                def red(out, a, op):
                    link(nc.vector.tensor_reduce(out, a, AX.X, op))

                def first_of(onehot, values, top, scratch, idx, iota, iotap, shape):
                    tt_(scratch, values, bcast(top[:, :, None], shape), ALU.is_ge)
                    link(nc.vector.scalar_tensor_tensor(
                        out=scratch, in0=scratch, scalar=-100.0, in1=bcast(iotap[:, None, :], shape),
                        op0=ALU.mult, op1=ALU.add))
                    red(idx, scratch, ALU.min)
                    tt_(onehot, bcast(iota[:, None, :], shape), bcast(idx[:, :, None], shape), ALU.is_equal)

                link(nc.vector.memset(L, 0.0))
                link(nc.vector.memset(base, 0.0))
                link(nc.vector.memset(one, 1.0))
                dve.wait_ge(m.logits, 1)
                rb = sv[:, V_RB + 36 * n:V_RB + 36 * n + 36]
                tt_(L[:, 0:4, :], psum[:, 4, 0:144].rearrange("p (i e) -> p i e", i=4),
                    bcast(rb[:, None, :], [P, 4, 36]), ALU.add)
                tt_(L[0:SAMPLES, 4, :], psum[0:SAMPLES, 4, 144:180], rb[0:SAMPLES, :], ALU.add)
                gl = L[:, :, 0:EGROUPS]
                red(gmax, gl, ALU.max)
                nc.vector.tensor_tensor(g4, gl, bcast(gmax[:, :, None], [P, TILES, 4]), ALU.subtract
                                        ).then_inc(m.gshift, 1)
                first_of(t4, gl, gmax, t4, gidx, const(C_GI, 4), const(C_GIP, 4), [P, TILES, 4])
                ts_(t4, t4, -1.0, 1e30, ALU.add, ALU.mult)
                for i in range(TILES):
                    tt_(em[:, i, :].rearrange("p (g e) -> p g e", g=4),
                        L[:, i, 4:36].rearrange("p (g e) -> p g e", g=4),
                        bcast(t4[:, i, :][:, :, None], [P, 4, 8]), ALU.add)
                red(m1, em, ALU.max)
                first_of(o1, em, m1, tt, eidx, const(C_IOTA, 32), const(C_IOTAP, 32), S5)
                link(nc.vector.scalar_tensor_tensor(out=em, in0=o1, scalar=-3e30, in1=em, op0=ALU.mult, op1=ALU.add))
                red(m2, em, ALU.max)
                first_of(o2, em, m2, tt, eidx, const(C_IOTA, 32), const(C_IOTAP, 32), S5)
                tt_(mk, o1, o2, ALU.add)
                nc.vector.tensor_tensor(mk, mk, bcast(const(C_VALID, 5)[:, :, None], S5), ALU.mult
                                        ).then_inc(m.picks, 1)
                nc.vector.tensor_tensor(m2, m2, m1, ALU.subtract).then_inc(m.eshift, 1)
                dve.wait_ge(m.gexp, 1)
                red(gsum, g4, ALU.add)
                dve.wait_ge(m.eexp, 1)
                te = vec[:, 30:35]
                ts_(gval, te, 1.0, None, ALU.add)
                tt_(gval, gval, gsum, ALU.mult)
                link(nc.vector.reciprocal(cw[:, :, 0], gval))
                tt_(cw[:, :, 1], cw[:, :, 0], te, ALU.mult)
                dve.wait_ge(m.ranks, 1)
                for i in range(TILES):
                    tt_(base[:, i + 1, :], base[:, i, :], psum[:, 5, 32 * i:32 * i + 32], ALU.add)
                tt_(rank, psum[:, 6, 0:160].rearrange("p (i e) -> p i e", i=TILES), base[:, 0:TILES, :], ALU.add)
                cnt = base[:, TILES, :]

                def before(out, counts, incl):
                    link(nc.vector.tensor_tensor_scan(incl, counts, one, 0.0, ALU.add, ALU.bypass))
                    tt_(out, incl, counts, ALU.subtract)

                before(off, cnt, inc)
                tt_(tt, rank, bcast(off[:, None, :], S5), ALU.add)
                for k, oh in enumerate((o1, o2)):
                    tt_(em, oh, tt, ALU.mult)
                    red(place[:, :, k], em, ALU.add)
                tt_(bigger, bcast(cnt[:, :, None], [P, EXPERTS, 8]),
                    bcast(const(C_THR, 8)[:, None, :], [P, EXPERTS, 8]), ALU.is_gt)
                red(extra, bigger, ALU.add)
                before(xb, extra, inc)
                ts_(d64, xb, 64.0, 64.0 * 31, ALU.mult, ALU.add)
                tt_(d64, d64, const(C_E64, 32), ALU.subtract)
                ts_(tt, rank, 64.0, None, ALU.is_ge)
                tt_(tt, tt, bcast(d64[:, None, :], S5), ALU.mult)
                tt_(tt, tt, bcast(const(C_E64, 32)[:, None, :], S5), ALU.add)
                tt_(tt, tt, rank, ALU.add)
                for k, oh in enumerate((o1, o2)):
                    tt_(em, oh, tt, ALU.mult)
                    red(place[:, :, 2 + k], em, ALU.add)
                nc.vector.tensor_copy(ix[:, :, :], place).then_inc(m.places, 1)
                ts_(joh, inc, const(C_JM, 1), None, ALU.is_le)
                red(tab[:, 0:1], joh, ALU.add)
                ts_(tab[:, 0:1], tab[:, 0:1], const(C_JLO, 1), float(EXPERTS - 1), ALU.add, ALU.min)
                ts_(joh, const(C_IOTA, 32), tab[:, 0:1], None, ALU.is_equal)
                ts_(xb, xb, const(C_HI, 1), None, ALU.mult)
                tt_(xb, off, xb, ALU.subtract)
                tt_(joh, joh, xb, ALU.mult)
                red(tab[:, 1:2], joh, ALU.add)
                ts_(tab[:, 1:2], tab[:, 1:2], const(C_HI1, 1), float(ASSIGNED), ALU.add, ALU.min)
                ts_(bigger[:, 0, 0:4], const(C_THJ, 4), inc[:, 31:32], None, ALU.is_lt)
                red(tab[:, 2:3], bigger[:, 0, 0:4], ALU.add)
                nc.vector.tensor_scalar(tab[:, 2:3], tab[:, 2:3], 8.0, None, ALU.add).then_inc(m.table, 1)
                dve.wait_ge(m.table, 1)
                link(nc.vector.tensor_copy(jt[0:1, 128:129], tab[0:1, 2:3]))
                dve.wait_ge(m.rowed, 1)
                nc.vector.tensor_copy(jt[0:1, 0:128], psum[0:1, 7, 0:128]).then_inc(m.jobs, 1)
                for t in range(9):
                    r = min(P, ASSIGNED - P * t)
                    for h in range(2):
                        q = 2 * t + h
                        dve.wait_ge(m.st_turned, q + 1)
                        g = sv[:, V_GPK + 8 * n + 4 * h:V_GPK + 8 * n + 4 * h + 4]
                        nc.vector.tensor_tensor(
                            xsT[:, 4 * h:4 * h + 4, P * t:P * t + r],
                            psum[:, q % 4, :].rearrange("p (k t) -> p k t", k=4)[:, :, 0:r],
                            bcast(g[:, :, None], [P, 4, r]), ALU.mult).then_inc(m.xs_kept, 1)
                dve.wait_ge(m.xs_kept, 18)
                nc.vector.memset(xsT[:, :, ASSIGNED:XCOLS], 0.0).then_inc(m.xs_tail, 1)
                dve.wait_ge(m.jobs, 1)
                iters = dve.value_load(jt[0:1, 128:129], min_val=8, max_val=MAX_ITERS)

                def gate_up(it, u, first):
                    dve.wait_ge(m.sg_ready, 4 * it + (u + 1))
                    if not first or u >= 2:
                        dve.wait_ge(m.at_done, 4 * it + (u - 1))
                    nc.vector.tensor_tensor(av[u % 2], sg[u % 2], psum[:, u % 2, P:2 * P], ALU.mult
                                            ).then_inc(m.act_ready, 1)

                def keep_at(it, u, first):
                    dve.wait_ge(m.at_done, 4 * it + (u + 1))
                    if not first or u >= 2:
                        dve.wait_ge(m.down_done, 4 * it + (u - 1))
                    nc.vector.tensor_copy(aT[u % 2], psum[:, 2 + u % 2, 0:P]).then_inc(m.at_kept, 1)

                def steps(it, first):
                    gate_up(it, 0, first)
                    for u in range(1, SLOTS + 1):
                        keep_at(it, u - 1, first)
                        if u < SLOTS:
                            gate_up(it, u, first)

                steps(0, True)
                with dve.Fori(1, iters) as it:
                    steps(it, False)
                for q in range(2 * TILES):
                    i, k = q // 2, q % 2
                    r = ROWS[i]
                    dve.wait_ge(m.gathered[q % 4], 16 * (q // 4 + 1))
                    if k:
                        dve.wait_ge(m.combined, i + 1)
                    nc.vector.scalar_tensor_tensor(out=X[0:r, i, :], in0=yg[q % 4][0:r, :],
                                                   scalar=cw[0:r, i, k:k + 1], in1=X[0:r, i, :],
                                                   op0=ALU.mult, op1=ALU.add).then_inc(x_updated if k else m.combined, 1)

            dve.wait_ge(outs_done, 16 * 5)
            norm(1)
            experts(0)

            norm(2)
            dve.wait_ge(xn_act, 6)
            dve.wait_ge(xn_dve, 9)
            dve.wait_ge(row_in, 16)
            for i in range(TILES):
                r = ROWS[i]
                link(nc.vector.tensor_tensor(X[0:r, i, :], X[0:r, i, :], brow[0:r, :], ALU.add))
            win = view(B_WIN, SAMPLES * CK, "p (b i j) -> p b i j", b=DEC_B, i=DEC_T)
            for c in range(KD):
                b = 2 * ((2 * c + 1) % 3)
                ba = sv[:, V_BP1 + c:V_BP1 + c + 1]
                dve.wait_ge(z_done, 2 * c + 2)
                dve.wait_ge(sig_ready, c + 1)
                if c == 0:
                    dve.wait_ge(pool_link, 3)
                    dve.wait_ge(state_c_in, 16)
                s = sigm[:, c % 2, :]
                link(nc.vector.scalar_tensor_tensor(out=cu[:, c, CK - 1:CK - 1 + HALF], in0=psum[:, b, 0:HALF],
                                                    scalar=ba, in1=s[:, 0:HALF], op0=ALU.add, op1=ALU.mult))
                link(nc.vector.scalar_tensor_tensor(out=cu[:, c, CK - 1 + HALF:UP], in0=psum[:, b + 1, 0:SEQ - HALF],
                                                    scalar=ba, in1=s[:, HALF:SEQ], op0=ALU.add, op1=ALU.mult))
                nc.vector.scalar_tensor_tensor(
                    out=cs[:, c, :, CK - 1:US], in0=psum[:, b + 1, SEQ - HALF:HALF].rearrange("p (b t) -> p b t", b=DEC_B),
                    scalar=ba, in1=s[:, SEQ:TOK].rearrange("p (b t) -> p b t", b=DEC_B),
                    op0=ALU.add, op1=ALU.mult).then_inc(u_ready, 1)
                dve.wait_ge(u_ready, c + 1)
                for j in range(CK):
                    w = sv[:, V_DW + CK * c + j:V_DW + CK * c + j + 1]
                    src = cu[:, c, j:j + SEQ]
                    if j == 0:
                        link(nc.vector.tensor_scalar(cT[:, c, 0:SEQ], src, w, sv[:, V_DWB + c:V_DWB + c + 1],
                                                     ALU.mult, ALU.add))
                    else:
                        link(nc.vector.scalar_tensor_tensor(out=cT[:, c, 0:SEQ], in0=src, scalar=w,
                                                            in1=cT[:, c, 0:SEQ], op0=ALU.mult, op1=ALU.add))
                rows_ = cs[:, c, :, :]
                windows = bass.AP(rows_.tensor, rows_.offset, [rows_.ap[0], [US, DEC_B], [1, DEC_T], [1, CK]])
                wj = sv[:, V_DW + CK * c:V_DW + CK * c + CK]
                link(nc.vector.tensor_tensor(win, windows, bcast(wj[:, None, None, :], [P, DEC_B, DEC_T, CK]), ALU.mult))
                cs_out = cT[:, c, SEQ:TOK].rearrange("p (b t) -> p b t", b=DEC_B)
                link(nc.vector.tensor_reduce(cs_out, win, AX.X, ALU.add))
                nc.vector.tensor_scalar(cs_out, cs_out, sv[:, V_DWB + c:V_DWB + c + 1], None, ALU.add
                                        ).then_inc(conv_done, 1)
            dve.wait_ge(mean_done, 1)
            dve.wait_ge(conv_done, KD)
            for k in range(KD):
                nc.vector.tensor_tensor(cT[:, k, :].rearrange("p (h t) -> p h t", h=2),
                                        cT[:, k, :].rearrange("p (h t) -> p h t", h=2),
                                        psum[:, 6:8, 0:HALF], ALU.subtract).then_inc(centred, 1)
            dve.wait_ge(std_ready, 1)
            link(nc.vector.reciprocal(std, std))
            dve.wait_ge(centred, KD)
            for k in range(KD):
                nc.vector.tensor_tensor(cT[:, k, :], cT[:, k, :], std, ALU.mult).then_inc(scaled, 1)
            add_from_psum(pw2_done, 2)
            dve.wait_ge(outs_done, 16 * 7)
            norm(3)
            experts(1)
            wait_residual(dve, 4)
            dve.wait_ge(root_ready, 5)
            nc.vector.reciprocal(stat[:, 2, 0:TILES], stat[:, 1, 0:TILES]).then_inc(inv_ready, 1)
            dve.wait_ge(inv_ready, 5)
            dve.wait_ge(row_in, 32)
            for i in range(TILES):
                r = ROWS[i]
                nc.vector.scalar_tensor_tensor(out=view(D * i, D, parts=r), in0=X[0:r, i, :],
                                               scalar=stat[0:r, 2, i:i + 1], in1=brow[0:r, :],
                                               op0=ALU.mult, op1=ALU.mult).then_inc(y_ready, 1)

        @block.tensor
        def _(pe):
            mm, tr = nc.tensor.matmul, nc.tensor.transpose
            pe.wait_ge(consts_in, 16)

            def turn(call):
                xn = xn_of(call)
                for i in range(TILES):
                    r = ROWS[i]
                    if i % 2:
                        pe.wait_ge(xn_act, 2 * call + i // 2 + 1)
                    else:
                        pe.wait_ge(xn_dve, 3 * call + i // 2 + 1)
                    for h in range(2):
                        n = 2 * i + h
                        if n >= 4:
                            pe.wait_ge(hT_ready, 10 * call + n - 3)
                        for k in range(4):
                            t = tr(psum[:, n % 4, P * k:P * k + r], xn[0:r, i, P * (4 * h + k):P * (4 * h + k) + P],
                                   ident[0:r, 0:r])
                        t.then_inc(turned, 1)
                pe.wait_ge(hT_ready, 10 * (call + 1))

            turn(0)
            hT = hT_of(0)
            for m in range(23):
                b = 2 * (m % 3)
                chunk = 0 if m < 6 else 1 if m < 12 else 2 if m < 17 else 3
                if m in (0, 6, 12, 17):
                    pe.wait_ge(proj_w[chunk], 16)
                if m >= 3:
                    p = m - 3
                    pe.wait_ge(proj_kept, min(p + 1, 19) if p < 21 else p - 1)
                    if p in (19, 20):
                        pe.wait_ge(u_made, 3 * (p - 18))
                w = ring[:, chunk, :].rearrange("p (k c) -> p k c", k=KD)
                if 12 <= m < 17:
                    i = m - 12
                    for h in range(2):
                        for k in range(KD):
                            t = mm(psum[0:ROWS[i], b + h, 0:384], hT[:, k, P * i:P * i + ROWS[i]],
                                   w[:, k, 384 * h:384 * h + 384], start=k == 0, stop=k == KD - 1)
                else:
                    c = m % 6 if m < 12 else (4, 5, 2, 3, 0, 1)[m - 17]
                    for h in range(2):
                        for k in range(KD):
                            t = mm(psum[:, b + h, 0:HALF], w[:, k, P * c:P * c + P],
                                   hT[:, k, HALF * h:HALF * h + HALF], start=k == 0, stop=k == KD - 1)
                t.then_inc(proj_done, 1)

            pe.wait_ge(proj_kept, 21)
            pe.wait_ge(u_made, 6)
            pe.wait_ge(qbd_made, 24)
            for c in range(3):
                pe.wait_ge(kv_w[c], 16)
            for g in range(GROUPS):
                for bb in range(2):
                    for r in range(2):
                        for q in range(4):
                            b = 2 * q + bb
                            mm(psum[32 * q:32 * q + 32, 0, KOFF[g]:KOFF[g] + KEYS[g]], qbd[:, g, r, b, :],
                               kt_of(b)[:, r, KOFF[g]:KOFF[g] + KEYS[g]],
                               start=bb + r == 0, stop=bb + r == 2, tile_position=(0, 32 * q))
            for g in range(GROUPS):
                for bb in range(2):
                    for r in range(2):
                        for q in range(4):
                            t = mm(psum[32 * q:32 * q + 32, 1, 32 * g:32 * g + 32], qbd[:, g, r, 2 * q + bb, :],
                                   qkT[:, 6 + 2 * g + r, SEQ:TOK], start=bb + r == 0, stop=bb + r == 2,
                                   tile_position=(0, 32 * q))
            t.then_inc(ss_done, 1)
            pe.wait_ge(ss_norm, 1)
            ps = view(A_PS, 544)
            for t_, (rows_, _) in enumerate(VT):
                tr(psum[0:rows_, 2, P * t_:P * t_ + P], ps[:, P * t_:P * t_ + rows_], ident)
            for g in range(GROUPS):
                t = tr(psum[0:32, 3, P * g:P * g + P], ps[:, CACHED + 32 * g:CACHED + 32 * g + 32], ident)
            t.then_inc(ss_turned, 1)
            pe.wait_ge(ss_kept, 2)
            for r in range(2):
                for g in range(GROUPS):
                    mm(psum[:, 4, P * r:P * r + P], vS[0:SAMPLES, 4, 256 * g + P * r:256 * g + P * r + P],
                       view(A_PTN + P * g, P, parts=32), start=g == 0, stop=False, skip_group_check=True)
                for b in range(DEC_B):
                    for t_, (rows_, _) in enumerate(VT):
                        last = r == 1 and b == DEC_B - 1 and t_ == 3
                        t = mm(psum[:, 4, P * r + 16 * b:P * r + 16 * b + 16], v_of(b)[0:rows_, t_, P * r:P * r + P],
                               view(A_PTC + P * t_ + 16 * b, 16, parts=rows_), start=False,
                               stop=b == DEC_B - 1 and t_ == 3, skip_group_check=True)
            t.then_inc(so_done, 1)

            def scores(n):
                i, h = n // 4, n % 4
                pe.wait_ge(qz_ready, n + 1)
                if n < 2:
                    pe.wait_ge(qz_zero, 2)
                if n:
                    pe.wait_ge(max_ready, n)
                for g in range(GROUPS):
                    lo = P * (i - 1) if g == 0 and i else 0
                    t = mm(psum[:, g, 0:P * (i + 1) - lo], qz[h % 2][:, g, :],
                           qkT[:, 6 + 2 * g + h // 2, lo:P * (i + 1)], start=True, stop=True)
                t.then_inc(s_done, 1)

            scores(0)
            for n in range(16):
                i, h = n // 4, n % 4
                hh = h % 2
                if n < 15:
                    scores(n + 1)
                tiles = [(0, j) for j in range(max(i - 1, 0), i + 1)]
                tiles += [(g, j) for g in (1, 2) for j in range(i + 1)]
                pe.wait_ge(p_ready, n + 1)
                if n:
                    pe.wait_ge(pt_kept, n)
                sc = view(A_SC + 1280 * (n % 2), P * len(tiles))
                for t_ in range(len(tiles)):
                    t = tr(psum[:, 3 + t_ // 4, P * (t_ % 4):P * (t_ % 4) + P], sc[:, P * t_:P * t_ + P], ident)
                t.then_inc(pt_done, 1)
                pe.wait_ge(pt_kept, n + 1)
                if n >= 4:
                    pe.wait_ge(o_kept, n - 3)
                for t_, (g, j) in enumerate(tiles):
                    t = mm(psum[64 * hh:64 * hh + 64, 6 + (n // 2) % 2, 0:P],
                           vS[:, j, 256 * g + 64 * h:256 * g + 64 * h + 64], view(A_PT + P * t_, P),
                           start=t_ == 0, stop=t_ == len(tiles) - 1)
                t.then_inc(o_done, 1)

            def project(src, blocks, weights, done):
                for i in range(TILES):
                    r, b = ROWS[i], 2 * (i % 3)
                    if i >= 3:
                        pe.wait_ge(x_updated, x_base[0] + i - 2)
                    for h in range(2):
                        for k in range(blocks):
                            t = mm(psum[0:r, b + h, :], src[:, k, P * i:P * i + r], weights(k, h),
                                   start=k == 0, stop=k == blocks - 1)
                    t.then_inc(done, 1)

            x_base = [0]
            pe.wait_ge(wout_w, 16)
            pe.wait_ge(ya_made, 2)
            pe.wait_ge(so_kept, 4)
            pe.wait_ge(o_kept, 16)
            project(yT, 4, lambda k, h: ring[:, 3, D * k + 512 * h:D * k + 512 * h + 512], wo_done)

            def experts(n):
                m = moe[n]
                hT = hT_of(2 * n + 1)
                for i in range(TILES):
                    r = ROWS[i]
                    for k in range(KD):
                        o = V_RW + 36 * (KD * n + k)
                        t = mm(psum[0:r, 4, 36 * i:36 * i + 36], hT[:, k, P * i:P * i + r], sv[:, o:o + 36],
                               start=k == 0, stop=k == KD - 1)
                t.then_inc(m.logits, 1)
                pe.wait_ge(m.picks, 1)
                mk = view(M_R + 180 + 40 + 4 * 160, 160)
                mm(psum[:, 5, 0:160], ones, mk, start=True, stop=True)
                mm(psum[:, 6, 0:160], cst[:, C_TRI:C_TRI + P], mk, start=True, stop=True).then_inc(m.ranks, 1)
                pe.wait_ge(m.table, 1)
                for c in range(2):
                    t = mm(psum[0:1, 7, 64 * c:64 * c + 64], vec[:, 60 + c:61 + c], ident[:, 0:64], start=True, stop=True)
                t.then_inc(m.rowed, 1)
                for t_ in range(9):
                    r = min(P, ASSIGNED - P * t_)
                    pe.wait_ge(m.staged[t_ % 2], 16 * (t_ // 2 + 1))
                    rows_ = stg[t_ % 2].rearrange("t (d k) -> t k d", k=KD)
                    for h in range(2):
                        q = 2 * t_ + h
                        if q >= 4:
                            pe.wait_ge(m.xs_kept, q - 3)
                        for k in range(4):
                            t = tr(psum[:, q % 4, P * k:P * k + r], rows_[0:r, 4 * h + k, :], ident[0:r, 0:r])
                        t.then_inc(m.st_turned, 1)
                pe.wait_ge(m.jobs, 1)
                iters = pe.value_load(jt[0:1, 128:129], min_val=8, max_val=MAX_ITERS)

                def gate_up(it, u, first):
                    pe.wait_ge(m.w_in[u], 16 * it + 16)
                    pe.wait_ge(m.xj_ready, 4 * it + (u + 1))
                    if not first or u >= 2:
                        pe.wait_ge(m.act_ready, 4 * it + (u - 1))
                    w = ring[:, u, 0:4096].rearrange("p (k f c) -> p k f c", k=KD, f=2)
                    for k in range(KD):
                        for f in range(2):
                            t = mm(psum[64 * f:64 * f + 64, u % 2, 0:2 * P], xj[u % 2][:, k, :], w[:, k, f, :],
                                   start=k == 0, stop=k == KD - 1)
                    t.then_inc(m.gu_done, 1)

                def turn_act(it, u, first):
                    pe.wait_ge(m.act_ready, 4 * it + (u + 1))
                    if not first or u >= 2:
                        pe.wait_ge(m.at_kept, 4 * it + (u - 1))
                    tr(psum[:, 2 + u % 2, 0:P], av[u % 2], ident).then_inc(m.at_done, 1)

                def down(it, u, first):
                    pe.wait_ge(m.at_kept, 4 * it + (u + 1))
                    if not first or u >= 2:
                        pe.wait_ge(m.y_kept, 4 * it + (u - 1))
                    for k in range(2):
                        for h in range(2):
                            o = 4096 + D * k + 512 * h
                            t = mm(psum[64 * h:64 * h + 64, 4 + u % 2, :], aT[u % 2][:, 64 * k:64 * k + 64],
                                   ring[:, u, o:o + 512], start=k == 0, stop=k == 1)
                    t.then_inc(m.down_done, 1)

                def body(it, first):
                    for u in range(SLOTS + 1):
                        if u < SLOTS:
                            gate_up(it, u, first)
                        if u:
                            turn_act(it, u - 1, first)
                            down(it, u - 1, first)

                body(0, True)
                with pe.Fori(1, iters) as it:
                    body(it, False)

            turn(1)
            experts(0)

            turn(2)
            hT2 = hT_of(2)
            for m in range(2 * KD):
                c, gate = m // 2, m % 2 == 0
                b = 2 * (m % 3)
                if m % 4 == 0:
                    pe.wait_ge(pw1_w[m // 4], 16)
                if m >= 3:
                    p = m - 3
                    if p % 2 == 0:
                        pe.wait_ge(sig_ready, p // 2 + 1)
                    else:
                        pe.wait_ge(u_ready, p // 2 + 1)
                w = ring[:, m // 4, 0:4096].rearrange("p (k c) -> p k c", k=KD)
                o = (256 if gate else 0) + P * (c % 2)
                for h in range(2):
                    for k in range(KD):
                        t = mm(psum[:, b + h, 0:HALF], w[:, k, o:o + P], hT2[:, k, HALF * h:HALF * h + HALF],
                               start=k == 0, stop=k == KD - 1)
                t.then_inc(z_done, 1)
            mean = cst[:, C_MEAN:C_MEAN + P]
            for k in range(KD):
                pe.wait_ge(conv_done, k + 1)
                for h in range(2):
                    t = mm(psum[:, 6 + h, 0:HALF], mean, cT[:, k, HALF * h:HALF * h + HALF], start=k == 0,
                           stop=k == KD - 1)
            t.then_inc(mean_done, 1)
            for k in range(KD):
                pe.wait_ge(squared, k + 1)
                for h in range(2):
                    t = mm(psum[:, 2 + h, 0:HALF], mean, hT2[:, k, HALF * h:HALF * h + HALF], start=k == 0,
                           stop=k == KD - 1)
            t.then_inc(var_done, 1)
            x_base[0] = 2 * TILES
            for c in range(2):
                pe.wait_ge(pw2_w[c], 16)
            pe.wait_ge(swish_done, KD)
            project(cT, KD, lambda k, h: ring[:, h, 512 * k:512 * k + 512], pw2_done)
            turn(3)
            experts(1)


def constants():
    c = np.zeros((P, C_END), np.float32)
    p = np.arange(P)
    c[:, C_ID:C_ID + P] = np.eye(P)
    c[:, C_TRI:C_TRI + P] = p[:, None] < p[None, :]
    c[:, C_ONE:C_ONE + P] = 1
    c[:, C_MEAN:C_MEAN + P] = 1.0 / D
    q, k = p[:, None], p[None, :]
    neg = np.float32(NEG)
    c[:, C_M[0]:C_M[0] + P] = np.where(k >= q, 0, neg)
    c[:, C_M[0] + P:C_M[0] + 2 * P] = np.where(k <= q, 0, neg)
    for g, dil in ((1, 4), (2, 16)):
        same = q % dil == k % dil
        for j in range(4):
            ok = same if j < 3 else same & (k <= q)
            c[:, C_M[g] + P * j:C_M[g] + P * j + P] = np.where(ok, 0, neg)
    b, i = p // 16, p % 4
    cols = np.arange(CACHED)
    ok = np.zeros((P, CACHED + 96), bool)
    ok[:, 0:128] = cols[None, 0:128] >= i[:, None]
    ok[:, 128:384] = (cols[None, 0:256] % 4) == i[:, None]
    ok[:, 384:448] = (cols[None, 0:64] % 4) == i[:, None]
    new = np.arange(32)
    for g in range(3):
        mine = (new[None] // 4) == b[:, None]
        ok[:, CACHED + 32 * g:CACHED + 32 * g + 32] = mine & (
            (new[None] % 4 <= i[:, None]) if g == 0 else (new[None] % 4 == i[:, None]))
    c[:, C_SM:C_SM + 544] = np.where(ok, 0, neg)
    c[:, C_IOTA:C_IOTA + 32] = np.arange(32)
    c[:, C_IOTAP:C_IOTAP + 32] = np.arange(32) + 100
    c[:, C_E64:C_E64 + 32] = 64 * np.arange(32)
    c[:, C_THR:C_THR + 8] = 64 * np.arange(1, 9)
    c[:, C_THJ:C_THJ + 4] = 4 * np.arange(4)
    c[:, C_JM] = p - 32
    c[:, C_JLO] = np.where(p < 32, p, 0)
    c[:, C_HI] = np.where(p < 32, 0, 64)
    c[:, C_HI1] = np.where(p < 32, 0, 64 * (p - 31))
    c[:, C_VALID:C_VALID + 5] = 1
    c[SAMPLES:, C_VALID + 4] = 0
    c[:, C_GI:C_GI + 4] = np.arange(4)
    c[:, C_GIP:C_GIP + 4] = np.arange(4) + 100
    return c


def blocks_of(w):
    k, n = w.shape[0] // P, w.shape[1]
    return w.reshape(k, P, n).transpose(1, 0, 2).reshape(P, k * n)


def kernel(**inputs):
    import concourse.bacc as bacc
    from concourse.bass_utils import run_bass_kernel_spmd

    a = {k: np.asarray(v) for k, v in inputs.items()}
    cat, con = np.concatenate, np.ascontiguousarray
    arrays = {}
    arrays["x_in"] = cat([a["x_prompt"].reshape(SEQ, D), a["x_sample"].reshape(SAMPLES, D)])
    w = a["w_in"][0]
    arrays["w_mix0"] = np.stack([blocks_of(con(w[:, c:c + 768])) for c in (768, 1536, 2304, 0)])
    kv = np.zeros((3, P, SLOT), np.float32)
    caches = [a["cache_kv_w128"][0], a["cache_kv_w512"][0],
              a["cache_kv_w2048"][0].reshape(DEC_B, 16, 16, 2, 4, HD)[:, :, 0:4].reshape(DEC_B, 64, 2, 4, HD)]
    for b in range(DEC_B):
        o = KV * (b % 3)
        for g, c in enumerate(caches):
            kt = c[b, :, 0].reshape(KEYS[g], 2, P).transpose(2, 1, 0)
            img = kv[b // 3, :, o:o + 2 * CACHED].reshape(P, 2, CACHED)
            img[:, :, KOFF[g]:KOFF[g] + KEYS[g]] = kt
            kv[b // 3, :, o:o + 2 * CACHED] = img.reshape(P, 2 * CACHED)
        o += 2 * CACHED
        v = [c[b, :, 1].reshape(KEYS[g], 256) for g, c in enumerate(caches)]
        for t, part in enumerate((v[0], v[1][0:P], v[1][P:], v[2])):
            kv[b // 3, 0:len(part), o + 256 * t:o + 256 * t + 256] = part
    arrays["kv_in"] = kv
    arrays["w_out"] = blocks_of(a["w_out"][0])
    w = a["w_pw1"][0]
    arrays["w_pw1"] = np.stack([blocks_of(cat([w[:, 256 * c:256 * c + 256], w[:, D + 256 * c:D + 256 * c + 256]], 1))
                                for c in range(4)])
    arrays["w_pw2"] = np.stack([blocks_of(con(a["w_pw2"][0][:, 512 * c:512 * c + 512])) for c in range(2)])
    moe = np.empty((2, EXPERTS, P, SLOT), np.float32)
    gu = moe[..., 0:4096].reshape(2, EXPERTS, P, KD, 2, 2, P)
    gu[:, :, :, :, :, 0] = a["w_gate"].reshape(2, EXPERTS, P, KD, 2, P)
    gu[:, :, :, :, :, 1] = a["w_up"].reshape(2, EXPERTS, P, KD, 2, P)
    moe[..., 0:4096] = gu.reshape(2, EXPERTS, P, 4096)
    moe[..., 4096:] = a["w_down"].reshape(2, EXPERTS, 2, P, D).transpose(0, 1, 3, 2, 4).reshape(2, EXPERTS, P, 2 * D)
    arrays["w_moe"] = moe

    def col(v):
        return v.reshape(-1, P).T

    def spread(v):
        return np.broadcast_to(v.reshape(1, -1), (P, v.size))

    router = [cat([a["w_router_group"][n], a["w_router_expert"][n]], 1) for n in range(2)]
    arrays["smalls"] = con(cat(
        [col(a["g_mix"][0]), col(a["g_ffn"][0]), col(a["g_mix"][1]), col(a["g_ffn"][1]),
         a["g_ffn"][0].reshape(P, KD), a["g_ffn"][1].reshape(P, KD), col(a["b_pw1"][0]), col(a["dw_b"][0]),
         col(a["ln_g"][0]), col(a["ln_b"][0]),
         a["conv_a_w"][0].reshape(3, 2, P).transpose(2, 1, 0).reshape(P, 6),
         a["dw_w"][0].reshape(CK, KD, P).transpose(2, 1, 0).reshape(P, KD * CK)]
        + [spread(cat([a["b_router_group"][n], a["b_router_expert"][n]])) for n in range(2)]
        + [blocks_of(r) for r in router], 1))
    arrays["consts"] = constants()
    arrays["rows"] = np.stack([a["b_pw2"][0], a["g_final"]])
    arrays["st_a"] = con(a["state_shortconv"][0].reshape(DEC_B, 2, 2, P).transpose(3, 2, 0, 1))
    arrays["st_c"] = con(a["state_conformer"][0].reshape(DEC_B, CK - 1, KD, P).transpose(3, 2, 0, 1))
    outs = {"y": (TOK, D), "k": (P, 6, TOK), "v": (TOK, 768), "ua_p": (P, 2, 2), "ua_s": (P, 2, DEC_B, 2),
            "uc_p": (P, KD, CK - 1), "uc_s": (P, KD, DEC_B, CK - 1)}

    nc = bacc.Bacc("TRN2", target_bir_lowering=False, num_devices=1)
    args = [nc.dram_tensor(n, v.shape, F32, kind="ExternalInput").ap() for n, v in arrays.items()]
    args += [nc.dram_tensor("out_" + n, s, F32, kind="ExternalOutput").ap() for n, s in outs.items()]
    program(nc, *args)
    r = run_bass_kernel_spmd(nc, [arrays], core_ids=[0]).results[0]
    y, k, v, ua_p, ua_s, uc_p, uc_s = (np.asarray(r["out_" + n]) for n in outs)

    kv = np.stack([k.transpose(2, 1, 0).reshape(TOK, 3, 4, HD), v.reshape(TOK, 3, 4, HD)], 1)
    prompt, new = kv[0:SEQ], kv[SEQ:].reshape(DEC_B, DEC_T, 2, 3, 4, HD)
    p_kv = [con(prompt[SEQ - n:, :, g])[None, None] for g, n in enumerate((128, SEQ, SEQ))]
    s_kv = [con(new[:, :, :, g])[None] for g in range(3)]
    return (y[0:SEQ].reshape(1, SEQ, D), y[SEQ:].reshape(DEC_B, DEC_T, D),
            con(ua_p.transpose(2, 1, 0)).reshape(1, 1, 2, 256), *p_kv,
            con(uc_p.transpose(2, 1, 0)).reshape(1, 1, CK - 1, D),
            con(ua_s.transpose(2, 3, 1, 0)).reshape(1, DEC_B, 2, 256), *s_kv,
            con(uc_s.transpose(2, 3, 1, 0)).reshape(1, DEC_B, CK - 1, D))
```

```python
from contextlib import ExitStack

import concourse.bass as bass
import numpy as np
from concourse import mybir

F32 = mybir.dt.float32
BF16 = mybir.dt.bfloat16
I32 = mybir.dt.int32
ALU = mybir.AluOpType
ACT = mybir.ActivationFunctionType
AX = mybir.AxisListType

P = 128
D = 1024
KD = D // P
SEQ = 512
DEC_B, DEC_T = 8, 4
SAMPLES = DEC_B * DEC_T
TOK = SEQ + SAMPLES
TILES = 5
HALF = TOK // 2
ROWS = [P, P, P, P, SAMPLES]
GROUPS = 3
HD = 64
SCALE = HD ** -0.5
NEG = -1e30
EXPERTS = 32
EGROUPS = 4
FE = 256
JOB = 64
ASSIGNED = 2 * TOK
XCOLS = ASSIGNED + JOB
MORE = (ASSIGNED - 1) // JOB
SLOT = 6144
SLOTS = 4
CK = 31
PE_CONV = (1, 4)
UP = SEQ + CK - 1
US = DEC_T + CK - 1
KEYS = [128, 256, 64]
KOFF = [0, 128, 384]
CACHED = 448
KV = 2 * CACHED + 4 * 256
C_ID, C_TRI, C_ONE, C_MEAN = 0, 128, 256, 384
C_SM = 512
C_SMALL = C_SM + CACHED + 3 * SAMPLES
(C_IOTA, C_IOTAP, C_E64, C_THR, C_VALID, C_GI, C_GIP, C_SEL) = (
    C_SMALL, C_SMALL + 32, C_SMALL + 64, C_SMALL + 96, C_SMALL + 104, C_SMALL + 109, C_SMALL + 113,
    C_SMALL + 117)
C_END = C_SEL + 36
V_GAIN = 0
V_GPK = 32
V_BP1, V_DWB, V_LNG, V_LNB, V_CA, V_DW = 48, 64, 72, 80, 88, 94
V_RB = V_DW + KD * CK
V_RW = V_RB + 72
V_END = V_RW + 2 * KD * 64
A_HT = 0
A_QK = A_HT + KD * TOK
A_V = A_QK + 12 * TOK
A_GB = A_V + TILES * 768
A_U = A_GB + 2 * TOK
A_YT = A_U + 2 * 514 + 2 * 48
A_AIN = A_YT + 2 * TOK
A_XN0 = A_QK
A_SC = 0
A_PT = 2560
A_QZ = 3840
A_PS = 0
A_PTC = A_PS + 544
A_PTN = A_PTC + 512
A_OS = A_PTN + 384
R_QBD = KV * 2
R_PT, R_QZ = 4096, 4096 + 1280
B_U = KD * TOK
B_US = B_U + KD * UP
B_C = B_US + KD * DEC_B * US
B_SIG = B_C + KD * TOK
B_WIN = B_SIG + 2 * TOK
B_STD = B_WIN + SAMPLES * CK
B_ROW = B_STD + TOK
M_XN = 0
M_HT = TILES * D
M_XS = 0
M_STG = 9472
M_XJ = M_STG + 2 * D
M_SG = M_XJ + 2 * KD * JOB
M_ACT = M_SG + 2 * P
M_AT = M_ACT + 2 * P
M_Y = M_AT + 2 * P
M_YG = M_Y + 2 * 512
M_R = M_YG
M_EX = M_YG
M_GF = M_STG + D
ARENA = max(B_ROW + D, A_YT + 4 * TOK, M_YG + 4 * D)


def program(nc, x_in, w_mix0, kv_in, w_out, w_pw1, w_pw2, w_moe, smalls, consts, masks, rows, st_a, st_c,
            y_out, k_out, v_out, ua_p_out, ua_s_out, uc_p_out, uc_s_out):
    ctx = ExitStack()
    with ctx:
        def sb(name, shape, dt=F32):
            return ctx.enter_context(nc.sbuf_tensor(name, shape, dt))

        def sem(name):
            return ctx.enter_context(nc.semaphore(name))

        xs_dram = nc.dram_tensor("rows_by_expert", (ASSIGNED, D), F32, kind="Internal").ap()
        ys_dram = nc.dram_tensor("expert_outputs", ((EXPERTS + MORE) * JOB, D), F32, kind="Internal").ap()
        ring = sb("ring", [P, SLOTS, SLOT])
        X = sb("X", [P, TILES, D])
        cst = sb("cst", [P, C_END])
        sv = sb("sv", [P, V_END])
        ar = sb("ar", [P, ARENA])
        stat = sb("stat", [P, 3, 8])
        vec = sb("vec", [P, 64])
        mb = sb("mb", [P, P + 1280], BF16)
        eps = sb("eps", [P, 2])
        cw = sb("cw", [P, TILES, 2])
        ix = sb("ix", [P, TILES, 4], I32)
        jt = sb("jt", [1, 3 * EXPERTS], I32)
        psum = ctx.enter_context(nc.psum_tensor("psum", [P, 8, 512], F32))

        def view(off, n, pat=None, parts=P, **dims):
            a = ar[0:parts, off:off + n]
            return a.rearrange(pat, **dims) if pat else a

        ident = cst[:, C_ID:C_ID + P]
        ones = cst[:, C_ONE:C_ONE + P]

        def bcast(ap, shape):
            return ap.to_broadcast(shape)

        x_in_done = sem("x_in_done")
        consts_in = sem("consts_in")
        masks_in = sem("masks_in")
        masks_made = sem("masks_made")
        smalls_in = sem("smalls_in")
        proj_w = [sem(f"proj_w{c}") for c in range(4)]
        kv_w = [sem(f"kv_w{c}") for c in range(3)]
        wout_w = sem("wout_w")
        pw1_w = [sem(f"pw1_w{c}") for c in range(4)]
        pw2_w = [sem(f"pw2_w{c}") for c in range(2)]
        state_a_in = sem("state_a_in")
        state_c_in = sem("state_c_in")
        row_in = sem("row_in")
        zeros_made = sem("zeros_made")
        zeros_out = sem("zeros_out")
        outs_done = sem("outs_done")
        dve_link = sem("dve_link")
        act_link = sem("act_link")
        pool_link = sem("pool_link")
        stats_set = sem("stats_set")
        root_ready = sem("root_ready")
        inv_ready = sem("inv_ready")
        xn_ready = sem("xn_ready")
        turned = sem("turned")
        hT_ready = sem("hT_ready")
        proj_done = sem("proj_done")
        proj_kept = sem("proj_kept")
        u_made = sem("u_made")
        ya_made = sem("ya_made")
        qbd_made = sem("qbd_made")
        ss_done = sem("ss_done")
        ss_max = sem("ss_max")
        ss_exp = sem("ss_exp")
        ss_norm = sem("ss_norm")
        ss_turned = sem("ss_turned")
        ss_kept = sem("ss_kept")
        so_done = sem("so_done")
        so_sum = sem("so_sum")
        so_turned = sem("so_turned")
        so_kept = sem("so_kept")
        qz_zero = sem("qz_zero")
        qz_ready = sem("qz_ready")
        s_done = sem("s_done")
        max_ready = sem("max_ready")
        exp_done = sem("exp_done")
        p_ready = sem("p_ready")
        pt_done = sem("pt_done")
        pt_kept = sem("pt_kept")
        o_done = sem("o_done")
        o_kept = sem("o_kept")
        wo_done = sem("wo_done")
        x_updated = sem("x_updated")
        z_done = sem("z_done")
        sig_ready = sem("sig_ready")
        u_ready = sem("u_ready")
        conv_done = sem("conv_done")
        diag_made = sem("diag_made")
        pe_conv_done = sem("pe_conv_done")
        pe_conv_kept = sem("pe_conv_kept")
        sconv_made = sem("sconv_made")
        sconv_summed = sem("sconv_summed")
        sconv_kept = sem("sconv_kept")
        mean_done = sem("mean_done")
        centred = sem("centred")
        squared = sem("squared")
        var_done = sem("var_done")
        std_ready = sem("std_ready")
        scaled = sem("scaled")
        swish_done = sem("swish_done")
        pw2_done = sem("pw2_done")
        spread_kept = sem("spread_kept")
        y_ready = sem("y_ready")

        class Moe:
            def __init__(self):
                self.logits = sem("logits")
                self.gshift = sem("gshift")
                self.gexp = sem("gexp")
                self.eshift = sem("eshift")
                self.eexp = sem("eexp")
                self.picks = sem("picks")
                self.ranks = sem("ranks")
                self.routers = sem("routers")
                self.routers_kept = sem("routers_kept")
                self.places = sem("places")
                self.jobs = sem("jobs")
                self.scattered = sem("scattered")
                self.staged = [sem(f"staged_{b}") for b in range(6)]
                self.st_turned = sem("st_turned")
                self.xs_kept = sem("xs_kept")
                self.xs_tail = sem("xs_tail")
                self.w_in = [sem(f"w_in_{u}") for u in range(SLOTS)]
                self.xj_ready = sem("xj_ready")
                self.gu_done = sem("gu_done")
                self.sg_ready = sem("sg_ready")
                self.act_ready = sem("act_ready")
                self.at_done = sem("at_done")
                self.at_kept = sem("at_kept")
                self.down_done = sem("down_done")
                self.y_kept = sem("y_kept")
                self.y_out = [sem(f"y_out_{b}") for b in range(2)]
                self.gathered = [sem(f"gathered_{b}") for b in range(4)]
                self.all_out = sem("all_out")
                self.combined = sem("combined")

        class Further:
            def __init__(self, n):
                self.rows = sem(f"ex_rows{n}")
                self.gu = sem(f"ex_gu{n}")
                self.sg = sem(f"ex_sg{n}")
                self.act = sem(f"ex_act{n}")
                self.at = sem(f"ex_at{n}")
                self.atk = sem(f"ex_atk{n}")
                self.down = sem(f"ex_down{n}")
                self.kept = sem(f"ex_kept{n}")
                self.out = sem(f"ex_out{n}")
                self.stored = sem(f"ex_stored{n}")

        moe, ex = Moe(), [Further(0), Further(1)]
        block = ctx.enter_context(nc.Block())

        qkT = view(A_QK, 12 * TOK, "p (m t) -> p m t", m=12)
        vS = view(A_V, TILES * 768, "p (i c) -> p i c", i=TILES)
        gB = view(A_GB, 2 * TOK, "p (m t) -> p m t", m=2)
        aIn = view(A_AIN, 2 * TOK, "p (m t) -> p m t", m=2)
        uP = view(A_U, 2 * 514, "p (m t) -> p m t", m=2)
        uS = view(A_U + 2 * 514, 96, "p (m b t) -> p m b t", m=2, b=DEC_B)
        yT = view(A_YT, 4 * TOK, "p (m t) -> p m t", m=4)
        qz = [view(A_QZ, 384, "p (g t) -> p g t", g=3),
              ring[:, 3, R_QZ:R_QZ + 384].rearrange("p (g t) -> p g t", g=3)]
        pT = [view(A_PT, 1280), ring[:, 3, R_PT:R_PT + 1280]]
        qbd = ring[:, 2, R_QBD:R_QBD + 1536].rearrange("p (g r b c) -> p g r b c", g=3, r=2, b=DEC_B)
        cu = view(B_U, KD * UP, "p (k t) -> p k t", k=KD)
        cs = view(B_US, KD * DEC_B * US, "p (k b t) -> p k b t", k=KD, b=DEC_B)
        cT = view(B_C, KD * TOK, "p (k t) -> p k t", k=KD)
        sigm = view(B_SIG, 2 * TOK, "p (h t) -> p h t", h=2)
        std = view(B_STD, TOK)
        brow = view(B_ROW, D)
        win = [view(o, SAMPLES * CK, "p (b i j) -> p b i j", b=DEC_B, i=DEC_T) for o in (B_WIN, B_ROW)]
        gfin = view(M_GF, D)
        xsT = view(M_XS, KD * XCOLS, "p (k t) -> p k t", k=KD)
        stg = [view(M_STG + D * b, D) for b in range(2)] + [view(M_YG + D * b, D) for b in range(4)]
        xj = [view(M_XJ + 512 * b, 512, "p (k t) -> p k t", k=KD) for b in range(2)]
        sg = [view(M_SG + P * b, P) for b in range(2)]
        av = [view(M_ACT + P * b, P) for b in range(2)]
        aT = [view(M_AT + P * b, P) for b in range(2)]
        yj = [view(M_Y + 512 * b, 512) for b in range(2)]
        yg = [view(M_YG + D * b, D) for b in range(4)]
        xe = view(M_EX, 512, "p (k t) -> p k t", k=KD)
        sge, ave, aTe = (view(M_EX + 512 + P * b, P) for b in range(3))
        ye = view(M_EX + 896, 512)

        def hT_of(call):
            return view(M_HT if call % 2 else A_HT, KD * TOK, "p (k t) -> p k t", k=KD)

        def xn_of(call):
            o = (A_XN0, M_XN, A_XN0, M_XN, M_HT)[call]
            return view(o, TILES * D, "p (i c) -> p i c", i=TILES)

        def wait_residual(eng, call, i=TILES - 1):
            if call == 0:
                eng.wait_ge(x_in_done, 16 * TILES)
            else:
                eng.wait_ge(x_updated, TILES * (call - 1) + i + 1)

        def turn_bank(call, i, h):
            return 6 + h if call % 2 else (2 * i + h) % 4

        def diag(n, j):
            q = CK * n + j
            return ring[:, q // 16, 4096 + P * (q % 16):4096 + P * (q % 16) + P]

        def wait_conv(eng, k):
            eng.wait_ge(sconv_kept, k + 1)
            if k in PE_CONV:
                eng.wait_ge(pe_conv_kept, PE_CONV.index(k) + 1)
            else:
                eng.wait_ge(conv_done, k + 1 - sum(c < k for c in PE_CONV))

        def kt_of(b):
            return ring[:, b // 3, KV * (b % 3):KV * (b % 3) + 2 * CACHED].rearrange("p (r t) -> p r t", r=2)

        def v_of(b):
            o = KV * (b % 3) + 2 * CACHED
            return ring[:, b // 3, o:o + 1024].rearrange("p (t c) -> p t c", t=4)

        VT = [(P, 0), (P, 1), (P, 1), (64, 2)]

        def scores_of(n):
            return psum[:, 0:3, :].rearrange("p b c -> p (b c)")[:, 0:P * len(key_tiles(n))]

        def key_tiles(n):
            i = n // 4
            return [(0, j) for j in range(max(i - 1, 0), i + 1)] + [(g, j) for g in (1, 2) for j in range(i + 1)]

        @block.sync
        def _(sp):
            sp.dma_start(sv[:, :], smalls).then_inc(smalls_in, 16)
            sp.dma_start(cst[:, :], consts).then_inc(consts_in, 16)
            sp.dma_start(view(A_YT, 6 * P), masks).then_inc(masks_in, 16)
            sp.wait_ge(x_in_done, 16 * TILES)
            sp.dma_start(ring[:, 0, :], w_mix0[0]).then_inc(proj_w[0], 16)
            sp.dma_start(ring[:, 1, :], w_mix0[1]).then_inc(proj_w[1], 16)
            sp.dma_start(ring[:, 2, :], w_mix0[2]).then_inc(proj_w[2], 16)
            sp.wait_ge(zeros_out, 16 * 8)
            sp.dma_start(ring[:, 3, :], w_mix0[3]).then_inc(proj_w[3], 16)
            for c, m in enumerate((6, 12, 17)):
                n = KV * (3 if c < 2 else 2)
                sp.wait_ge(proj_done, m)
                sp.dma_start(ring[:, c, 0:n], kv_in[c, :, 0:n]).then_inc(kv_w[c], 16)
            sp.wait_ge(proj_done, 23)
            sp.dma_start(ring[:, 3, 0:4096], w_out).then_inc(wout_w, 16)

            def experts(n):
                for u in (2, 0, 1, 3) if n == 0 else (2, 3, 0, 1):
                    if n == 0:
                        if u < 3:
                            sp.wait_ge(so_done, 1)
                        else:
                            sp.wait_ge(wo_done, TILES)
                    elif u >= 2:
                        sp.wait_ge(z_done, 2 * KD)
                        sp.wait_ge(pe_conv_done, len(PE_CONV))
                    else:
                        sp.wait_ge(pw2_done, TILES)
                    sp.dma_start(ring[:, u, :], w_moe[n, u]).then_inc(moe.w_in[u], 16)
                sp.wait_ge(moe.jobs, n + 1)
                sp.wait_ge(moe.scattered, 160 * (n + 1))
                for t in range(9):
                    if t >= 6:
                        sp.wait_ge(moe.st_turned, 18 * n + 2 * (t - 5))
                    r = min(P, ASSIGNED - P * t)
                    sp.dma_start(stg[t % 6][0:r, :], xs_dram[P * t:P * t + r, :]).then_inc(moe.staged[t % 6], 16)
                with sp.Fori(1, EXPERTS // SLOTS) as it:
                    for u in range(SLOTS):
                        sp.wait_ge(moe.down_done, 4 * it + (EXPERTS * n + u - 3))
                        sp.dma_start(ring[:, u, :], w_moe[n, bass.ds(4 * it + u, 1), :, :].rearrange(
                            "a p c -> (a p) c")).then_inc(moe.w_in[u], 16)

            experts(0)
            sp.wait_ge(moe.all_out, 1)
            for c in range(4):
                sp.dma_start(ring[:, c, 0:4096], w_pw1[c]).then_inc(pw1_w[c], 16)
            for c in range(2):
                sp.wait_ge(z_done, 4 * (c + 1))
                sp.dma_start(ring[:, c, 0:4096], w_pw2[c]).then_inc(pw2_w[c], 16)
            experts(1)
            for i in range(TILES):
                sp.wait_ge(y_ready, i + 1)
                sp.dma_start(y_out[P * i:P * i + ROWS[i], :], view(D * i, D, parts=ROWS[i])).then_inc(outs_done, 16)
            sp.wait_ge(outs_done, 16 * (TILES + 7))

        @block.gpsimd
        def _(pool):
            nc.gpsimd.memset(ring[:, 3, 0:D], 0.0).then_inc(zeros_made, 1)
            pool.wait_ge(zeros_made, 1)
            pool.wait_ge(proj_w[1], 16)
            for t in range(8):
                o = EXPERTS * JOB + P * t
                pool.dma_start(ys_dram[o:o + P, :], ring[:, 3, 0:D]).then_inc(zeros_out, 16)
            nc.gpsimd.memset(uP[:, :, 0:2], 0.0).then_inc(pool_link, 1)
            pool.dma_start(uS[:, :, :, 0:2], st_a).then_inc(state_a_in, 16)
            pool.wait_ge(proj_kept, 6)
            pool.wait_ge(proj_done, 17)
            nc.gpsimd.memset(ring[:, 2, R_QBD:R_QBD + 1536], 0.0).then_inc(pool_link, 1)
            pool.wait_ge(pool_link, 2)
            made = 0
            for g in range(GROUPS):
                for r in range(2):
                    for hh in range(2):
                        for bb in range(2):
                            src = qkT[64 * hh:64 * hh + 64, 2 * g + r, SEQ:TOK].rearrange(
                                "p (q b i) -> p q b i", q=4, b=2)[:, :, bb, :]
                            c = 16 * bb + 4 * (2 * r + hh)
                            dst = qbd[64 * hh:64 * hh + 64, g, r, :, :].rearrange(
                                "p (q b) c -> p q b c", b=2)[:, :, bb, c:c + 4]
                            nc.gpsimd.tensor_copy(dst, src).then_inc(qbd_made, 1)
                            made += 1
                            pool.wait_ge(qbd_made, made)
            pool.wait_ge(proj_done, 23)
            for h in range(2):
                nc.gpsimd.memset(qz[h][64 * (1 - h):64 * (1 - h) + 64, :, :], 0.0).then_inc(qz_zero, 1)
                pool.wait_ge(qz_zero, h + 1)
            for n in range(16):
                i, h = n // 4, n % 4
                hh = h % 2
                if n >= 2:
                    pool.wait_ge(s_done, n - 1)
                if n:
                    pool.wait_ge(qz_ready, n)
                nc.gpsimd.tensor_copy(
                    qz[hh][64 * hh:64 * hh + 64, :, :],
                    qkT[64 * hh:64 * hh + 64, h // 2:6:2, P * i:P * i + P]).then_inc(qz_ready, 1)

            def experts(n):
                pool.wait_ge(moe.places, n + 1)
                for i in range(TILES):
                    for k in range(2):
                        pool.indirect_dma_start(
                            xs_dram, bass.IndirectOffsetOnAxis(ix[0:ROWS[i], i, k:k + 1], 0),
                            xn_of(2 * n + 1)[0:ROWS[i], i, :], None).then_inc(moe.scattered, 16)
                pool.wait_ge(moe.xs_tail, n + 1)
                pool.wait_ge(moe.jobs, n + 1)

                def rows_of(it, u, first):
                    at = pool.value_load(jt[0:1, bass.ds(4 * it + u, 1)], min_val=0, max_val=ASSIGNED)
                    if not first or u >= 2:
                        pool.wait_ge(moe.gu_done, 4 * it + (EXPERTS * n + u - 1))
                    nc.gpsimd.tensor_copy(xj[u % 2], xsT[:, :, bass.ds(at, JOB)]).then_inc(moe.xj_ready, 1)

                def further_rows(it, u):
                    at, chunks, before = (pool.value_load(jt[0:1, bass.ds(4 * it + (EXPERTS * w + u), 1)],
                                                          min_val=0, max_val=ASSIGNED) for w in range(3))
                    with pool.If(chunks > 0):
                        with pool.Fori(0, chunks) as c:
                            pool.wait_ge(ex[n].down, before + c + 1)
                            o = nc.s_assert_within(at + JOB * c + JOB, 0, ASSIGNED,
                                                   skip_runtime_bounds_check_because="the chunk has a row")
                            nc.gpsimd.tensor_copy(xe, xsT[:, :, bass.ds(o, JOB)]).then_inc(ex[n].rows, 1)

                def job_rows(it, first):
                    for u in range(SLOTS + 1):
                        if u < SLOTS:
                            rows_of(it, u, first)
                        if u:
                            further_rows(it, u - 1)

                job_rows(0, True)
                with pool.Fori(1, EXPERTS // SLOTS) as it:
                    job_rows(it, False)
                pool.wait_ge(moe.all_out, n + 1)
                for q in range(2 * TILES):
                    i, k = q // 2, q % 2
                    if q >= 4:
                        if k:
                            pool.wait_ge(x_updated, TILES * (2 * n + 1) + i - 1)
                        else:
                            pool.wait_ge(moe.combined, TILES * n + i - 1)
                    pool.indirect_dma_start(
                        yg[q % 4][0:ROWS[i], :], None, ys_dram,
                        bass.IndirectOffsetOnAxis(ix[0:ROWS[i], i, 2 + k:3 + k], 0)).then_inc(moe.gathered[q % 4], 16)

            experts(0)
            pool.wait_ge(hT_ready, 30)
            nc.gpsimd.memset(cu[:, :, 0:CK - 1], 0.0).then_inc(pool_link, 1)
            pool.dma_start(cs[:, :, :, 0:CK - 1], st_c).then_inc(state_c_in, 16)
            for c in range(KD):
                pool.wait_ge(u_ready, c + 1)
                if c >= 2:
                    pool.wait_ge(sconv_summed, c - 1)
                rows_ = cs[:, c, :, :]
                windows = bass.AP(rows_.tensor, rows_.offset, [rows_.ap[0], [US, DEC_B], [1, DEC_T], [1, CK]])
                taps = sv[:, V_DW + CK * c:V_DW + CK * c + CK]
                nc.gpsimd.tensor_tensor(win[c % 2], windows, bcast(taps[:, None, None, :], [P, DEC_B, DEC_T, CK]), ALU.mult
                                        ).then_inc(sconv_made, 1)
            experts(1)

        @block.scalar
        def _(act):
            for i in range(TILES):
                act.dma_start(X[0:ROWS[i], i, :], x_in[P * i:P * i + ROWS[i], :]).then_inc(x_in_done, 16)
            links = [0]

            def link(ins):
                links[0] += 1
                ins.then_inc(act_link, 1)
                act.wait_ge(act_link, links[0])

            def norm(call):
                act.wait_ge(stats_set, 1)
                xn = xn_of(call)
                for i in range(TILES):
                    r = ROWS[i]
                    if call % 2 and i == TILES - 1:
                        act.wait_ge(pw2_done if call == 3 else wo_done, TILES)
                        for q in range(4):
                            t = nc.scalar.activation(xn[0:r, i, 256 * q:256 * q + 256],
                                                     psum[32 * q:32 * q + 32, 2, 0:256], ACT.Copy)
                            if q < 3:
                                link(t)
                        t.then_inc(spread_kept, 1)
                    wait_residual(act, call, i)
                    link(nc.scalar.activation(xn[0:r, i, :], X[0:r, i, :], ACT.Square,
                                              accum_out=stat[0:r, 0, i:i + 1]))
                    nc.scalar.activation(stat[0:r, 1, i:i + 1], stat[0:r, 0, i:i + 1], ACT.Sqrt, scale=1.0 / D,
                                         bias=eps[0:r, 0:1]).then_inc(root_ready, 1)
                    if call < 4:
                        act.wait_ge(inv_ready, TILES * call + i + 1)
                        nc.scalar.activation(xn[0:r, i, :], X[0:r, i, :], ACT.Copy,
                                             scale=stat[0:r, 2, i:i + 1]).then_inc(xn_ready, 1)

            norm(0)
            for m in range(23):
                b = 2 * (m % 3)
                if 19 <= m <= 20:
                    continue
                act.wait_ge(proj_done, m + 1)
                if m == 16:
                    for q in range(4):
                        t = nc.scalar.activation(vS[0:SAMPLES, 4, 192 * q:192 * q + 192],
                                                 psum[32 * q:32 * q + 32, b, 0:192], ACT.Copy)
                        if q < 3:
                            link(t)
                    t.then_inc(proj_kept, 1)
                    continue
                if 12 <= m < 16:
                    r = ROWS[m - 12]
                    nc.scalar.activation(vS[0:r, m - 12, :].rearrange("p (h c) -> p h c", h=2),
                                         psum[0:r, b:b + 2, 0:384], ACT.Copy).then_inc(proj_kept, 1)
                    continue
                dst = qkT[:, m, :] if m < 12 else (aIn[:, m - 17, :] if m < 19 else gB[:, m - 21, :])
                nc.scalar.activation(dst.rearrange("p (h t) -> p h t", h=2), psum[:, b:b + 2, 0:HALF],
                                     ACT.Copy, scale=SCALE if m < 6 else 1.0).then_inc(proj_kept, 1)
                if m == 11:
                    act.wait_ge(proj_kept, 12)
                    act.dma_start(k_out, qkT[:, 6:12, :]).then_inc(outs_done, 16)
                if m == 17:
                    act.wait_ge(proj_kept, 17)
                    act.dma_start(v_out[0:SEQ, :].rearrange("(i p) c -> p i c", p=P), vS[:, 0:4, :]
                                  ).then_inc(outs_done, 16)
                    act.dma_start(v_out[SEQ:TOK, :], vS[0:SAMPLES, 4, :]).then_inc(outs_done, 16)
            act.wait_ge(u_made, 6)
            act.dma_start(ua_p_out, uP[:, :, SEQ:SEQ + 2]).then_inc(outs_done, 16)
            act.dma_start(ua_s_out, uS[:, :, :, 4:6]).then_inc(outs_done, 16)

            act.wait_ge(ss_max, 1)
            nc.scalar.activation(view(A_PS, 544), view(A_PS, 544), ACT.Exp, bias=vec[:, 0:1],
                                 accum_out=vec[:, 1:2]).then_inc(ss_exp, 1)
            act.wait_ge(ss_turned, 1)
            nc.scalar.activation(view(A_PTC, 512), psum[:, 2, :], ACT.Copy).then_inc(ss_kept, 1)
            nc.scalar.activation(view(A_PTN, 384, parts=32), psum[0:32, 3, 0:384], ACT.Copy).then_inc(ss_kept, 1)

            act.wait_ge(so_done, 1)
            nc.scalar.activation(view(A_OS, 512, "p (b c) -> p b c", b=2), psum[:, 4:6, 0:256], ACT.Copy
                                 ).then_inc(so_sum, 1)

            def exps(n):
                sc = view(A_SC + 1280 * (n % 2), P * len(key_tiles(n)))
                if n == 0:
                    act.wait_ge(so_kept, 8)
                if n >= 2:
                    act.wait_ge(pt_done, n - 1)
                act.wait_ge(max_ready, n + 1)
                nc.scalar.activation(sc, scores_of(n), ACT.Exp, bias=vec[:, 4 + n % 2:5 + n % 2],
                                     accum_out=vec[:, 6 + n % 2:7 + n % 2]).then_inc(exp_done, 1)

            def keep_o(n):
                i, h = n // 4, n % 4
                hh = h % 2
                act.wait_ge(o_done, n + 1)
                nc.scalar.activation(yT[64 * hh:64 * hh + 64, 2 + h // 2, P * i:P * i + P],
                                     psum[64 * hh:64 * hh + 64, 6 + (n // 2) % 2, 0:P], ACT.Copy
                                     ).then_inc(o_kept, 1)

            exps(0)
            for n in range(16):
                w = P * len(key_tiles(n))
                if n < 15:
                    exps(n + 1)
                act.wait_ge(pt_done, n + 1)
                if n >= 2:
                    act.wait_ge(o_done, n - 1)
                nc.scalar.activation(pT[n % 2][:, 0:w], psum[:, 3:6, :].rearrange("p b c -> p (b c)")[:, 0:w],
                                     ACT.Copy).then_inc(pt_kept, 1)
                if n:
                    keep_o(n - 1)
            keep_o(15)

            def experts(n):
                act.wait_ge(moe.routers, n + 1)
                nc.scalar.activation(view(M_R, TOK).rearrange("p (h t) -> p h t", h=2), psum[:, 0:2, 0:HALF],
                                     ACT.Copy).then_inc(moe.routers_kept, 1)
                act.wait_ge(moe.gshift, n + 1)
                g4 = view(M_R + 724, 20)
                nc.scalar.activation(g4, g4, ACT.Exp).then_inc(moe.gexp, 1)
                act.wait_ge(moe.eshift, n + 1)
                nc.scalar.activation(vec[:, 30:35], vec[:, 25:30], ACT.Exp).then_inc(moe.eexp, 1)
                act.sem_inc(ex[n].kept, 1)
                act.wait_ge(moe.jobs, n + 1)
                if n == 1:
                    act.wait_ge(moe.st_turned, 36)
                    act.dma_start(gfin, rows[1:2, :].to_broadcast([P, D])).then_inc(row_in, 16)

                def silu(it, u, first):
                    act.wait_ge(moe.gu_done, 4 * it + (EXPERTS * n + u + 1))
                    if not first or u >= 2:
                        act.wait_ge(moe.act_ready, 4 * it + (EXPERTS * n + u - 1))
                    nc.scalar.activation(sg[u % 2], psum[:, u % 2, 0:P], ACT.Silu).then_inc(moe.sg_ready, 1)

                def store(job, y, done):
                    rows = ys_dram.rearrange("(j r) c -> j r c", r=JOB)[bass.ds(job, 1), :, :].rearrange(
                        "a r c -> (a r) c")
                    for q in range(2):
                        act.dma_start(rows[:, 512 * q:512 * q + 512], y[64 * q:64 * q + 64, :]).then_inc(done, 16)

                def keep_y(it, u, first):
                    b = u % 2
                    act.wait_ge(moe.down_done, 4 * it + (EXPERTS * n + u + 1))
                    if not first or u >= 2:
                        act.wait_ge(moe.y_out[b], 64 * it + (512 * n + 32 * (u // 2)))
                    nc.scalar.activation(yj[b], psum[:, 4 + b, :], ACT.Copy).then_inc(moe.y_kept, 1)
                    act.wait_ge(moe.y_kept, 4 * it + (EXPERTS * n + u + 1))
                    store(4 * it + u, yj[b], moe.y_out[b])

                def further(it, u):
                    chunks, before = (act.value_load(jt[0:1, bass.ds(4 * it + (EXPERTS * w + u), 1)],
                                                     min_val=0, max_val=MORE) for w in (1, 2))
                    with act.If(chunks > 0):
                        with act.Fori(0, chunks) as c:
                            act.wait_ge(ex[n].gu, before + c + 1)
                            nc.scalar.activation(sge, psum[:, 6, 0:P], ACT.Silu).then_inc(ex[n].sg, 1)
                            act.wait_ge(ex[n].down, before + c + 2)
                            nc.scalar.activation(ye, psum[:, 6, :], ACT.Copy).then_inc(ex[n].kept, 1)
                            act.wait_ge(ex[n].kept, before + c + 2)
                            job = nc.s_assert_within(before + c + EXPERTS, EXPERTS, EXPERTS + MORE - 1,
                                                     skip_runtime_bounds_check_because="at most MORE chunks")
                            store(job, ye, ex[n].out)
                            act.wait_ge(ex[n].out, 32 * (before + c) + 32)
                            act.sem_inc(ex[n].stored, 1)

                def body(it, first):
                    for u in range(SLOTS + 1):
                        if u < SLOTS:
                            silu(it, u, first)
                        if u:
                            further(it, u - 1)
                            keep_y(it, u - 1, first)

                body(0, True)
                with act.Fori(1, EXPERTS // SLOTS) as it:
                    body(it, False)
                for b in range(2):
                    act.wait_ge(moe.y_out[b], 512 * (n + 1))
                act.sem_inc(moe.all_out, 1)

            act.wait_ge(outs_done, 16 * 5)
            norm(1)
            experts(0)

            norm(2)
            act.dma_start(brow, rows[0:1, :].to_broadcast([P, D])).then_inc(row_in, 16)
            def keep_sconv(c):
                act.wait_ge(sconv_summed, c + 1)
                out = cT[:, c, SEQ:TOK]
                nc.scalar.activation(out, out, ACT.Identity, bias=sv[:, V_DWB + c:V_DWB + c + 1]
                                     ).then_inc(sconv_kept, 1)

            def keep_pe_conv(n):
                c = PE_CONV[n]
                act.wait_ge(pe_conv_done, n + 1)
                nc.scalar.activation(cT[:, c, 0:SEQ], psum[:, 6 + n, :], ACT.Identity,
                                     bias=sv[:, V_DWB + c:V_DWB + c + 1]).then_inc(pe_conv_kept, 1)

            for c in range(KD):
                if c == 6:
                    keep_pe_conv(0)
                b = 2 * ((2 * c) % 3)
                act.wait_ge(z_done, 2 * c + 1)
                if c >= 2:
                    act.wait_ge(u_ready, c - 1)
                nc.scalar.activation(sigm[:, c % 2, :].rearrange("p (h t) -> p h t", h=2), psum[:, b:b + 2, 0:HALF],
                                     ACT.Sigmoid, bias=sv[:, V_BP1 + 8 + c:V_BP1 + 9 + c]).then_inc(sig_ready, 1)
                if c < 2:
                    for j in range(CK):
                        o = V_DW + CK * PE_CONV[c] + j
                        nc.scalar.activation(diag(c, j), ident, ACT.Copy, scale=sv[:, o:o + 1]).then_inc(diag_made, 1)
                else:
                    keep_sconv(c - 2)
            keep_sconv(6)
            keep_pe_conv(1)
            keep_sconv(7)
            act.wait_ge(u_ready, KD)
            act.wait_ge(state_c_in, 16)
            act.dma_start(uc_p_out, cu[:, :, SEQ:UP]).then_inc(outs_done, 16)
            act.dma_start(uc_s_out, cs[:, :, :, DEC_T:US]).then_inc(outs_done, 16)
            sq = hT_of(2)
            for k in range(KD):
                act.wait_ge(centred, k + 1)
                nc.scalar.activation(sq[:, k, :], cT[:, k, :], ACT.Square).then_inc(squared, 1)
            act.wait_ge(var_done, 1)
            nc.scalar.activation(std.rearrange("p (h t) -> p h t", h=2), psum[:, 4:6, 0:HALF], ACT.Sqrt,
                                 bias=eps[:, 1:2]).then_inc(std_ready, 1)
            for k in range(KD):
                act.wait_ge(scaled, k + 1)
                nc.scalar.activation(cT[:, k, :], cT[:, k, :], ACT.Silu, scale=sv[:, V_LNG + k:V_LNG + k + 1],
                                     bias=sv[:, V_LNB + k:V_LNB + k + 1]).then_inc(swish_done, 1)
            act.wait_ge(outs_done, 16 * 7)
            norm(3)
            experts(1)
            norm(4)

        @block.vector
        def _(dve):
            links = [0]

            def link(ins):
                links[0] += 1
                ins.then_inc(dve_link, 1)
                dve.wait_ge(dve_link, links[0])

            nc.vector.memset(eps[:, 0:1], 1e-6).then_inc(dve_link, 1)
            nc.vector.memset(eps[:, 1:2], 1e-5).then_inc(dve_link, 1)
            links[0] = 2
            dve.wait_ge(dve_link, 2)
            nc.vector.memset(stat[:, :, :], 1.0).then_inc(stats_set, 1)
            dve.wait_ge(consts_in, 16)
            dve.wait_ge(smalls_in, 16)

            def norm(call, update):
                hT = hT_of(call)
                for i in range(TILES + 1):
                    if i < TILES:
                        r = ROWS[i]
                        update(i)
                        dve.wait_ge(root_ready, TILES * call + i + 1)
                        nc.vector.reciprocal(stat[0:r, 2, i:i + 1], stat[0:r, 1, i:i + 1]).then_inc(inv_ready, 1)
                    if i:
                        t = i - 1
                        r = ROWS[t]
                        for h in range(2):
                            dve.wait_ge(turned, 10 * call + 2 * t + h + 1)
                            g = sv[:, V_GAIN + 8 * call + 4 * h:V_GAIN + 8 * call + 4 * h + 4]
                            nc.vector.tensor_tensor(
                                hT[:, 4 * h:4 * h + 4, P * t:P * t + r],
                                psum[:, turn_bank(call, t, h), :].rearrange("p (k t) -> p k t", k=4)[:, :, 0:r],
                                bcast(g[:, :, None], [P, 4, r]), ALU.mult).then_inc(hT_ready, 1)

            norm(0, lambda i: None)
            dve.wait_ge(masks_in, 16)
            nc.vector.tensor_copy(mb[:, 0:P], ident).then_inc(masks_made, 1)
            nc.vector.tensor_copy(mb[:, P:3 * P], view(A_YT, 2 * P)).then_inc(masks_made, 1)
            for g in (1, 2):
                src = view(A_YT + 2 * P * g, 2 * P)
                o = 3 * P + 4 * P * (g - 1)
                nc.vector.tensor_copy(mb[:, o:o + 3 * P].rearrange("p (j k) -> p j k", j=3),
                                      bcast(src[:, 0:P][:, None, :], [P, 3, P])).then_inc(masks_made, 1)
                nc.vector.tensor_copy(mb[:, o + 3 * P:o + 4 * P], src[:, P:2 * P]).then_inc(masks_made, 1)
            dve.wait_ge(masks_made, 6)
            for c in range(2):
                b = 2 * ((19 + c) % 3)
                dve.wait_ge(proj_done, 20 + c)
                dve.wait_ge(proj_kept, 18 + c)
                if c == 0:
                    dve.wait_ge(state_a_in, 16)
                    dve.wait_ge(pool_link, 1)
                nc.vector.tensor_tensor(uP[:, c, 2:2 + HALF], psum[:, b, 0:HALF], aIn[:, c, 0:HALF],
                                        ALU.mult).then_inc(u_made, 1)
                nc.vector.tensor_tensor(uP[:, c, 2 + HALF:2 + SEQ], psum[:, b + 1, 0:SEQ - HALF],
                                        aIn[:, c, HALF:SEQ], ALU.mult).then_inc(u_made, 1)
                nc.vector.tensor_tensor(
                    uS[:, c, :, 2:6], psum[:, b + 1, SEQ - HALF:HALF].rearrange("p (b t) -> p b t", b=DEC_B),
                    aIn[:, c, SEQ:TOK].rearrange("p (b t) -> p b t", b=DEC_B), ALU.mult).then_inc(u_made, 1)
            dve.wait_ge(u_made, 6)
            dve.wait_ge(proj_kept, 21)
            for c in range(2):
                yp = yT[:, c, 0:SEQ]
                ys = yT[:, c, SEQ:TOK].rearrange("p (b t) -> p b t", b=DEC_B)
                for j in range(3):
                    w = sv[:, V_CA + 3 * c + j:V_CA + 3 * c + j + 1]
                    for dst, src in ((yp, uP[:, c, j:j + SEQ]), (ys, uS[:, c, :, j:j + 4])):
                        if j == 0:
                            link(nc.vector.tensor_scalar(dst, src, w, None, ALU.mult))
                        else:
                            link(nc.vector.scalar_tensor_tensor(out=dst, in0=src, scalar=w, in1=dst,
                                                                op0=ALU.mult, op1=ALU.add))
                nc.vector.tensor_tensor(yT[:, c, :], yT[:, c, :], gB[:, c, :], ALU.mult).then_inc(ya_made, 1)

            ps = view(A_PS, 544)
            dve.wait_ge(ss_done, 1)
            link(nc.vector.tensor_tensor(ps[:, 0:CACHED], psum[:, 0, 0:CACHED], cst[:, C_SM:C_SM + CACHED], ALU.add))
            link(nc.vector.tensor_tensor(ps[:, CACHED:544], psum[:, 1, 0:96], cst[:, C_SM + CACHED:C_SM + 544],
                                         ALU.add))
            nc.vector.tensor_reduce(vec[:, 0:1], ps, AX.X, ALU.max, negate=True).then_inc(ss_max, 1)
            dve.wait_ge(ss_exp, 1)
            link(nc.vector.reciprocal(vec[:, 2:3], vec[:, 1:2]))
            nc.vector.tensor_scalar(ps, ps, vec[:, 2:3], None, ALU.mult).then_inc(ss_norm, 1)
            dve.wait_ge(so_turned, 1)
            for r in range(2):
                for hh in range(2):
                    for bb in range(2):
                        c = P * (2 * bb + r)
                        src = psum[64 * hh:64 * hh + 64, 0, c:c + P].rearrange("p (q c) -> p q c", q=4)
                        o = 16 * bb + 4 * (2 * r + hh)
                        dst = yT[64 * hh:64 * hh + 64, 2 + r, SEQ:TOK].rearrange(
                            "p (q b t) -> p q b t", q=4, b=2)[:, :, bb, :]
                        nc.vector.tensor_copy(dst, src[:, :, o:o + 4]).then_inc(so_kept, 1)

            def maxima(n):
                dve.wait_ge(s_done, n + 1)
                nc.vector.tensor_reduce(vec[:, 4 + n % 2:5 + n % 2], scores_of(n), AX.X, ALU.max, negate=True
                                        ).then_inc(max_ready, 1)

            def normalise(n):
                sc = view(A_SC + 1280 * (n % 2), P * len(key_tiles(n)))
                dve.wait_ge(exp_done, n + 1)
                link(nc.vector.reciprocal(vec[:, 8 + n % 2:9 + n % 2], vec[:, 6 + n % 2:7 + n % 2]))
                nc.vector.tensor_scalar(sc, sc, vec[:, 8 + n % 2:9 + n % 2], None, ALU.mult).then_inc(p_ready, 1)

            maxima(0)
            for n in range(16):
                normalise(n)
                if n < 15:
                    maxima(n + 1)

            def add_from_psum(call, done):
                def update(i):
                    r, b = ROWS[i], 2 * (i % 3)
                    if i == TILES - 1:
                        dve.wait_ge(spread_kept, call // 2 + 1)
                        nc.vector.tensor_tensor(X[0:r, i, :], X[0:r, i, :], xn_of(call)[0:r, i, :], ALU.add
                                                ).then_inc(x_updated, 1)
                        return
                    dve.wait_ge(done, i + 1)
                    nc.vector.tensor_tensor(X[0:r, i, :], X[0:r, i, :],
                                            psum[0:r, b:b + 2, :].rearrange("p b c -> p (b c)"), ALU.add
                                            ).then_inc(x_updated, 1)
                return update

            def combine(n):
                def update(i):
                    r = ROWS[i]
                    for k in range(2):
                        q = 2 * i + k
                        dve.wait_ge(moe.gathered[q % 4], 16 * ((3 if q % 4 < 2 else 2) * n + q // 4 + 1))
                        if k:
                            dve.wait_ge(moe.combined, TILES * n + i + 1)
                        nc.vector.scalar_tensor_tensor(out=X[0:r, i, :], in0=yg[q % 4][0:r, :],
                                                       scalar=cw[0:r, i, k:k + 1], in1=X[0:r, i, :],
                                                       op0=ALU.mult, op1=ALU.add
                                                       ).then_inc(x_updated if k else moe.combined, 1)
                return update

            def experts(n):
                o = [M_R]

                def new(k, pat=None, **dims):
                    o[0] += k
                    return view(o[0] - k, k, pat, **dims)

                def const(c, k):
                    return cst[:, c:c + k]

                S5 = [P, TILES, EXPERTS]
                new(TOK)
                L = new(180, "p (i e) -> p i e", i=TILES)
                g4 = new(20, "p (i e) -> p i e", i=TILES)
                t4 = new(20, "p (i e) -> p i e", i=TILES)
                em = new(160, "p (i e) -> p i e", i=TILES)
                tt = new(160, "p (i e) -> p i e", i=TILES)
                o1 = new(160, "p (i e) -> p i e", i=TILES)
                o2 = new(160, "p (i e) -> p i e", i=TILES)
                mk = new(160, "p (i e) -> p i e", i=TILES)
                rank = new(160, "p (i e) -> p i e", i=TILES)
                base = new(192, "p (i e) -> p i e", i=6)
                bigger = new(256, "p (e m) -> p e m", m=8)
                one = new(32)
                off = new(32)
                extra = new(32)
                inc = new(32)
                xb = new(32)
                d64 = new(32)
                gmax, gsum, gval, gidx = vec[:, 0:5], vec[:, 5:10], vec[:, 10:15], vec[:, 15:20]
                m1, m2, eidx = vec[:, 20:25], vec[:, 25:30], vec[:, 35:40]
                place = vec[:, 40:60].rearrange("p (i k) -> p i k", i=TILES)

                def tt_(out, a, b, op):
                    link(nc.vector.tensor_tensor(out, a, b, op))

                def ts_(out, a, s1, s2, op0, op1=ALU.bypass):
                    link(nc.vector.tensor_scalar(out, a, s1, s2, op0, op1))

                def red(out, a, op):
                    link(nc.vector.tensor_reduce(out, a, AX.X, op))

                def first_of(onehot, values, top, scratch, idx, iota, iotap, shape):
                    tt_(scratch, values, bcast(top[:, :, None], shape), ALU.is_ge)
                    link(nc.vector.scalar_tensor_tensor(
                        out=scratch, in0=scratch, scalar=-100.0, in1=bcast(iotap[:, None, :], shape),
                        op0=ALU.mult, op1=ALU.add))
                    red(idx, scratch, ALU.min)
                    tt_(onehot, bcast(iota[:, None, :], shape), bcast(idx[:, :, None], shape), ALU.is_equal)

                link(nc.vector.memset(L, 0.0))
                link(nc.vector.memset(base, 0.0))
                link(nc.vector.memset(one, 1.0))
                dve.wait_ge(moe.logits, n + 1)
                rb = sv[:, V_RB + 36 * n:V_RB + 36 * n + 36]
                tt_(L[:, 0:4, :], psum[:, 4, 0:144].rearrange("p (i e) -> p i e", i=4),
                    bcast(rb[:, None, :], [P, 4, 36]), ALU.add)
                tt_(L[0:SAMPLES, 4, :], psum[0:SAMPLES, 4, 144:180], rb[0:SAMPLES, :], ALU.add)
                gl = L[:, :, 0:EGROUPS]
                red(gmax, gl, ALU.max)
                nc.vector.tensor_tensor(g4, gl, bcast(gmax[:, :, None], [P, TILES, 4]), ALU.subtract
                                        ).then_inc(moe.gshift, 1)
                first_of(t4, gl, gmax, t4, gidx, const(C_GI, 4), const(C_GIP, 4), [P, TILES, 4])
                ts_(t4, t4, -1.0, 1e30, ALU.add, ALU.mult)
                for i in range(TILES):
                    tt_(em[:, i, :].rearrange("p (g e) -> p g e", g=4),
                        L[:, i, 4:36].rearrange("p (g e) -> p g e", g=4),
                        bcast(t4[:, i, :][:, :, None], [P, 4, 8]), ALU.add)
                red(m1, em, ALU.max)
                first_of(o1, em, m1, tt, eidx, const(C_IOTA, 32), const(C_IOTAP, 32), S5)
                link(nc.vector.scalar_tensor_tensor(out=em, in0=o1, scalar=-3e30, in1=em, op0=ALU.mult, op1=ALU.add))
                red(m2, em, ALU.max)
                first_of(o2, em, m2, tt, eidx, const(C_IOTA, 32), const(C_IOTAP, 32), S5)
                tt_(mk, o1, o2, ALU.add)
                nc.vector.tensor_tensor(mk, mk, bcast(const(C_VALID, 5)[:, :, None], S5), ALU.mult
                                        ).then_inc(moe.picks, 1)
                nc.vector.tensor_tensor(m2, m2, m1, ALU.subtract).then_inc(moe.eshift, 1)
                dve.wait_ge(moe.gexp, n + 1)
                red(gsum, g4, ALU.add)
                dve.wait_ge(moe.eexp, n + 1)
                te = vec[:, 30:35]
                ts_(gval, te, 1.0, None, ALU.add)
                tt_(gval, gval, gsum, ALU.mult)
                link(nc.vector.reciprocal(cw[:, :, 0], gval))
                tt_(cw[:, :, 1], cw[:, :, 0], te, ALU.mult)
                dve.wait_ge(moe.ranks, n + 1)
                for i in range(TILES):
                    tt_(base[:, i + 1, :], base[:, i, :], psum[:, 5, 32 * i:32 * i + 32], ALU.add)
                tt_(rank, psum[:, 6, 0:160].rearrange("p (i e) -> p i e", i=TILES), base[:, 0:TILES, :], ALU.add)
                cnt = base[:, TILES, :]

                def before(out, counts, incl):
                    link(nc.vector.tensor_tensor_scan(incl, counts, one, 0.0, ALU.add, ALU.bypass))
                    tt_(out, incl, counts, ALU.subtract)

                before(off, cnt, inc)
                tt_(tt, rank, bcast(off[:, None, :], S5), ALU.add)
                for k, oh in enumerate((o1, o2)):
                    tt_(em, oh, tt, ALU.mult)
                    red(place[:, :, k], em, ALU.add)
                tt_(bigger, bcast(cnt[:, :, None], [P, EXPERTS, 8]),
                    bcast(const(C_THR, 8)[:, None, :], [P, EXPERTS, 8]), ALU.is_gt)
                red(extra, bigger, ALU.add)
                before(xb, extra, inc)
                ts_(d64, xb, 64.0, 64.0 * 31, ALU.mult, ALU.add)
                tt_(d64, d64, const(C_E64, 32), ALU.subtract)
                ts_(tt, rank, 64.0, None, ALU.is_ge)
                tt_(tt, tt, bcast(d64[:, None, :], S5), ALU.mult)
                tt_(tt, tt, bcast(const(C_E64, 32)[:, None, :], S5), ALU.add)
                tt_(tt, tt, rank, ALU.add)
                for k, oh in enumerate((o1, o2)):
                    tt_(em, oh, tt, ALU.mult)
                    red(place[:, :, 2 + k], em, ALU.add)
                nc.vector.tensor_copy(ix[:, :, :], place).then_inc(moe.places, 1)
                for w, row in enumerate((off, extra, xb)):
                    last = nc.vector.tensor_copy(jt[0:1, EXPERTS * w:EXPERTS * (w + 1)], row[0:1, :])
                    if w < 2:
                        link(last)
                last.then_inc(moe.jobs, 1)
                for t in range(9):
                    r = min(P, ASSIGNED - P * t)
                    for h in range(2):
                        q = 2 * t + h
                        dve.wait_ge(moe.st_turned, 18 * n + q + 1)
                        g = sv[:, V_GPK + 8 * n + 4 * h:V_GPK + 8 * n + 4 * h + 4]
                        nc.vector.tensor_tensor(
                            xsT[:, 4 * h:4 * h + 4, P * t:P * t + r],
                            psum[:, q % 4, :].rearrange("p (k t) -> p k t", k=4)[:, :, 0:r],
                            bcast(g[:, :, None], [P, 4, r]), ALU.mult).then_inc(moe.xs_kept, 1)
                dve.wait_ge(moe.xs_kept, 18 * (n + 1))
                nc.vector.memset(xsT[:, :, ASSIGNED:XCOLS], 0.0).then_inc(moe.xs_tail, 1)
                dve.wait_ge(moe.jobs, n + 1)

                def gate_up(it, u, first):
                    dve.wait_ge(moe.sg_ready, 4 * it + (EXPERTS * n + u + 1))
                    if not first or u >= 2:
                        dve.wait_ge(moe.at_done, 4 * it + (EXPERTS * n + u - 1))
                    nc.vector.tensor_tensor(av[u % 2], sg[u % 2], psum[:, u % 2, P:2 * P], ALU.mult
                                            ).then_inc(moe.act_ready, 1)

                def keep_at(it, u, first):
                    dve.wait_ge(moe.at_done, 4 * it + (EXPERTS * n + u + 1))
                    if not first or u >= 2:
                        dve.wait_ge(moe.down_done, 4 * it + (EXPERTS * n + u - 1))
                    nc.vector.tensor_copy(aT[u % 2], psum[:, 2 + u % 2, 0:P]).then_inc(moe.at_kept, 1)

                def further(it, u):
                    chunks, before = (dve.value_load(jt[0:1, bass.ds(4 * it + (EXPERTS * w + u), 1)],
                                                     min_val=0, max_val=MORE) for w in (1, 2))
                    with dve.If(chunks > 0):
                        with dve.Fori(0, chunks) as c:
                            dve.wait_ge(ex[n].sg, before + c + 1)
                            nc.vector.tensor_tensor(ave, sge, psum[:, 6, P:2 * P], ALU.mult).then_inc(ex[n].act, 1)
                            dve.wait_ge(ex[n].at, before + c + 1)
                            nc.vector.tensor_copy(aTe, psum[:, 7, 0:P]).then_inc(ex[n].atk, 1)

                def steps(it, first):
                    gate_up(it, 0, first)
                    for u in range(1, SLOTS + 1):
                        if u < SLOTS:
                            gate_up(it, u, first)
                        further(it, u - 1)
                        keep_at(it, u - 1, first)

                steps(0, True)
                with dve.Fori(1, EXPERTS // SLOTS) as it:
                    steps(it, False)

            dve.wait_ge(outs_done, 16 * 5)
            norm(1, add_from_psum(1, wo_done))
            experts(0)

            norm(2, combine(0))
            dve.wait_ge(xn_ready, 3 * TILES)
            dve.wait_ge(row_in, 16)
            for i in range(TILES):
                r = ROWS[i]
                link(nc.vector.tensor_tensor(X[0:r, i, :], X[0:r, i, :], brow[0:r, :], ALU.add))

            def glu(c):
                b = 2 * ((2 * c + 1) % 3)
                ba = sv[:, V_BP1 + c:V_BP1 + c + 1]
                dve.wait_ge(z_done, 2 * c + 2)
                dve.wait_ge(sig_ready, c + 1)
                if c == 0:
                    dve.wait_ge(pool_link, 3)
                    dve.wait_ge(state_c_in, 16)
                s = sigm[:, c % 2, :]
                link(nc.vector.scalar_tensor_tensor(out=cu[:, c, CK - 1:CK - 1 + HALF], in0=psum[:, b, 0:HALF],
                                                    scalar=ba, in1=s[:, 0:HALF], op0=ALU.add, op1=ALU.mult))
                link(nc.vector.scalar_tensor_tensor(out=cu[:, c, CK - 1 + HALF:UP], in0=psum[:, b + 1, 0:SEQ - HALF],
                                                    scalar=ba, in1=s[:, HALF:SEQ], op0=ALU.add, op1=ALU.mult))
                nc.vector.scalar_tensor_tensor(
                    out=cs[:, c, :, CK - 1:US], in1=s[:, SEQ:TOK].rearrange("p (b t) -> p b t", b=DEC_B),
                    in0=psum[:, b + 1, SEQ - HALF:HALF].rearrange("p (b t) -> p b t", b=DEC_B),
                    scalar=ba, op0=ALU.add, op1=ALU.mult).then_inc(u_ready, 1)

            def conv(c):
                dve.wait_ge(u_ready, c + 1)
                out = cT[:, c, 0:SEQ]
                for j in range(CK):
                    w = sv[:, V_DW + CK * c + j:V_DW + CK * c + j + 1]
                    src = cu[:, c, j:j + SEQ]
                    if j == 0:
                        t = nc.vector.tensor_scalar(out, src, w, sv[:, V_DWB + c:V_DWB + c + 1], ALU.mult, ALU.add)
                    else:
                        t = nc.vector.scalar_tensor_tensor(out=out, in0=src, scalar=w, in1=out,
                                                           op0=ALU.mult, op1=ALU.add)
                    if j < CK - 1:
                        link(t)
                t.then_inc(conv_done, 1)

            def sample_sums(c):
                dve.wait_ge(sconv_made, c + 1)
                nc.vector.tensor_reduce(cT[:, c, SEQ:TOK].rearrange("p (b t) -> p b t", b=DEC_B), win[c % 2],
                                        AX.X, ALU.add).then_inc(sconv_summed, 1)

            for us, c, sums in (((0,), 0, (0,)), ((1, 2), 2, (1, 2)), ((3,), 3, (3,)), ((4, 5), 5, (4,)),
                                ((6,), 6, (5, 6)), ((7,), 7, (7,))):
                for u in us:
                    glu(u)
                conv(c)
                for u in sums:
                    sample_sums(u)
            dve.wait_ge(mean_done, 1)
            for k in range(KD):
                wait_conv(dve, k)
                nc.vector.tensor_tensor(cT[:, k, :].rearrange("p (h t) -> p h t", h=2),
                                        cT[:, k, :].rearrange("p (h t) -> p h t", h=2),
                                        psum[:, 2:4, 0:HALF], ALU.subtract).then_inc(centred, 1)
            dve.wait_ge(std_ready, 1)
            link(nc.vector.reciprocal(std, std))
            dve.wait_ge(centred, KD)
            for k in range(KD):
                nc.vector.tensor_tensor(cT[:, k, :], cT[:, k, :], std, ALU.mult).then_inc(scaled, 1)
            dve.wait_ge(outs_done, 16 * 7)
            norm(3, add_from_psum(3, pw2_done))
            experts(1)
            dve.wait_ge(row_in, 32)
            for i in range(TILES):
                r = ROWS[i]
                combine(1)(i)
                dve.wait_ge(root_ready, 4 * TILES + i + 1)
                link(nc.vector.reciprocal(stat[0:r, 2, i:i + 1], stat[0:r, 1, i:i + 1]))
                nc.vector.scalar_tensor_tensor(out=view(D * i, D, parts=r), in0=X[0:r, i, :],
                                               scalar=stat[0:r, 2, i:i + 1], in1=gfin[0:r, :],
                                               op0=ALU.mult, op1=ALU.mult).then_inc(y_ready, 1)

        @block.tensor
        def _(pe):
            mm, tr = nc.tensor.matmul, nc.tensor.transpose
            pe.wait_ge(consts_in, 16)

            def turn(call, i):
                r = ROWS[i]
                pe.wait_ge(xn_ready, TILES * call + i + 1)
                for h in range(2):
                    back = 1 if call % 2 else 2
                    if i >= back:
                        pe.wait_ge(hT_ready, 10 * call + 2 * (i - back) + h + 1)
                    for k in range(4):
                        t = tr(psum[:, turn_bank(call, i, h), P * k:P * k + r],
                               xn_of(call)[0:r, i, P * (4 * h + k):P * (4 * h + k) + P], ident[0:r, 0:r])
                    t.then_inc(turned, 1)

            for i in range(TILES):
                turn(0, i)
            pe.wait_ge(hT_ready, 10)
            hT = hT_of(0)
            for m in range(23):
                b = 2 * (m % 3)
                chunk = 0 if m < 6 else 1 if m < 12 else 2 if m < 17 else 3
                if m in (0, 6, 12, 17):
                    pe.wait_ge(proj_w[chunk], 16)
                if m >= 3:
                    p = m - 3
                    pe.wait_ge(proj_kept, min(p + 1, 19) if p < 21 else p - 1)
                    if p in (19, 20):
                        pe.wait_ge(u_made, 3 * (p - 18))
                w = ring[:, chunk, :].rearrange("p (k c) -> p k c", k=KD)
                if m == 16:
                    for k in range(KD):
                        for q in range(4):
                            t = mm(psum[32 * q:32 * q + 32, b, 0:192], hT[:, k, SEQ:TOK],
                                   w[:, k, 192 * q:192 * q + 192], start=k == 0, stop=k == KD - 1,
                                   tile_position=(0, 32 * q))
                elif 12 <= m < 16:
                    i = m - 12
                    for h in range(2):
                        for k in range(KD):
                            t = mm(psum[0:ROWS[i], b + h, 0:384], hT[:, k, P * i:P * i + ROWS[i]],
                                   w[:, k, 384 * h:384 * h + 384], start=k == 0, stop=k == KD - 1)
                else:
                    c = m % 6 if m < 12 else (4, 5, 2, 3, 0, 1)[m - 17]
                    for h in range(2):
                        for k in range(KD):
                            t = mm(psum[:, b + h, 0:HALF], w[:, k, P * c:P * c + P],
                                   hT[:, k, HALF * h:HALF * h + HALF], start=k == 0, stop=k == KD - 1)
                t.then_inc(proj_done, 1)

            pe.wait_ge(proj_kept, 21)
            pe.wait_ge(u_made, 6)
            pe.wait_ge(qbd_made, 24)
            for c in range(3):
                pe.wait_ge(kv_w[c], 16)
            for g in range(GROUPS):
                for bb in range(2):
                    for r in range(2):
                        for q in range(4):
                            b = 2 * q + bb
                            mm(psum[32 * q:32 * q + 32, 0, KOFF[g]:KOFF[g] + KEYS[g]], qbd[:, g, r, b, :],
                               kt_of(b)[:, r, KOFF[g]:KOFF[g] + KEYS[g]],
                               start=bb + r == 0, stop=bb + r == 2, tile_position=(0, 32 * q))
            for g in range(GROUPS):
                for bb in range(2):
                    for r in range(2):
                        for q in range(4):
                            t = mm(psum[32 * q:32 * q + 32, 1, 32 * g:32 * g + 32], qbd[:, g, r, 2 * q + bb, :],
                                   qkT[:, 6 + 2 * g + r, SEQ:TOK], start=bb + r == 0, stop=bb + r == 2,
                                   tile_position=(0, 32 * q))
            t.then_inc(ss_done, 1)
            pe.wait_ge(ss_norm, 1)
            ps = view(A_PS, 544)
            for t_, (rows_, _) in enumerate(VT):
                tr(psum[0:rows_, 2, P * t_:P * t_ + P], ps[:, P * t_:P * t_ + rows_], ident)
            for g in range(GROUPS):
                t = tr(psum[0:32, 3, P * g:P * g + P], ps[:, CACHED + 32 * g:CACHED + 32 * g + 32], ident)
            t.then_inc(ss_turned, 1)
            pe.wait_ge(ss_kept, 2)
            for bb in range(2):
                for s_, (rows_, g) in enumerate([(SAMPLES, g) for g in range(GROUPS)] + VT):
                    for q in range(4):
                        new = s_ < GROUPS
                        w = view((A_PTN if new else A_PTC) + P * (s_ if new else s_ - GROUPS) + 32 * q, 32, parts=rows_)
                        v = vS[0:SAMPLES, 4, 256 * g:256 * g + 256] if new else v_of(2 * q + bb)[0:rows_, s_ - GROUPS, :]
                        t = mm(psum[32 * q:32 * q + 32, 4 + bb, 0:256], w, v, start=s_ == 0,
                               stop=s_ == GROUPS + 3, tile_position=(0, 32 * q))
            t.then_inc(so_done, 1)
            pe.wait_ge(so_sum, 1)
            for c in range(4):
                t = tr(psum[:, 0, P * c:P * c + P], view(A_OS + P * c, P), ident)
            t.then_inc(so_turned, 1)

            def scores(n):
                i, h = n // 4, n % 4
                pe.wait_ge(qz_ready, n + 1)
                if n < 2:
                    pe.wait_ge(qz_zero, 2)
                if n == 0:
                    pe.wait_ge(masks_made, 6)
                    pe.wait_ge(so_kept, 8)
                if n:
                    pe.wait_ge(exp_done, n)
                at = 0
                for g in range(GROUPS):
                    lo = max(i - 1, 0) if g == 0 else 0
                    w = P * (i + 1 - lo)
                    mask_end = P + (2 * P if g == 0 else 2 * P + 4 * P * g)
                    done_ = 0
                    while done_ < w:
                        step = min(w - done_, 512 - at % 512)
                        out = psum[:, at // 512, at % 512:at % 512 + step]
                        mm(out, qz[h % 2][:, g, :], qkT[:, 6 + 2 * g + h // 2, P * lo + done_:P * lo + done_ + step],
                           start=True, stop=False)
                        o = mask_end - w + done_
                        t = mm(out, mb[:, 0:P], mb[:, o:o + step], start=False, stop=True)
                        at += step
                        done_ += step
                t.then_inc(s_done, 1)

            def weighted(n):
                h, hh = n % 4, n % 2
                pe.wait_ge(pt_kept, n + 1)
                if n >= 4:
                    pe.wait_ge(o_kept, n - 3)
                tiles = key_tiles(n)
                for t_, (g, j) in enumerate(tiles):
                    t = mm(psum[64 * hh:64 * hh + 64, 6 + (n // 2) % 2, 0:P],
                           vS[:, j, 256 * g + 64 * h:256 * g + 64 * h + 64], pT[n % 2][:, P * t_:P * t_ + P],
                           start=t_ == 0, stop=t_ == len(tiles) - 1)
                t.then_inc(o_done, 1)

            scores(0)
            for n in range(16):
                if n < 15:
                    scores(n + 1)
                pe.wait_ge(p_ready, n + 1)
                if n:
                    pe.wait_ge(pt_kept, n)
                w = len(key_tiles(n))
                sc = view(A_SC + 1280 * (n % 2), P * w)
                for t_ in range(w):
                    t = tr(psum[:, 3 + t_ // 4, P * (t_ % 4):P * (t_ % 4) + P], sc[:, P * t_:P * t_ + P], ident)
                t.then_inc(pt_done, 1)
                if n:
                    weighted(n - 1)
            weighted(15)

            def project(call, src, blocks, weights, done):
                for i in range(TILES):
                    r, b = ROWS[i], 2 * (i % 3)
                    if i >= 3:
                        pe.wait_ge(x_updated, TILES * (call - 1) + i - 2)
                    if i == TILES - 1:
                        for k in range(blocks):
                            for q in range(4):
                                t = mm(psum[32 * q:32 * q + 32, b, 0:256], src[:, k, SEQ:TOK],
                                       weights(k, q // 2)[:, 256 * (q % 2):256 * (q % 2) + 256],
                                       start=k == 0, stop=k == blocks - 1, tile_position=(0, 32 * q))
                    for h in range(2 if i < TILES - 1 else 0):
                        for k in range(blocks):
                            if call == 3 and i + h == 0:
                                pe.wait_ge(swish_done, k + 1)
                            t = mm(psum[0:r, b + h, :], src[:, k, P * i:P * i + r], weights(k, h),
                                   start=k == 0, stop=k == blocks - 1)
                    t.then_inc(done, 1)
                    if i:
                        turn(call, i - 1)
                turn(call, TILES - 1)
                pe.wait_ge(hT_ready, 10 * (call + 1))

            pe.wait_ge(wout_w, 16)
            pe.wait_ge(ya_made, 2)
            pe.wait_ge(so_kept, 8)
            pe.wait_ge(o_kept, 16)
            project(1, yT, 4, lambda k, h: ring[:, 3, D * k + 512 * h:D * k + 512 * h + 512], wo_done)

            def experts(n):
                hT = hT_of(2 * n + 1)
                for k in range(KD // 2):
                    for c in range(2):
                        for h in range(2):
                            o = V_RW + 64 * (KD * n + k + 4 * h)
                            t = mm(psum[64 * h:64 * h + 64, c, 0:HALF], sv[:, o:o + 64],
                                   hT[:, k + 4 * h, HALF * c:HALF * c + HALF], start=k == 0, stop=k == 3)
                t.then_inc(moe.routers, 1)
                pe.wait_ge(moe.routers_kept, n + 1)
                for i in range(TILES):
                    r = ROWS[i]
                    t = mm(psum[0:r, 4, 36 * i:36 * i + 36], view(M_R + P * i, r), cst[:, C_SEL:C_SEL + 36],
                           start=True, stop=True)
                t.then_inc(moe.logits, 1)
                pe.wait_ge(moe.picks, n + 1)
                mk = view(M_R + TOK + 180 + 40 + 4 * 160, 160)
                mm(psum[:, 5, 0:160], ones, mk, start=True, stop=True)
                mm(psum[:, 6, 0:160], cst[:, C_TRI:C_TRI + P], mk, start=True, stop=True).then_inc(moe.ranks, 1)
                for t_ in range(9):
                    r = min(P, ASSIGNED - P * t_)
                    pe.wait_ge(moe.staged[t_ % 6], 16 * ((2 if t_ % 6 < 3 else 1) * n + t_ // 6 + 1))
                    rows_ = stg[t_ % 6].rearrange("t (d k) -> t k d", k=KD)
                    for h in range(2):
                        q = 2 * t_ + h
                        if q >= 4:
                            pe.wait_ge(moe.xs_kept, 18 * n + q - 3)
                        for k in range(4):
                            t = tr(psum[:, q % 4, P * k:P * k + r], rows_[0:r, 4 * h + k, :], ident[0:r, 0:r])
                        t.then_inc(moe.st_turned, 1)
                pe.sem_inc(ex[n].down, 1)
                pe.wait_ge(moe.jobs, n + 1)

                def gate_up(it, u, first):
                    pe.wait_ge(moe.w_in[u], 16 * it + (128 * n + 16))
                    pe.wait_ge(moe.xj_ready, 4 * it + (EXPERTS * n + u + 1))
                    if not first or u >= 2:
                        pe.wait_ge(moe.act_ready, 4 * it + (EXPERTS * n + u - 1))
                    w = ring[:, u, 0:4096].rearrange("p (k f c) -> p k f c", k=KD, f=2)
                    for k in range(KD):
                        for f in range(2):
                            t = mm(psum[64 * f:64 * f + 64, u % 2, 0:2 * P], xj[u % 2][:, k, :], w[:, k, f, :],
                                   start=k == 0, stop=k == KD - 1)
                    t.then_inc(moe.gu_done, 1)

                def further(it, u):
                    chunks, before = (pe.value_load(jt[0:1, bass.ds(4 * it + (EXPERTS * w + u), 1)],
                                                    min_val=0, max_val=MORE) for w in (1, 2))
                    w = ring[:, u, 0:4096].rearrange("p (k f c) -> p k f c", k=KD, f=2)
                    with pe.If(chunks > 0):
                        with pe.Fori(0, chunks) as c:
                            pe.wait_ge(ex[n].kept, before + c + 1)
                            pe.wait_ge(ex[n].rows, before + c + 1)
                            for k in range(KD):
                                for f in range(2):
                                    t = mm(psum[64 * f:64 * f + 64, 6, 0:2 * P], xe[:, k, :], w[:, k, f, :],
                                           start=k == 0, stop=k == KD - 1)
                            t.then_inc(ex[n].gu, 1)
                            pe.wait_ge(ex[n].act, before + c + 1)
                            tr(psum[:, 7, 0:P], ave, ident).then_inc(ex[n].at, 1)
                            pe.wait_ge(ex[n].atk, before + c + 1)
                            for k in range(2):
                                for h in range(2):
                                    o = 4096 + D * k + 512 * h
                                    t = mm(psum[64 * h:64 * h + 64, 6, :], aTe[:, 64 * k:64 * k + 64],
                                           ring[:, u, o:o + 512], start=k == 0, stop=k == 1)
                            t.then_inc(ex[n].down, 1)

                def turn_act(it, u, first):
                    pe.wait_ge(moe.act_ready, 4 * it + (EXPERTS * n + u + 1))
                    if not first or u >= 2:
                        pe.wait_ge(moe.at_kept, 4 * it + (EXPERTS * n + u - 1))
                    tr(psum[:, 2 + u % 2, 0:P], av[u % 2], ident).then_inc(moe.at_done, 1)

                def down(it, u, first):
                    pe.wait_ge(moe.at_kept, 4 * it + (EXPERTS * n + u + 1))
                    if not first or u >= 2:
                        pe.wait_ge(moe.y_kept, 4 * it + (EXPERTS * n + u - 1))
                    for k in range(2):
                        for h in range(2):
                            o = 4096 + D * k + 512 * h
                            t = mm(psum[64 * h:64 * h + 64, 4 + u % 2, :], aT[u % 2][:, 64 * k:64 * k + 64],
                                   ring[:, u, o:o + 512], start=k == 0, stop=k == 1)
                    t.then_inc(moe.down_done, 1)

                def body(it, first):
                    for u in range(SLOTS + 1):
                        if u < SLOTS:
                            gate_up(it, u, first)
                        if u:
                            further(it, u - 1)
                            turn_act(it, u - 1, first)
                            down(it, u - 1, first)

                body(0, True)
                with pe.Fori(1, EXPERTS // SLOTS) as it:
                    body(it, False)

            experts(0)

            for i in range(TILES):
                turn(2, i)
            pe.wait_ge(hT_ready, 30)
            hT2 = hT_of(2)

            def conv(n):
                c = PE_CONV[n]
                pe.wait_ge(u_ready, c + 1)
                pe.wait_ge(diag_made, CK * (n + 1))
                for j in range(CK):
                    t = mm(psum[:, 6 + n, :], diag(n, j), cu[:, c, j:j + SEQ], start=j == 0, stop=j == CK - 1)
                t.then_inc(pe_conv_done, 1)

            for m in range(2 * KD):
                if m == 12:
                    conv(0)
                c, gate = m // 2, m % 2 == 0
                b = 2 * (m % 3)
                if m % 4 == 0:
                    pe.wait_ge(pw1_w[m // 4], 16)
                if m >= 3:
                    p = m - 3
                    if p % 2 == 0:
                        pe.wait_ge(sig_ready, p // 2 + 1)
                    else:
                        pe.wait_ge(u_ready, p // 2 + 1)
                w = ring[:, m // 4, 0:4096].rearrange("p (k c) -> p k c", k=KD)
                o = (256 if gate else 0) + P * (c % 2)
                for h in range(2):
                    for k in range(KD):
                        t = mm(psum[:, b + h, 0:HALF], w[:, k, o:o + P], hT2[:, k, HALF * h:HALF * h + HALF],
                               start=k == 0, stop=k == KD - 1)
                t.then_inc(z_done, 1)
            conv(1)
            mean = cst[:, C_MEAN:C_MEAN + P]
            pe.wait_ge(u_ready, KD)
            for k in range(KD):
                wait_conv(pe, k)
                for h in range(2):
                    t = mm(psum[:, 2 + h, 0:HALF], mean, cT[:, k, HALF * h:HALF * h + HALF], start=k == 0,
                           stop=k == KD - 1)
            t.then_inc(mean_done, 1)
            for k in range(KD):
                pe.wait_ge(squared, k + 1)
                for h in range(2):
                    t = mm(psum[:, 4 + h, 0:HALF], mean, hT2[:, k, HALF * h:HALF * h + HALF], start=k == 0,
                           stop=k == KD - 1)
            t.then_inc(var_done, 1)
            for c in range(2):
                pe.wait_ge(pw2_w[c], 16)
            project(3, cT, KD, lambda k, h: ring[:, h, 512 * k:512 * k + 512], pw2_done)
            experts(1)


def constants():
    c = np.zeros((P, C_END), np.float32)
    p = np.arange(P)
    c[:, C_ID:C_ID + P] = np.eye(P)
    c[:, C_TRI:C_TRI + P] = p[:, None] < p[None, :]
    c[:, C_ONE:C_ONE + P] = 1
    c[:, C_MEAN:C_MEAN + P] = 1.0 / D
    neg = np.float32(NEG)
    b, i = p // 16, p % 4
    cols = np.arange(CACHED)
    ok = np.zeros((P, CACHED + 96), bool)
    ok[:, 0:128] = cols[None, 0:128] >= i[:, None]
    ok[:, 128:384] = (cols[None, 0:256] % 4) == i[:, None]
    ok[:, 384:448] = (cols[None, 0:64] % 4) == i[:, None]
    new = np.arange(32)
    for g in range(3):
        mine = (new[None] // 4) == b[:, None]
        ok[:, CACHED + 32 * g:CACHED + 32 * g + 32] = mine & (
            (new[None] % 4 <= i[:, None]) if g == 0 else (new[None] % 4 == i[:, None]))
    c[:, C_SM:C_SM + 544] = np.where(ok, 0, neg)
    c[:, C_IOTA:C_IOTA + 32] = np.arange(32)
    c[:, C_IOTAP:C_IOTAP + 32] = np.arange(32) + 100
    c[:, C_E64:C_E64 + 32] = 64 * np.arange(32)
    c[:, C_THR:C_THR + 8] = 64 * np.arange(1, 9)
    c[:, C_VALID:C_VALID + 5] = 1
    c[SAMPLES:, C_VALID + 4] = 0
    c[:, C_GI:C_GI + 4] = np.arange(4)
    c[:, C_GIP:C_GIP + 4] = np.arange(4) + 100
    for h in range(2):
        c[64 * h:64 * h + 36, C_SEL:C_SEL + 36] = np.eye(36)
    return c


def prompt_masks():
    p = np.arange(P)
    q, k = p[:, None], p[None, :]
    ok = [k >= q, k <= q]
    for dil in (4, 16):
        same = q % dil == k % dil
        ok += [same, same & (k <= q)]
    return np.concatenate([np.where(o, 0, NEG) for o in ok], 1).astype(np.float32)


def blocks_of(w):
    k, n = w.shape[0] // P, w.shape[1]
    return w.reshape(k, P, n).transpose(1, 0, 2).reshape(P, k * n)


def kernel(**inputs):
    import concourse.bacc as bacc
    from concourse.bass_utils import run_bass_kernel_spmd

    a = {k: np.asarray(v) for k, v in inputs.items()}
    cat, con = np.concatenate, np.ascontiguousarray
    arrays = {}
    arrays["x_in"] = cat([a["x_prompt"].reshape(SEQ, D), a["x_sample"].reshape(SAMPLES, D)])
    w = a["w_in"][0]
    arrays["w_mix0"] = np.stack([blocks_of(con(w[:, c:c + 768])) for c in (768, 1536, 2304, 0)])
    kv = np.zeros((3, P, SLOT), np.float32)
    caches = [a["cache_kv_w128"][0], a["cache_kv_w512"][0],
              a["cache_kv_w2048"][0].reshape(DEC_B, 16, 16, 2, 4, HD)[:, :, 0:4].reshape(DEC_B, 64, 2, 4, HD)]
    for b in range(DEC_B):
        o = KV * (b % 3)
        for g, c in enumerate(caches):
            kt = c[b, :, 0].reshape(KEYS[g], 2, P).transpose(2, 1, 0)
            img = kv[b // 3, :, o:o + 2 * CACHED].reshape(P, 2, CACHED)
            img[:, :, KOFF[g]:KOFF[g] + KEYS[g]] = kt
            kv[b // 3, :, o:o + 2 * CACHED] = img.reshape(P, 2 * CACHED)
        o += 2 * CACHED
        v = [c[b, :, 1].reshape(KEYS[g], 256) for g, c in enumerate(caches)]
        for t, part in enumerate((v[0], v[1][0:P], v[1][P:], v[2])):
            kv[b // 3, 0:len(part), o + 256 * t:o + 256 * t + 256] = part
    arrays["kv_in"] = kv
    arrays["w_out"] = blocks_of(a["w_out"][0])
    w = a["w_pw1"][0]
    arrays["w_pw1"] = np.stack([blocks_of(cat([w[:, 256 * c:256 * c + 256], w[:, D + 256 * c:D + 256 * c + 256]], 1))
                                for c in range(4)])
    arrays["w_pw2"] = np.stack([blocks_of(con(a["w_pw2"][0][:, 512 * c:512 * c + 512])) for c in range(2)])
    moe = np.empty((2, EXPERTS, P, SLOT), np.float32)
    gu = moe[..., 0:4096].reshape(2, EXPERTS, P, KD, 2, 2, P)
    gu[:, :, :, :, :, 0] = a["w_gate"].reshape(2, EXPERTS, P, KD, 2, P)
    gu[:, :, :, :, :, 1] = a["w_up"].reshape(2, EXPERTS, P, KD, 2, P)
    moe[..., 0:4096] = gu.reshape(2, EXPERTS, P, 4096)
    moe[..., 4096:] = a["w_down"].reshape(2, EXPERTS, 2, P, D).transpose(0, 1, 3, 2, 4).reshape(2, EXPERTS, P, 2 * D)
    arrays["w_moe"] = moe

    def col(v):
        return v.reshape(-1, P).T

    def spread(v):
        return np.broadcast_to(v.reshape(1, -1), (P, v.size))

    router = [cat([a["w_router_group"][n], a["w_router_expert"][n], np.zeros((D, 28), np.float32)], 1)
              for n in range(2)]
    arrays["smalls"] = con(cat(
        [col(a["g_mix"][0]), col(a["g_ffn"][0]), col(a["g_mix"][1]), col(a["g_ffn"][1]),
         a["g_ffn"][0].reshape(P, KD), a["g_ffn"][1].reshape(P, KD), col(a["b_pw1"][0]), col(a["dw_b"][0]),
         col(a["ln_g"][0]), col(a["ln_b"][0]),
         a["conv_a_w"][0].reshape(3, 2, P).transpose(2, 1, 0).reshape(P, 6),
         a["dw_w"][0].reshape(CK, KD, P).transpose(2, 1, 0).reshape(P, KD * CK)]
        + [spread(cat([a["b_router_group"][n], a["b_router_expert"][n]])) for n in range(2)]
        + [blocks_of(r) for r in router], 1))
    arrays["consts"] = constants()
    arrays["masks"] = prompt_masks()
    arrays["rows"] = np.stack([a["b_pw2"][0], a["g_final"]])
    arrays["st_a"] = con(a["state_shortconv"][0].reshape(DEC_B, 2, 2, P).transpose(3, 2, 0, 1))
    arrays["st_c"] = con(a["state_conformer"][0].reshape(DEC_B, CK - 1, KD, P).transpose(3, 2, 0, 1))
    outs = {"y": (TOK, D), "k": (P, 6, TOK), "v": (TOK, 768), "ua_p": (P, 2, 2), "ua_s": (P, 2, DEC_B, 2),
            "uc_p": (P, KD, CK - 1), "uc_s": (P, KD, DEC_B, CK - 1)}

    nc = bacc.Bacc("TRN2", target_bir_lowering=False, num_devices=1)
    args = [nc.dram_tensor(n, v.shape, F32, kind="ExternalInput").ap() for n, v in arrays.items()]
    args += [nc.dram_tensor("out_" + n, s, F32, kind="ExternalOutput").ap() for n, s in outs.items()]
    program(nc, *args)
    r = run_bass_kernel_spmd(nc, [arrays], core_ids=[0]).results[0]
    y, k, v, ua_p, ua_s, uc_p, uc_s = (np.asarray(r["out_" + n]) for n in outs)

    kv = np.stack([k.transpose(2, 1, 0).reshape(TOK, 3, 4, HD), v.reshape(TOK, 3, 4, HD)], 1)
    prompt, new = kv[0:SEQ], kv[SEQ:].reshape(DEC_B, DEC_T, 2, 3, 4, HD)
    p_kv = [con(prompt[SEQ - n:, :, g])[None, None] for g, n in enumerate((128, SEQ, SEQ))]
    s_kv = [con(new[:, :, :, g])[None] for g in range(3)]
    return (y[0:SEQ].reshape(1, SEQ, D), y[SEQ:].reshape(DEC_B, DEC_T, D),
            con(ua_p.transpose(2, 1, 0)).reshape(1, 1, 2, 256), *p_kv,
            con(uc_p.transpose(2, 1, 0)).reshape(1, 1, CK - 1, D),
            con(ua_s.transpose(2, 3, 1, 0)).reshape(1, DEC_B, 2, 256), *s_kv,
            con(uc_s.transpose(2, 3, 1, 0)).reshape(1, DEC_B, CK - 1, D))
```

```python
from contextlib import ExitStack

import concourse.bass as bass
import numpy as np
from concourse import mybir

F32 = mybir.dt.float32
BF16 = mybir.dt.bfloat16
I32 = mybir.dt.int32
ALU = mybir.AluOpType
ACT = mybir.ActivationFunctionType
AX = mybir.AxisListType

P = 128
D = 1024
KD = D // P
SEQ = 512
DEC_B, DEC_T = 8, 4
SAMPLES = DEC_B * DEC_T
TOK = SEQ + SAMPLES
TILES = 5
HALF = TOK // 2
ROWS = [P, P, P, P, SAMPLES]
GROUPS = 3
HD = 64
SCALE = HD ** -0.5
NEG = -1e30
EXPERTS = 32
EGROUPS = 4
JOB = 64
ASSIGNED = 2 * TOK
MORE = (ASSIGNED - 1) // JOB
SLOT = 6144
SLOTS = 4
MSLOTS = SLOTS + 2
CK = 31
PE_CONV = (1, 4)
UP = SEQ + CK - 1
US = DEC_T + CK - 1
KEYS = [128, 256, 64]
KOFF = [0, 128, 384]
CACHED = 448
KV = 2 * CACHED + 4 * 256
C_ID, C_TRI, C_MEAN = 0, 128, 256
C_SM = 384
C_SMALL = C_SM + CACHED + 3 * SAMPLES
(C_IOTAP, C_E64, C_THR, C_VALID, C_SEL) = (
    C_SMALL, C_SMALL + 32, C_SMALL + 64, C_SMALL + 72, C_SMALL + 77)
C_ROW, C_JOB, C_TOKEN = C_SEL + 36, C_SEL + 100, C_SEL + 148
C_END = C_TOKEN + TILES
V_GAIN = 0
V_GPK = 32
V_BP1, V_DWB, V_LNG, V_LNB, V_CA, V_DW = 48, 64, 72, 80, 88, 94
V_RB = V_DW + KD * CK
V_RW = V_RB + 72
V_END = V_RW + 2 * KD * 64
A_HT = 0
A_QK = A_HT + KD * TOK
A_V = A_QK + 12 * TOK
A_GB = A_V + TILES * 768
A_U = A_GB + 2 * TOK
A_YT = A_U + 2 * 514 + 2 * 48
A_AIN = A_YT + 2 * TOK
A_XN0 = A_QK
A_SC = 0
A_PT = 2560
A_QZ = 3840
A_PTC = 0
A_PTN = A_PTC + 512
A_OS = A_PTN + 384
R_QBD = KV * 2
R_PS = R_QBD + 1536
R_PT, R_QZ = 4096, 4096 + 1280
B_U = KD * TOK
B_US = B_U + KD * UP
B_C = B_US + KD * DEC_B * US
B_SIG = B_C + KD * TOK
B_WIN = B_SIG + 2 * TOK
B_STD = B_WIN + SAMPLES * CK
B_ROW = B_STD + TOK
M_XN = 0
M_HT = TILES * D
M_W = 0
M_R = 2 * SLOT
M_ROW = M_R + 2560
M_JOB = M_ROW + 10 * JOB
M_G = 2 * SLOT
M_XT = M_G + 3 * D
M_SG = M_XT + D
M_ACT = M_SG + P
M_AT = M_ACT + 2 * P
M_Y = M_AT + P
M_EX = M_Y + 3 * 512
M_EXT = M_EX + D
M_GF = 2 * SLOT - D
ARENA = max(B_ROW + D, A_YT + 4 * TOK, M_EXT + 512)


def program(nc, x_in, w_mix0, kv_in, w_out, w_pw1, w_pw2, w_moe, smalls, consts, masks, rows, st_a, st_c,
            y_out, k_out, v_out, ua_p_out, ua_s_out, uc_p_out, uc_s_out):
    ctx = ExitStack()
    with ctx:
        def sb(name, shape, dt=F32):
            return ctx.enter_context(nc.sbuf_tensor(name, shape, dt))

        def sem(name):
            return ctx.enter_context(nc.semaphore(name))

        xn_dram = nc.dram_tensor("normed_rows", (TOK, D), F32, kind="Internal").ap()
        ys_dram = nc.dram_tensor("expert_outputs", ((EXPERTS + MORE) * JOB, D), F32, kind="Internal").ap()
        ring = sb("ring", [P, SLOTS, SLOT])
        X = sb("X", [P, TILES, D])
        cst = sb("cst", [P, C_END])
        sv = sb("sv", [P, V_END])
        ar = sb("ar", [P, ARENA])
        stat = sb("stat", [P, 3, 8])
        vec = sb("vec", [P, 64])
        mb = sb("mb", [P, P + 1280], BF16)
        eps = sb("eps", [P, 2])
        cw = sb("cw", [P, TILES, 2])
        ix = sb("ix", [P, TILES, 2], I32)
        tb = sb("tb", [P, 2 * MORE], I32)
        ixg = sb("ixg", [P, 3], I32)
        ixe = sb("ixe", [P, 1], I32)
        jt = sb("jt", [1, 2 * EXPERTS], I32)
        psum = ctx.enter_context(nc.psum_tensor("psum", [P, 8, 512], F32))

        def view(off, n, pat=None, parts=P, **dims):
            a = ar[0:parts, off:off + n]
            return a.rearrange(pat, **dims) if pat else a

        ident = cst[:, C_ID:C_ID + P]
        mean_of = cst[:, C_MEAN:C_MEAN + P]

        def bcast(ap, shape):
            return ap.to_broadcast(shape)

        x_in_done = [sem(f"x_in_done_{i}") for i in range(TILES)]
        consts_in = sem("consts_in")
        masks_in = sem("masks_in")
        masks_made = sem("masks_made")
        smalls_in = sem("smalls_in")
        dense_w = [sem(f"dense_w{c}") for c in range(4)]
        later_w = [sem(f"later_w{c}") for c in range(3)]
        wout_w = sem("wout_w")
        state_a_in = sem("state_a_in")
        state_c_in = sem("state_c_in")
        row_in = sem("row_in")
        zeros_made = sem("zeros_made")
        zeros_out = sem("zeros_out")
        outs_done = sem("outs_done")
        dve_link = sem("dve_link")
        act_link = sem("act_link")
        pool_link = sem("pool_link")
        stats_set = sem("stats_set")
        root_ready = sem("root_ready")
        inv_ready = sem("inv_ready")
        xn_ready = sem("xn_ready")
        turned = sem("turned")
        hT_ready = sem("hT_ready")
        proj_done = sem("proj_done")
        proj_kept = sem("proj_kept")
        u_made = sem("u_made")
        ya_made = sem("ya_made")
        qbd_made = sem("qbd_made")
        ss_done = sem("ss_done")
        ss_max = sem("ss_max")
        ss_exp = sem("ss_exp")
        ss_norm = sem("ss_norm")
        ss_turned = sem("ss_turned")
        ss_kept = sem("ss_kept")
        so_done = sem("so_done")
        so_sum = sem("so_sum")
        so_turned = sem("so_turned")
        so_kept = sem("so_kept")
        qz_zero = sem("qz_zero")
        qz_ready = sem("qz_ready")
        s_done = sem("s_done")
        max_ready = sem("max_ready")
        exp_done = sem("exp_done")
        p_ready = sem("p_ready")
        pt_done = sem("pt_done")
        pt_kept = sem("pt_kept")
        o_done = sem("o_done")
        o_kept = sem("o_kept")
        wo_done = sem("wo_done")
        x_updated = sem("x_updated")
        z_done = sem("z_done")
        sig_ready = sem("sig_ready")
        u_ready = sem("u_ready")
        conv_done = sem("conv_done")
        diag_made = sem("diag_made")
        pe_conv_done = sem("pe_conv_done")
        pe_conv_kept = sem("pe_conv_kept")
        sconv_made = sem("sconv_made")
        sconv_summed = sem("sconv_summed")
        sconv_kept = sem("sconv_kept")
        mean_done = sem("mean_done")
        centred = sem("centred")
        squared = sem("squared")
        var_done = sem("var_done")
        std_ready = sem("std_ready")
        scaled = sem("scaled")
        swish_done = sem("swish_done")
        pw2_done = sem("pw2_done")
        spread_kept = sem("spread_kept")
        y_ready = sem("y_ready")

        class Moe:
            def __init__(self):
                self.logits = sem("logits")
                self.gshift = sem("gshift")
                self.gexp = sem("gexp")
                self.eshift = sem("eshift")
                self.eexp = sem("eexp")
                self.picks = sem("picks")
                self.ranks = sem("ranks")
                self.routers = sem("routers")
                self.routers_kept = sem("routers_kept")
                self.places = sem("places")
                self.table = sem("table")
                self.tokens = sem("tokens")
                self.jobs = sem("jobs")
                self.xn_out = sem("xn_out")
                self.ix_ready = sem("ix_ready")
                self.seen = sem("seen")
                self.rows_in = [sem(f"rows_in_{v}") for v in range(3)]
                self.rows_turned = sem("rows_turned")
                self.rows_kept = sem("rows_kept")
                self.w_in = [sem(f"w_in_{u}") for u in range(MSLOTS)]
                self.gu_done = sem("gu_done")
                self.sg_ready = sem("sg_ready")
                self.act_ready = sem("act_ready")
                self.at_done = sem("at_done")
                self.at_kept = sem("at_kept")
                self.down_done = sem("down_done")
                self.y_kept = sem("y_kept")
                self.y_out = [sem(f"y_out_{b}") for b in range(3)]
                self.gathered = [sem(f"gathered_{q}") for q in range(2 * TILES)]
                self.all_out = sem("all_out")
                self.combined = sem("combined")

        class Further:
            def __init__(self, n):
                self.ix = sem(f"ex_ix{n}")
                self.rows = sem(f"ex_rows{n}")
                self.turned = sem(f"ex_turned{n}")
                self.turns_kept = sem(f"ex_turns_kept{n}")
                self.gu = sem(f"ex_gu{n}")
                self.sg = sem(f"ex_sg{n}")
                self.act = sem(f"ex_act{n}")
                self.at = sem(f"ex_at{n}")
                self.atk = sem(f"ex_atk{n}")
                self.down = sem(f"ex_down{n}")
                self.kept = sem(f"ex_kept{n}")
                self.out = sem(f"ex_out{n}")

        moe, ex = Moe(), [Further(0), Further(1)]
        block = ctx.enter_context(nc.Block())

        qkT = view(A_QK, 12 * TOK, "p (m t) -> p m t", m=12)
        vS = view(A_V, TILES * 768, "p (i c) -> p i c", i=TILES)
        gB = view(A_GB, 2 * TOK, "p (m t) -> p m t", m=2)
        aIn = view(A_AIN, 2 * TOK, "p (m t) -> p m t", m=2)
        uP = view(A_U, 2 * 514, "p (m t) -> p m t", m=2)
        uS = view(A_U + 2 * 514, 96, "p (m b t) -> p m b t", m=2, b=DEC_B)
        yT = view(A_YT, 4 * TOK, "p (m t) -> p m t", m=4)
        qz = [view(A_QZ, 384, "p (g t) -> p g t", g=3),
              ring[:, 3, R_QZ:R_QZ + 384].rearrange("p (g t) -> p g t", g=3)]
        pT = [view(A_PT, 1280), ring[:, 3, R_PT:R_PT + 1280]]
        qbd = ring[:, 2, R_QBD:R_QBD + 1536].rearrange("p (g r b c) -> p g r b c", g=3, r=2, b=DEC_B)
        ps = ring[:, 2, R_PS:R_PS + 544]
        cu = view(B_U, KD * UP, "p (k t) -> p k t", k=KD)
        cs = view(B_US, KD * DEC_B * US, "p (k b t) -> p k b t", k=KD, b=DEC_B)
        cT = view(B_C, KD * TOK, "p (k t) -> p k t", k=KD)
        sigm = view(B_SIG, 2 * TOK, "p (h t) -> p h t", h=2)
        std = view(B_STD, TOK)
        brow = view(B_ROW, D)
        win = [view(o, SAMPLES * CK, "p (b i j) -> p b i j", b=DEC_B, i=DEC_T) for o in (B_WIN, B_ROW)]
        gfin = view(M_GF, D)
        xg = [view(M_G + D * v, D) for v in range(3)]
        xt = view(M_XT, D, "p (k t) -> p k t", k=KD)
        sg = view(M_SG, P)
        av = [view(M_ACT + P * b, P) for b in range(2)]
        aT = view(M_AT, P)
        yj = [view(M_Y + 512 * b, 512) for b in range(3)]
        yg = [ring[:, q // 2, 4096 + D * (q % 2):4096 + D * (q % 2) + D] for q in range(8)] + [xg[0], xg[1]]
        xe = view(M_EX, D, parts=JOB)
        xeT = view(M_EXT, 512, "p (k t) -> p k t", k=KD)
        ye = cst[:, C_SM:C_SM + 512]
        sge, ave, aTe = (view(M_EXT + P * b, P) for b in range(3))

        def slot(u):
            return ring[:, u, :] if u < SLOTS else view(M_W + SLOT * (u - SLOTS), SLOT)

        def loads_before(n, u):
            return n * len(range(u, EXPERTS, MSLOTS))

        def over_experts(eng, body):
            body(0, True, MSLOTS)
            with eng.Fori(1, EXPERTS // MSLOTS) as it:
                body(it, False, MSLOTS)
            body(EXPERTS // MSLOTS, False, EXPERTS % MSLOTS)

        def hT_of(call):
            return view(M_HT if call % 2 else A_HT, KD * TOK, "p (k t) -> p k t", k=KD)

        def xn_of(call):
            o = (A_XN0, M_XN, A_XN0, M_XN, M_HT)[call]
            return view(o, TILES * D, "p (i c) -> p i c", i=TILES)

        def wait_residual(eng, call, s, i):
            if call == 0:
                eng.wait_ge(x_in_done[i], 16)
            else:
                eng.wait_ge(x_updated, TILES * (call - 1) + s + 1)

        def tiles_of(call):
            return list(enumerate((4, 0, 1, 2, 3) if call % 2 else range(TILES)))

        def turn_bank(call, s, h):
            return 6 + h if call % 2 else (2 * s + h) % 4

        def diag(n, j):
            q = CK * n + j
            return ring[:, q // 16, 4096 + P * (q % 16):4096 + P * (q % 16) + P]

        def wait_conv(eng, k):
            eng.wait_ge(sconv_kept, k + 1)
            if k in PE_CONV:
                eng.wait_ge(pe_conv_kept, PE_CONV.index(k) + 1)
            else:
                eng.wait_ge(conv_done, k + 1 - sum(c < k for c in PE_CONV))

        def kt_of(b):
            return ring[:, b // 3, KV * (b % 3):KV * (b % 3) + 2 * CACHED].rearrange("p (r t) -> p r t", r=2)

        def v_of(b):
            o = KV * (b % 3) + 2 * CACHED
            return ring[:, b // 3, o:o + 1024].rearrange("p (t c) -> p t c", t=4)

        VT = [(P, 0), (P, 1), (P, 1), (64, 2)]

        def scores_of(n):
            return psum[:, 0:3, :].rearrange("p b c -> p (b c)")[:, 0:P * len(key_tiles(n))]

        def key_tiles(n):
            i = n // 4
            return [(0, j) for j in range(max(i - 1, 0), i + 1)] + [(g, j) for g in (1, 2) for j in range(i + 1)]

        @block.sync
        def _(sp):
            sp.dma_start(cst[:, :], consts).then_inc(consts_in, 16)
            sp.dma_start(sv[:, :], smalls).then_inc(smalls_in, 16)
            for i in range(3):
                sp.wait_ge(x_in_done[i], 16)
            sp.dma_start(ring[:, 0, :], w_mix0[0]).then_inc(dense_w[0], 16)
            sp.dma_start(view(A_YT, 6 * P), masks).then_inc(masks_in, 16)
            sp.dma_start(ring[:, 1, :], w_mix0[1]).then_inc(dense_w[1], 16)
            sp.dma_start(ring[:, 2, :], w_mix0[2]).then_inc(dense_w[2], 16)
            sp.wait_ge(zeros_out, 16 * 8)
            sp.dma_start(ring[:, 3, :], w_mix0[3]).then_inc(dense_w[3], 16)
            for c, m in enumerate((6, 12, 17)):
                n = KV * (3 if c < 2 else 2)
                sp.wait_ge(proj_done, m)
                sp.dma_start(ring[:, c, 0:n], kv_in[c, :, 0:n]).then_inc(later_w[c], 16)
            sp.wait_ge(proj_done, 23)
            sp.dma_start(ring[:, 3, 0:4096], w_out).then_inc(wout_w, 16)

            def experts(n):
                for u in (2, 0, 1, 3) if n == 0 else (2, 3, 0, 1):
                    if n == 0:
                        if u < 3:
                            sp.wait_ge(so_done, 1)
                        else:
                            sp.wait_ge(wo_done, TILES)
                    elif u >= 2:
                        sp.wait_ge(z_done, 2 * KD)
                        sp.wait_ge(pe_conv_done, len(PE_CONV))
                    else:
                        sp.wait_ge(pw2_done, TILES)
                    sp.dma_start(ring[:, u, :], w_moe[n, u]).then_inc(moe.w_in[u], 16)
                sp.wait_ge(moe.xn_out, 16 * TILES * (n + 1))
                sp.wait_ge(moe.routers, n + 1)
                for u in range(SLOTS, MSLOTS):
                    sp.dma_start(slot(u), w_moe[n, u]).then_inc(moe.w_in[u], 16)

                def weights(it, jobs):
                    for u in range(jobs):
                        sp.wait_ge(moe.down_done, MSLOTS * it + (EXPERTS * n + u + 1 - MSLOTS))
                        sp.sem_inc(moe.seen, 1)
                        b = (u - 2) % MSLOTS
                        sp.wait_ge(moe.w_in[b], 16 * it + 16 * (loads_before(n, b) + (u >= 2)))
                        sp.dma_start(slot(u), w_moe[n, bass.ds(MSLOTS * it + u, 1), :, :].rearrange(
                            "a p c -> (a p) c")).then_inc(moe.w_in[u], 16)

                with sp.Fori(1, EXPERTS // MSLOTS) as it:
                    weights(it, MSLOTS)
                weights(EXPERTS // MSLOTS, EXPERTS % MSLOTS)

            experts(0)
            sp.wait_ge(moe.all_out, 1)
            for c in range(4):
                if c == 0:
                    sp.wait_ge(moe.gathered[2 * TILES - 1], 16)
                sp.dma_start(ring[:, c, 0:4096], w_pw1[c]).then_inc(dense_w[c], 16)
            for c in range(2):
                sp.wait_ge(z_done, 4 * (c + 1))
                sp.dma_start(ring[:, c, 0:4096], w_pw2[c]).then_inc(later_w[c], 16)
            experts(1)
            for i in range(TILES):
                sp.wait_ge(y_ready, i + 1)
                sp.dma_start(y_out[P * i:P * i + ROWS[i], :], view(D * i, D, parts=ROWS[i])).then_inc(outs_done, 16)
            sp.wait_ge(outs_done, 16 * (TILES + 7))

        @block.gpsimd
        def _(pool):
            nc.gpsimd.memset(ring[:, 3, 0:D], 0.0).then_inc(zeros_made, 1)
            pool.wait_ge(zeros_made, 1)
            pool.wait_ge(dense_w[1], 16)
            for t in range(8):
                o = EXPERTS * JOB + P * t
                pool.dma_start(ys_dram[o:o + P, :], ring[:, 3, 0:D]).then_inc(zeros_out, 16)
            nc.gpsimd.memset(uP[:, :, 0:2], 0.0).then_inc(pool_link, 1)
            pool.dma_start(uS[:, :, :, 0:2], st_a).then_inc(state_a_in, 16)
            pool.wait_ge(proj_kept, 6)
            pool.wait_ge(proj_done, 17)
            nc.gpsimd.memset(ring[:, 2, R_QBD:R_QBD + 1536], 0.0).then_inc(pool_link, 1)
            pool.wait_ge(pool_link, 2)
            made = 0
            for g in range(GROUPS):
                for r in range(2):
                    for hh in range(2):
                        for bb in range(2):
                            src = qkT[64 * hh:64 * hh + 64, 2 * g + r, SEQ:TOK].rearrange(
                                "p (q b i) -> p q b i", q=4, b=2)[:, :, bb, :]
                            c = 16 * bb + 4 * (2 * r + hh)
                            dst = qbd[64 * hh:64 * hh + 64, g, r, :, :].rearrange(
                                "p (q b) c -> p q b c", b=2)[:, :, bb, c:c + 4]
                            nc.gpsimd.tensor_copy(dst, src).then_inc(qbd_made, 1)
                            made += 1
                            pool.wait_ge(qbd_made, made)
            pool.wait_ge(proj_done, 23)
            for h in range(2):
                nc.gpsimd.memset(qz[h][64 * (1 - h):64 * (1 - h) + 64, :, :], 0.0).then_inc(qz_zero, 1)
                pool.wait_ge(qz_zero, h + 1)
            for n in range(16):
                i, h = n // 4, n % 4
                hh = h % 2
                if n >= 2:
                    pool.wait_ge(s_done, n - 1)
                if n:
                    pool.wait_ge(qz_ready, n)
                nc.gpsimd.tensor_copy(
                    qz[hh][64 * hh:64 * hh + 64, :, :],
                    qkT[64 * hh:64 * hh + 64, h // 2:6:2, P * i:P * i + P]).then_inc(qz_ready, 1)

            def experts(n):
                pool.wait_ge(moe.tokens, n + 1)
                pool.wait_ge(moe.jobs, n + 1)
                pool.wait_ge(moe.xn_out, 16 * TILES * (n + 1))

                def rows_of(pair, v, first=False):
                    if not first:
                        pool.wait_ge(moe.rows_turned, pair + (16 * n - 2))
                    nc.gpsimd.tensor_copy(ixg[:, v:v + 1], tb[:, bass.ds(pair, 1)]).then_inc(moe.ix_ready, 1)
                    pool.wait_ge(moe.ix_ready, pair + (16 * n + 1))
                    pool.sem_inc(moe.seen, 1)
                    pool.indirect_dma_start(xg[v], None, xn_dram, bass.IndirectOffsetOnAxis(ixg[:, v:v + 1], 0)
                                            ).then_inc(moe.rows_in[v], 16)

                def further_rows(it, u):
                    def count(what):
                        return pool.value_load(jt[0:1, bass.ds(MSLOTS * it + (EXPERTS * what + u), 1)],
                                                min_val=0, max_val=MORE)

                    chunks = count(0)
                    with pool.If(chunks > 0):
                        before = count(1)
                        with pool.Fori(0, chunks) as c:
                            pool.wait_ge(ex[n].turned, before + c + 1)
                            o = nc.s_assert_within(before + c + MORE, MORE, 2 * MORE - 1,
                                                   skip_runtime_bounds_check_because="at most MORE chunks")
                            nc.gpsimd.tensor_copy(ixe[0:JOB, 0:1], tb[0:JOB, bass.ds(o, 1)]).then_inc(ex[n].ix, 1)
                            pool.wait_ge(ex[n].ix, before + c + 1)
                            pool.sem_inc(moe.seen, 1)
                            pool.indirect_dma_start(xe, None, xn_dram, bass.IndirectOffsetOnAxis(ixe[0:JOB, 0:1], 0)
                                                    ).then_inc(ex[n].rows, 16)

                def body(it, gathers):
                    for v in range(MSLOTS // 2):
                        if v < gathers:
                            rows_of(3 * it + (v + 3), v)
                        further_rows(it, 2 * v + 2)
                        further_rows(it, 2 * v + 3)

                for v in range(3):
                    rows_of(v, v, True)
                further_rows(0, 0)
                further_rows(0, 1)
                with pool.Fori(0, 4) as it:
                    body(it, 3)
                body(4, 1)
                pool.wait_ge(moe.all_out, n + 1)
                for q in range(2 * TILES):
                    i, k = q // 2, q % 2
                    pool.indirect_dma_start(
                        yg[q][0:ROWS[i], :], None, ys_dram,
                        bass.IndirectOffsetOnAxis(ix[0:ROWS[i], i, k:k + 1], 0)).then_inc(moe.gathered[q], 16)

            experts(0)
            pool.wait_ge(hT_ready, 30)
            nc.gpsimd.memset(cu[:, :, 0:CK - 1], 0.0).then_inc(pool_link, 1)
            pool.dma_start(cs[:, :, :, 0:CK - 1], st_c).then_inc(state_c_in, 16)
            for c in range(KD):
                pool.wait_ge(u_ready, c + 1)
                if c >= 2:
                    pool.wait_ge(sconv_summed, c - 1)
                rows_ = cs[:, c, :, :]
                windows = bass.AP(rows_.tensor, rows_.offset, [rows_.ap[0], [US, DEC_B], [1, DEC_T], [1, CK]])
                taps = sv[:, V_DW + CK * c:V_DW + CK * c + CK]
                nc.gpsimd.tensor_tensor(win[c % 2], windows, bcast(taps[:, None, None, :], [P, DEC_B, DEC_T, CK]), ALU.mult
                                        ).then_inc(sconv_made, 1)
            experts(1)

        @block.scalar
        def _(act):
            for i in range(TILES):
                act.dma_start(X[0:ROWS[i], i, :], x_in[P * i:P * i + ROWS[i], :]).then_inc(x_in_done[i], 16)
            links = [0]

            def link(ins):
                links[0] += 1
                ins.then_inc(act_link, 1)
                act.wait_ge(act_link, links[0])

            def norm(call):
                act.wait_ge(stats_set, 1)
                xn = xn_of(call)
                for s, i in tiles_of(call):
                    r = ROWS[i]
                    if call % 2 and s == 0:
                        act.wait_ge(pw2_done if call == 3 else wo_done, 1)
                        for q in range(4):
                            t = nc.scalar.activation(xn[0:r, i, 256 * q:256 * q + 256],
                                                     psum[32 * q:32 * q + 32, 0, 0:256], ACT.Copy)
                            if q < 3:
                                link(t)
                        t.then_inc(spread_kept, 1)
                    wait_residual(act, call, s, i)
                    link(nc.scalar.activation(xn[0:r, i, :], X[0:r, i, :], ACT.Square,
                                              accum_out=stat[0:r, 0, i:i + 1]))
                    nc.scalar.activation(stat[0:r, 1, i:i + 1], stat[0:r, 0, i:i + 1], ACT.Sqrt, scale=1.0 / D,
                                         bias=eps[0:r, 0:1]).then_inc(root_ready, 1)
                    if call < 4:
                        act.wait_ge(inv_ready, TILES * call + s + 1)
                        nc.scalar.activation(xn[0:r, i, :], X[0:r, i, :], ACT.Copy,
                                             scale=stat[0:r, 2, i:i + 1]).then_inc(xn_ready, 1)
                    if call % 2:
                        act.wait_ge(xn_ready, TILES * call + s + 1)
                        act.dma_start(xn_dram[P * i:P * i + r, :], xn[0:r, i, :]).then_inc(moe.xn_out, 16)

            norm(0)
            for m in range(23):
                b = 2 * (m % 3)
                if m == 20:
                    act.wait_ge(ss_max, 1)
                    nc.scalar.activation(ps, ps, ACT.Exp, bias=vec[:, 0:1], accum_out=vec[:, 1:2]).then_inc(ss_exp, 1)
                if 19 <= m <= 20:
                    continue
                act.wait_ge(proj_done, m + 1)
                if m == 16:
                    for q in range(4):
                        t = nc.scalar.activation(vS[0:SAMPLES, 4, 192 * q:192 * q + 192],
                                                 psum[32 * q:32 * q + 32, b, 0:192], ACT.Copy)
                        if q < 3:
                            link(t)
                    t.then_inc(proj_kept, 1)
                    continue
                if 12 <= m < 16:
                    r = ROWS[m - 12]
                    nc.scalar.activation(vS[0:r, m - 12, :].rearrange("p (h c) -> p h c", h=2),
                                         psum[0:r, b:b + 2, 0:384], ACT.Copy).then_inc(proj_kept, 1)
                    continue
                dst = qkT[:, m, :] if m < 12 else (aIn[:, m - 17, :] if m < 19 else gB[:, m - 21, :])
                nc.scalar.activation(dst.rearrange("p (h t) -> p h t", h=2), psum[:, b:b + 2, 0:HALF],
                                     ACT.Copy, scale=SCALE if m < 6 else 1.0).then_inc(proj_kept, 1)
                if m == 11:
                    act.wait_ge(proj_kept, 12)
                    act.dma_start(k_out, qkT[:, 6:12, :]).then_inc(outs_done, 16)
                if m == 17:
                    act.wait_ge(proj_kept, 17)
                    act.dma_start(v_out[0:SEQ, :].rearrange("(i p) c -> p i c", p=P), vS[:, 0:4, :]
                                  ).then_inc(outs_done, 16)
                    act.dma_start(v_out[SEQ:TOK, :], vS[0:SAMPLES, 4, :]).then_inc(outs_done, 16)
            act.wait_ge(u_made, 6)
            act.dma_start(ua_p_out, uP[:, :, SEQ:SEQ + 2]).then_inc(outs_done, 16)
            act.dma_start(ua_s_out, uS[:, :, :, 4:6]).then_inc(outs_done, 16)

            act.wait_ge(ss_turned, 1)
            nc.scalar.activation(view(A_PTC, 512), psum[:, 2, :], ACT.Copy).then_inc(ss_kept, 1)
            nc.scalar.activation(view(A_PTN, 384, parts=32), psum[0:32, 3, 0:384], ACT.Copy).then_inc(ss_kept, 1)

            act.wait_ge(so_done, 1)
            nc.scalar.activation(view(A_OS, 512, "p (b c) -> p b c", b=2), psum[:, 4:6, 0:256], ACT.Copy
                                 ).then_inc(so_sum, 1)

            def exps(n):
                sc = view(A_SC + 1280 * (n % 2), P * len(key_tiles(n)))
                if n == 0:
                    act.wait_ge(so_kept, 8)
                if n >= 2:
                    act.wait_ge(pt_done, n - 1)
                act.wait_ge(max_ready, n + 1)
                nc.scalar.activation(sc, scores_of(n), ACT.Exp, bias=vec[:, 4 + n % 2:5 + n % 2],
                                     accum_out=vec[:, 6 + n % 2:7 + n % 2]).then_inc(exp_done, 1)

            def keep_o(n):
                i, h = n // 4, n % 4
                hh = h % 2
                act.wait_ge(o_done, n + 1)
                nc.scalar.activation(yT[64 * hh:64 * hh + 64, 2 + h // 2, P * i:P * i + P],
                                     psum[64 * hh:64 * hh + 64, 6 + (n // 2) % 2, 0:P], ACT.Copy
                                     ).then_inc(o_kept, 1)

            exps(0)
            for n in range(16):
                w = P * len(key_tiles(n))
                if n < 15:
                    exps(n + 1)
                act.wait_ge(pt_done, n + 1)
                if n >= 2:
                    act.wait_ge(o_done, n - 1)
                nc.scalar.activation(pT[n % 2][:, 0:w], psum[:, 3:6, :].rearrange("p b c -> p (b c)")[:, 0:w],
                                     ACT.Copy).then_inc(pt_kept, 1)
                if n:
                    keep_o(n - 1)
            keep_o(15)

            def experts(n):
                act.wait_ge(moe.routers, n + 1)
                nc.scalar.activation(view(M_R, TOK).rearrange("p (h t) -> p h t", h=2), psum[:, 0:2, 0:HALF],
                                     ACT.Copy).then_inc(moe.routers_kept, 1)
                act.wait_ge(moe.gshift, n + 1)
                g4 = view(M_R + 724, 20)
                nc.scalar.activation(g4, g4, ACT.Exp).then_inc(moe.gexp, 1)
                act.wait_ge(moe.eshift, n + 1)
                nc.scalar.activation(vec[:, 30:35], vec[:, 25:30], ACT.Exp).then_inc(moe.eexp, 1)
                act.sem_inc(ex[n].kept, 1)
                act.sem_inc(ex[n].out, 1)
                act.wait_ge(moe.jobs, n + 1)

                def silu(it, u, first):
                    act.wait_ge(moe.gu_done, MSLOTS * it + (EXPERTS * n + u + 1))
                    if not first or u:
                        act.wait_ge(moe.act_ready, MSLOTS * it + (EXPERTS * n + u))
                    nc.scalar.activation(sg, psum[:, u % 2, 0:P], ACT.Silu).then_inc(moe.sg_ready, 1)

                def store(job, y, done):
                    rows = ys_dram.rearrange("(j r) c -> j r c", r=JOB)[bass.ds(job, 1), :, :].rearrange(
                        "a r c -> (a r) c")
                    for q in range(2):
                        act.dma_start(rows[:, 512 * q:512 * q + 512], y[64 * q:64 * q + 64, :]).then_inc(done, 16)

                def keep_y(it, u, first):
                    b = u % 3
                    act.wait_ge(moe.down_done, MSLOTS * it + (EXPERTS * n + u + 1))
                    if not first or u >= 3:
                        act.wait_ge(moe.y_out[b], 64 * it + 32 * (n * len(range(b, EXPERTS, 3)) + u // 3))
                    nc.scalar.activation(yj[b], psum[:, 4 + u % 2, :], ACT.Copy).then_inc(moe.y_kept, 1)
                    act.wait_ge(moe.y_kept, MSLOTS * it + (EXPERTS * n + u + 1))
                    store(MSLOTS * it + u, yj[b], moe.y_out[b])

                def further(it, u):
                    def count(what):
                        return act.value_load(jt[0:1, bass.ds(MSLOTS * it + (EXPERTS * what + u), 1)],
                                                min_val=0, max_val=MORE)

                    chunks = count(0)
                    with act.If(chunks > 0):
                        before = count(1)
                        with act.Fori(0, chunks) as c:
                            act.wait_ge(ex[n].gu, before + c + 1)
                            nc.scalar.activation(sge, psum[:, 6, 0:P], ACT.Silu).then_inc(ex[n].sg, 1)
                            act.wait_ge(ex[n].out, 32 * (before + c) + 1)
                            act.sem_inc(moe.seen, 1)
                            act.wait_ge(ex[n].down, before + c + 1)
                            nc.scalar.activation(ye, psum[:, 6, :], ACT.Copy).then_inc(ex[n].kept, 1)
                            act.wait_ge(ex[n].kept, before + c + 2)
                            job = nc.s_assert_within(before + c + EXPERTS, EXPERTS, EXPERTS + MORE - 1,
                                                     skip_runtime_bounds_check_because="at most MORE chunks")
                            store(job, ye, ex[n].out)

                def body(it, first, jobs):
                    for u in range(jobs + 1):
                        if u < jobs:
                            silu(it, u, first)
                        if u:
                            further(it, u - 1)
                            keep_y(it, u - 1, first)

                over_experts(act, body)
                if n == 1:
                    act.dma_start(gfin, rows[1:2, :].to_broadcast([P, D])).then_inc(row_in, 16)
                for b in range(3):
                    act.wait_ge(moe.y_out[b], 32 * (n + 1) * len(range(b, EXPERTS, 3)))
                further_chunks, before_last = (act.value_load(jt[0:1, o:o + 1], min_val=0, max_val=MORE)
                                               for o in (EXPERTS - 1, 2 * EXPERTS - 1))
                act.wait_ge(ex[n].out, 32 * (before_last + further_chunks) + 1)
                act.sem_inc(moe.all_out, 1)

            act.wait_ge(outs_done, 16 * 5)
            norm(1)
            experts(0)

            norm(2)
            act.dma_start(brow, rows[0:1, :].to_broadcast([P, D])).then_inc(row_in, 16)
            def keep_sconv(c):
                act.wait_ge(sconv_summed, c + 1)
                out = cT[:, c, SEQ:TOK]
                nc.scalar.activation(out, out, ACT.Identity, bias=sv[:, V_DWB + c:V_DWB + c + 1]
                                     ).then_inc(sconv_kept, 1)

            def keep_pe_conv(n):
                c = PE_CONV[n]
                act.wait_ge(pe_conv_done, n + 1)
                nc.scalar.activation(cT[:, c, 0:SEQ], psum[:, 6 + n, :], ACT.Identity,
                                     bias=sv[:, V_DWB + c:V_DWB + c + 1]).then_inc(pe_conv_kept, 1)

            for c in range(KD):
                if c == 6:
                    keep_pe_conv(0)
                b = 2 * ((2 * c) % 3)
                act.wait_ge(z_done, 2 * c + 1)
                if c >= 2:
                    act.wait_ge(u_ready, c - 1)
                nc.scalar.activation(sigm[:, c % 2, :].rearrange("p (h t) -> p h t", h=2), psum[:, b:b + 2, 0:HALF],
                                     ACT.Sigmoid, bias=sv[:, V_BP1 + 8 + c:V_BP1 + 9 + c]).then_inc(sig_ready, 1)
                if c < 2:
                    for j in range(CK):
                        o = V_DW + CK * PE_CONV[c] + j
                        nc.scalar.activation(diag(c, j), ident, ACT.Copy, scale=sv[:, o:o + 1]).then_inc(diag_made, 1)
                else:
                    keep_sconv(c - 2)
            keep_sconv(6)
            keep_pe_conv(1)
            keep_sconv(7)
            act.wait_ge(u_ready, KD)
            act.wait_ge(state_c_in, 16)
            act.dma_start(uc_p_out, cu[:, :, SEQ:UP]).then_inc(outs_done, 16)
            act.dma_start(uc_s_out, cs[:, :, :, DEC_T:US]).then_inc(outs_done, 16)
            sq = hT_of(2)
            for k in range(KD):
                act.wait_ge(centred, k + 1)
                nc.scalar.activation(sq[:, k, :], cT[:, k, :], ACT.Square).then_inc(squared, 1)
            act.wait_ge(var_done, 1)
            nc.scalar.activation(std.rearrange("p (h t) -> p h t", h=2), psum[:, 4:6, 0:HALF], ACT.Sqrt,
                                 bias=eps[:, 1:2]).then_inc(std_ready, 1)
            for k in range(KD):
                act.wait_ge(scaled, k + 1)
                nc.scalar.activation(cT[:, k, :], cT[:, k, :], ACT.Silu, scale=sv[:, V_LNG + k:V_LNG + k + 1],
                                     bias=sv[:, V_LNB + k:V_LNB + k + 1]).then_inc(swish_done, 1)
            act.wait_ge(outs_done, 16 * 7)
            norm(3)
            experts(1)
            norm(4)

        @block.vector
        def _(dve):
            links = [0]

            def link(ins):
                links[0] += 1
                ins.then_inc(dve_link, 1)
                dve.wait_ge(dve_link, links[0])

            nc.vector.memset(eps[:, 0:1], 1e-6).then_inc(dve_link, 1)
            nc.vector.memset(eps[:, 1:2], 1e-5).then_inc(dve_link, 1)
            links[0] = 2
            dve.wait_ge(dve_link, 2)
            nc.vector.memset(stat[:, :, :], 1.0).then_inc(stats_set, 1)
            dve.wait_ge(consts_in, 16)
            dve.wait_ge(smalls_in, 16)

            def norm(call, update):
                hT = hT_of(call)
                ahead = call == 2
                order = [i for _, i in tiles_of(call)]
                if ahead:
                    update(0)
                for s in range(TILES + 1):
                    if s < TILES:
                        i = order[s]
                        r = ROWS[i]
                        if not ahead:
                            update(i)
                        elif s + 1 < TILES:
                            update(order[s + 1])
                        dve.wait_ge(root_ready, TILES * call + s + 1)
                        nc.vector.reciprocal(stat[0:r, 2, i:i + 1], stat[0:r, 1, i:i + 1]).then_inc(inv_ready, 1)
                    if s:
                        t = order[s - 1]
                        r = ROWS[t]
                        for h in range(2):
                            dve.wait_ge(turned, 10 * call + 2 * (s - 1) + h + 1)
                            g = sv[:, V_GAIN + 8 * call + 4 * h:V_GAIN + 8 * call + 4 * h + 4]
                            nc.vector.tensor_tensor(
                                hT[:, 4 * h:4 * h + 4, P * t:P * t + r],
                                psum[:, turn_bank(call, s - 1, h), :].rearrange("p (k t) -> p k t", k=4)[:, :, 0:r],
                                bcast(g[:, :, None], [P, 4, r]), ALU.mult).then_inc(hT_ready, 1)

            norm(0, lambda i: None)
            dve.wait_ge(masks_in, 16)
            nc.vector.tensor_copy(mb[:, 0:P], ident).then_inc(masks_made, 1)
            nc.vector.tensor_copy(mb[:, P:3 * P], view(A_YT, 2 * P)).then_inc(masks_made, 1)
            for g in (1, 2):
                src = view(A_YT + 2 * P * g, 2 * P)
                o = 3 * P + 4 * P * (g - 1)
                nc.vector.tensor_copy(mb[:, o:o + 3 * P].rearrange("p (j k) -> p j k", j=3),
                                      bcast(src[:, 0:P][:, None, :], [P, 3, P])).then_inc(masks_made, 1)
                nc.vector.tensor_copy(mb[:, o + 3 * P:o + 4 * P], src[:, P:2 * P]).then_inc(masks_made, 1)
            dve.wait_ge(masks_made, 6)
            for c in range(2):
                b = 2 * ((19 + c) % 3)
                dve.wait_ge(proj_done, 20 + c)
                dve.wait_ge(proj_kept, 18 + c)
                if c == 0:
                    dve.wait_ge(state_a_in, 16)
                    dve.wait_ge(pool_link, 1)
                nc.vector.tensor_tensor(uP[:, c, 2:2 + HALF], psum[:, b, 0:HALF], aIn[:, c, 0:HALF],
                                        ALU.mult).then_inc(u_made, 1)
                nc.vector.tensor_tensor(uP[:, c, 2 + HALF:2 + SEQ], psum[:, b + 1, 0:SEQ - HALF],
                                        aIn[:, c, HALF:SEQ], ALU.mult).then_inc(u_made, 1)
                nc.vector.tensor_tensor(
                    uS[:, c, :, 2:6], psum[:, b + 1, SEQ - HALF:HALF].rearrange("p (b t) -> p b t", b=DEC_B),
                    aIn[:, c, SEQ:TOK].rearrange("p (b t) -> p b t", b=DEC_B), ALU.mult).then_inc(u_made, 1)
            dve.wait_ge(ss_done, 1)
            link(nc.vector.tensor_tensor(ps[:, 0:CACHED], psum[:, 6, 0:CACHED], cst[:, C_SM:C_SM + CACHED], ALU.add))
            link(nc.vector.tensor_tensor(ps[:, CACHED:544], psum[:, 7, 0:96], cst[:, C_SM + CACHED:C_SM + 544],
                                         ALU.add))
            nc.vector.tensor_reduce(vec[:, 0:1], ps, AX.X, ALU.max, negate=True).then_inc(ss_max, 1)
            dve.wait_ge(ss_exp, 1)
            link(nc.vector.reciprocal(vec[:, 2:3], vec[:, 1:2]))
            nc.vector.tensor_scalar(ps, ps, vec[:, 2:3], None, ALU.mult).then_inc(ss_norm, 1)
            dve.wait_ge(u_made, 6)
            dve.wait_ge(proj_kept, 21)
            for c in range(2):
                yp = yT[:, c, 0:SEQ]
                ys = yT[:, c, SEQ:TOK].rearrange("p (b t) -> p b t", b=DEC_B)
                for j in range(3):
                    w = sv[:, V_CA + 3 * c + j:V_CA + 3 * c + j + 1]
                    for dst, src in ((yp, uP[:, c, j:j + SEQ]), (ys, uS[:, c, :, j:j + 4])):
                        if j == 0:
                            link(nc.vector.tensor_scalar(dst, src, w, None, ALU.mult))
                        else:
                            link(nc.vector.scalar_tensor_tensor(out=dst, in0=src, scalar=w, in1=dst,
                                                                op0=ALU.mult, op1=ALU.add))
                nc.vector.tensor_tensor(yT[:, c, :], yT[:, c, :], gB[:, c, :], ALU.mult).then_inc(ya_made, 1)

            dve.wait_ge(so_turned, 1)
            for r in range(2):
                for hh in range(2):
                    for bb in range(2):
                        c = P * (2 * bb + r)
                        src = psum[64 * hh:64 * hh + 64, 0, c:c + P].rearrange("p (q c) -> p q c", q=4)
                        o = 16 * bb + 4 * (2 * r + hh)
                        dst = yT[64 * hh:64 * hh + 64, 2 + r, SEQ:TOK].rearrange(
                            "p (q b t) -> p q b t", q=4, b=2)[:, :, bb, :]
                        nc.vector.tensor_copy(dst, src[:, :, o:o + 4]).then_inc(so_kept, 1)

            def maxima(n):
                dve.wait_ge(s_done, n + 1)
                nc.vector.tensor_reduce(vec[:, 4 + n % 2:5 + n % 2], scores_of(n), AX.X, ALU.max, negate=True
                                        ).then_inc(max_ready, 1)

            def normalise(n):
                sc = view(A_SC + 1280 * (n % 2), P * len(key_tiles(n)))
                dve.wait_ge(exp_done, n + 1)
                link(nc.vector.reciprocal(vec[:, 8 + n % 2:9 + n % 2], vec[:, 6 + n % 2:7 + n % 2]))
                nc.vector.tensor_scalar(sc, sc, vec[:, 8 + n % 2:9 + n % 2], None, ALU.mult).then_inc(p_ready, 1)

            maxima(0)
            for n in range(16):
                normalise(n)
                if n < 15:
                    maxima(n + 1)

            def add_from_psum(call, done):
                def update(i):
                    s = (i + 1) % TILES
                    r, b = ROWS[i], 2 * (s % 3)
                    if s == 0:
                        dve.wait_ge(spread_kept, call // 2 + 1)
                        nc.vector.tensor_tensor(X[0:r, i, :], X[0:r, i, :], xn_of(call)[0:r, i, :], ALU.add
                                                ).then_inc(x_updated, 1)
                        return
                    dve.wait_ge(done, s + 1)
                    nc.vector.tensor_tensor(X[0:r, i, :], X[0:r, i, :],
                                            psum[0:r, b:b + 2, :].rearrange("p b c -> p (b c)"), ALU.add
                                            ).then_inc(x_updated, 1)
                return update

            def combine(n):
                def update(i):
                    r = ROWS[i]
                    for k in range(2):
                        q = 2 * i + k
                        dve.wait_ge(moe.gathered[q], 16 * (n + 1))
                        if k:
                            dve.wait_ge(moe.combined, TILES * n + i + 1)
                        nc.vector.scalar_tensor_tensor(out=X[0:r, i, :], in0=yg[q][0:r, :],
                                                       scalar=cw[0:r, i, k:k + 1], in1=X[0:r, i, :],
                                                       op0=ALU.mult, op1=ALU.add
                                                       ).then_inc(x_updated if k else moe.combined, 1)
                return update

            def experts(n):
                o = [M_R]

                def new(k, pat=None, **dims):
                    o[0] += k
                    return view(o[0] - k, k, pat, **dims)

                def const(c, k):
                    return cst[:, c:c + k]

                S5 = [P, TILES, EXPERTS]
                new(TOK)
                L = new(180, "p (i e) -> p i e", i=TILES)
                g4 = new(20, "p (i e) -> p i e", i=TILES)
                t4 = new(20, "p (i e) -> p i e", i=TILES)
                em = new(160, "p (i e) -> p i e", i=TILES)
                tt = new(160, "p (i e) -> p i e", i=TILES)
                o1 = new(160, "p (i e) -> p i e", i=TILES)
                o2 = new(160, "p (i e) -> p i e", i=TILES)
                mk = new(160, "p (i e) -> p i e", i=TILES)
                rank = new(160, "p (i e) -> p i e", i=TILES)
                base = new(192, "p (i e) -> p i e", i=6)
                bigger = new(256, "p (e m) -> p e m", m=8)
                one = new(32)
                extra = new(32)
                inc = new(32)
                xb = new(32)
                d64 = new(32)
                gmax, gsum, gval, gidx = vec[:, 0:5], vec[:, 5:10], vec[:, 10:15], vec[:, 15:20]
                m1, m2, eidx = vec[:, 20:25], vec[:, 25:30], vec[:, 35:40]
                place = vec[:, 40:50].rearrange("p (i k) -> p i k", i=TILES)
                row, job = vec[:, 50:60], stat.rearrange("p a b -> p (a b)")[:, 8:18]

                def tt_(out, a, b, op):
                    link(nc.vector.tensor_tensor(out, a, b, op))

                def ts_(out, a, s1, s2, op0, op1=ALU.bypass):
                    link(nc.vector.tensor_scalar(out, a, s1, s2, op0, op1))

                def red(out, a, op):
                    link(nc.vector.tensor_reduce(out, a, AX.X, op))

                def first_of(onehot, values, top, scratch, idx, iota, iotap, shape):
                    tt_(scratch, values, bcast(top[:, :, None], shape), ALU.is_ge)
                    link(nc.vector.scalar_tensor_tensor(
                        out=scratch, in0=scratch, scalar=-100.0, in1=bcast(iotap[:, None, :], shape),
                        op0=ALU.mult, op1=ALU.add))
                    red(idx, scratch, ALU.min)
                    tt_(onehot, bcast(iota[:, None, :], shape), bcast(idx[:, :, None], shape), ALU.is_equal)

                link(nc.vector.memset(L, 0.0))
                link(nc.vector.memset(base, 0.0))
                link(nc.vector.memset(one, 1.0))
                dve.wait_ge(moe.logits, n + 1)
                rb = sv[:, V_RB + 36 * n:V_RB + 36 * n + 36]
                tt_(L[:, 0:4, :], psum[:, 4, 0:144].rearrange("p (i e) -> p i e", i=4),
                    bcast(rb[:, None, :], [P, 4, 36]), ALU.add)
                tt_(L[0:SAMPLES, 4, :], psum[0:SAMPLES, 4, 144:180], rb[0:SAMPLES, :], ALU.add)
                gl = L[:, :, 0:EGROUPS]
                red(gmax, gl, ALU.max)
                nc.vector.tensor_tensor(g4, gl, bcast(gmax[:, :, None], [P, TILES, 4]), ALU.subtract
                                        ).then_inc(moe.gshift, 1)
                first_of(t4, gl, gmax, t4, gidx, const(C_ROW, 4), const(C_IOTAP, 4), [P, TILES, 4])
                ts_(t4, t4, -1.0, 1e30, ALU.add, ALU.mult)
                for i in range(TILES):
                    tt_(em[:, i, :].rearrange("p (g e) -> p g e", g=4),
                        L[:, i, 4:36].rearrange("p (g e) -> p g e", g=4),
                        bcast(t4[:, i, :][:, :, None], [P, 4, 8]), ALU.add)
                red(m1, em, ALU.max)
                first_of(o1, em, m1, tt, eidx, const(C_ROW, 32), const(C_IOTAP, 32), S5)
                link(nc.vector.scalar_tensor_tensor(out=em, in0=o1, scalar=-3e30, in1=em, op0=ALU.mult, op1=ALU.add))
                red(m2, em, ALU.max)
                first_of(o2, em, m2, tt, eidx, const(C_ROW, 32), const(C_IOTAP, 32), S5)
                tt_(mk, o1, o2, ALU.add)
                nc.vector.tensor_tensor(mk, mk, bcast(const(C_VALID, 5)[:, :, None], S5), ALU.mult
                                        ).then_inc(moe.picks, 1)
                nc.vector.tensor_tensor(m2, m2, m1, ALU.subtract).then_inc(moe.eshift, 1)
                dve.wait_ge(moe.gexp, n + 1)
                red(gsum, g4, ALU.add)
                dve.wait_ge(moe.eexp, n + 1)
                te = vec[:, 30:35]
                ts_(gval, te, 1.0, None, ALU.add)
                tt_(gval, gval, gsum, ALU.mult)
                link(nc.vector.reciprocal(cw[:, :, 0], gval))
                tt_(cw[:, :, 1], cw[:, :, 0], te, ALU.mult)
                dve.wait_ge(moe.ranks, n + 1)
                for i in range(TILES):
                    link(nc.vector.scalar_tensor_tensor(out=base[:, i + 1, :], in0=psum[:, 5, 32 * i:32 * i + 32],
                                                        scalar=float(D), in1=base[:, i, :],
                                                        op0=ALU.mult, op1=ALU.add))
                tt_(rank, psum[:, 6, 0:160].rearrange("p (i e) -> p i e", i=TILES), base[:, 0:TILES, :], ALU.add)
                cnt = base[:, TILES, :]

                def before(out, counts, incl):
                    link(nc.vector.tensor_tensor_scan(incl, counts, one, 0.0, ALU.add, ALU.bypass))
                    tt_(out, incl, counts, ALU.subtract)

                tt_(bigger, bcast(cnt[:, :, None], [P, EXPERTS, 8]),
                    bcast(const(C_THR, 8)[:, None, :], [P, EXPERTS, 8]), ALU.is_gt)
                red(extra, bigger, ALU.add)
                before(xb, extra, inc)
                ts_(d64, xb, 64.0, 64.0 * 31, ALU.mult, ALU.add)
                tt_(d64, d64, const(C_E64, 32), ALU.subtract)
                ts_(tt, rank, 64.0, None, ALU.is_ge)
                tt_(tt, tt, bcast(d64[:, None, :], S5), ALU.mult)
                tt_(tt, tt, bcast(const(C_E64, 32)[:, None, :], S5), ALU.add)
                tt_(tt, tt, rank, ALU.add)
                for k, oh in enumerate((o1, o2)):
                    tt_(em, oh, tt, ALU.mult)
                    red(place[:, :, k], em, ALU.add)
                flat = vec[:, 40:50]
                rowi = tb[:, 0:2 * TILES]
                R = view(M_ROW, 10 * JOB, "p (i r) -> p i r", i=10)
                C = view(M_JOB, 480, "p (i j) -> p i j", i=10)
                link(nc.vector.tensor_copy(ix[:, :, :], place))
                link(nc.vector.tensor_scalar(rowi, ix[:, :, :].rearrange("p i k -> p (i k)"), JOB - 1, None,
                                             ALU.bitwise_and))
                link(nc.vector.tensor_copy(row, rowi))
                tt_(job, flat, row, ALU.subtract)
                tt_(R, bcast(const(C_ROW, JOB)[:, None, :], [P, 10, JOB]), bcast(row[:, :, None], [P, 10, JOB]),
                    ALU.is_equal)
                tt_(C, bcast(const(C_JOB, 48)[:, None, :], [P, 10, 48]), bcast(job[:, :, None], [P, 10, 48]),
                    ALU.is_equal)
                byt = view(M_JOB, 480, "p (i j) -> p i j", i=TILES)
                nc.vector.tensor_tensor(byt, byt, bcast(const(C_TOKEN, TILES)[:, :, None], [P, TILES, 96]), ALU.mult
                                        ).then_inc(moe.places, 1)
                link(nc.vector.tensor_copy(jt[0:1, 0:EXPERTS], extra[0:1, :]))
                nc.vector.tensor_copy(jt[0:1, EXPERTS:2 * EXPERTS], xb[0:1, :]).then_inc(moe.jobs, 1)
                dve.wait_ge(moe.table, n + 1)
                link(nc.vector.tensor_copy(tb[:, 0:MORE], psum[:, 7, 0:MORE]))
                nc.vector.tensor_copy(tb[0:JOB, MORE:2 * MORE], psum[0:JOB, 7, MORE:2 * MORE]).then_inc(moe.tokens, 1)

                def keep_rows(pair, first=False):
                    dve.wait_ge(moe.rows_turned, pair + (16 * n + 1))
                    if not first:
                        dve.wait_ge(moe.gu_done, 2 * pair + EXPERTS * n)
                    for h in range(2):
                        g = sv[:, V_GPK + 8 * n + 4 * h:V_GPK + 8 * n + 4 * h + 4]
                        nc.vector.tensor_tensor(
                            xt[:, 4 * h:4 * h + 4, :],
                            psum[:, 3 + 4 * h, :].rearrange("p (k t) -> p k t", k=4),
                            bcast(g[:, :, None], [P, 4, P]), ALU.mult).then_inc(moe.rows_kept, 1)

                keep_rows(0, True)

                def gate_up(it, u, first):
                    dve.wait_ge(moe.sg_ready, MSLOTS * it + (EXPERTS * n + u + 1))
                    if not first or u >= 2:
                        dve.wait_ge(moe.at_done, MSLOTS * it + (EXPERTS * n + u - 1))
                    nc.vector.tensor_tensor(av[u % 2], sg, psum[:, u % 2, P:2 * P], ALU.mult
                                            ).then_inc(moe.act_ready, 1)

                def keep_at(it, u, first):
                    dve.wait_ge(moe.at_done, MSLOTS * it + (EXPERTS * n + u + 1))
                    if not first or u:
                        dve.wait_ge(moe.down_done, MSLOTS * it + (EXPERTS * n + u))
                    nc.vector.tensor_copy(aT, psum[:, 2, 0:P]).then_inc(moe.at_kept, 1)

                def further(it, u):
                    def count(what):
                        return dve.value_load(jt[0:1, bass.ds(MSLOTS * it + (EXPERTS * what + u), 1)],
                                                min_val=0, max_val=MORE)

                    chunks = count(0)
                    with dve.If(chunks > 0):
                        before = count(1)
                        with dve.Fori(0, chunks) as c:
                            dve.wait_ge(ex[n].turned, before + c + 2)
                            nc.vector.tensor_tensor(
                                xeT, psum[:, 7, :].rearrange("p (k t) -> p k t", k=KD),
                                bcast(sv[:, V_GPK + 8 * n:V_GPK + 8 * n + 8][:, :, None], [P, KD, JOB]), ALU.mult
                                ).then_inc(ex[n].turns_kept, 1)
                            dve.wait_ge(ex[n].sg, before + c + 1)
                            nc.vector.tensor_tensor(ave, sge, psum[:, 6, P:2 * P], ALU.mult).then_inc(ex[n].act, 1)
                            dve.wait_ge(ex[n].at, before + c + 1)
                            nc.vector.tensor_copy(aTe, psum[:, 7, 0:P]).then_inc(ex[n].atk, 1)

                def body(it, first, jobs):
                    for u in range(jobs + 1):
                        if u < jobs:
                            gate_up(it, u, first)
                        if u % 2 and jobs == MSLOTS:
                            keep_rows(3 * it + (u // 2 + 1))
                        if u:
                            keep_at(it, u - 1, first)
                            further(it, u - 1)

                over_experts(dve, body)

            dve.wait_ge(outs_done, 16 * 5)
            norm(1, add_from_psum(1, wo_done))
            experts(0)

            norm(2, combine(0))
            dve.wait_ge(xn_ready, 3 * TILES)
            dve.wait_ge(row_in, 16)
            for i in range(TILES):
                r = ROWS[i]
                link(nc.vector.tensor_tensor(X[0:r, i, :], X[0:r, i, :], brow[0:r, :], ALU.add))

            def glu(c):
                b = 2 * ((2 * c + 1) % 3)
                ba = sv[:, V_BP1 + c:V_BP1 + c + 1]
                dve.wait_ge(z_done, 2 * c + 2)
                dve.wait_ge(sig_ready, c + 1)
                if c == 0:
                    dve.wait_ge(pool_link, 3)
                    dve.wait_ge(state_c_in, 16)
                s = sigm[:, c % 2, :]
                link(nc.vector.scalar_tensor_tensor(out=cu[:, c, CK - 1:CK - 1 + HALF], in0=psum[:, b, 0:HALF],
                                                    scalar=ba, in1=s[:, 0:HALF], op0=ALU.add, op1=ALU.mult))
                link(nc.vector.scalar_tensor_tensor(out=cu[:, c, CK - 1 + HALF:UP], in0=psum[:, b + 1, 0:SEQ - HALF],
                                                    scalar=ba, in1=s[:, HALF:SEQ], op0=ALU.add, op1=ALU.mult))
                nc.vector.scalar_tensor_tensor(
                    out=cs[:, c, :, CK - 1:US], in1=s[:, SEQ:TOK].rearrange("p (b t) -> p b t", b=DEC_B),
                    in0=psum[:, b + 1, SEQ - HALF:HALF].rearrange("p (b t) -> p b t", b=DEC_B),
                    scalar=ba, op0=ALU.add, op1=ALU.mult).then_inc(u_ready, 1)

            def conv(c):
                dve.wait_ge(u_ready, c + 1)
                out = cT[:, c, 0:SEQ]
                for j in range(CK):
                    w = sv[:, V_DW + CK * c + j:V_DW + CK * c + j + 1]
                    src = cu[:, c, j:j + SEQ]
                    if j == 0:
                        t = nc.vector.tensor_scalar(out, src, w, sv[:, V_DWB + c:V_DWB + c + 1], ALU.mult, ALU.add)
                    else:
                        t = nc.vector.scalar_tensor_tensor(out=out, in0=src, scalar=w, in1=out,
                                                           op0=ALU.mult, op1=ALU.add)
                    if j < CK - 1:
                        link(t)
                t.then_inc(conv_done, 1)

            def sample_sums(c):
                dve.wait_ge(sconv_made, c + 1)
                nc.vector.tensor_reduce(cT[:, c, SEQ:TOK].rearrange("p (b t) -> p b t", b=DEC_B), win[c % 2],
                                        AX.X, ALU.add).then_inc(sconv_summed, 1)

            for us, c, sums in (((0,), 0, (0,)), ((1, 2), 2, (1, 2)), ((3,), 3, (3,)), ((4, 5), 5, (4,)),
                                ((6,), 6, (5, 6)), ((7,), 7, (7,))):
                for u in us:
                    glu(u)
                conv(c)
                for u in sums:
                    sample_sums(u)
            dve.wait_ge(mean_done, 1)
            for k in range(KD):
                wait_conv(dve, k)
                nc.vector.tensor_tensor(cT[:, k, :].rearrange("p (h t) -> p h t", h=2),
                                        cT[:, k, :].rearrange("p (h t) -> p h t", h=2),
                                        psum[:, 2:4, 0:HALF], ALU.subtract).then_inc(centred, 1)
            dve.wait_ge(std_ready, 1)
            link(nc.vector.reciprocal(std, std))
            dve.wait_ge(centred, KD)
            for k in range(KD):
                nc.vector.tensor_tensor(cT[:, k, :], cT[:, k, :], std, ALU.mult).then_inc(scaled, 1)
            dve.wait_ge(outs_done, 16 * 7)
            norm(3, add_from_psum(3, pw2_done))
            experts(1)
            dve.wait_ge(row_in, 32)
            update = combine(1)
            update(0)
            for i in range(TILES):
                r = ROWS[i]
                if i + 1 < TILES:
                    update(i + 1)
                dve.wait_ge(root_ready, 4 * TILES + i + 1)
                link(nc.vector.reciprocal(stat[0:r, 2, i:i + 1], stat[0:r, 1, i:i + 1]))
                nc.vector.scalar_tensor_tensor(out=view(D * i, D, parts=r), in0=X[0:r, i, :],
                                               scalar=stat[0:r, 2, i:i + 1], in1=gfin[0:r, :],
                                               op0=ALU.mult, op1=ALU.mult).then_inc(y_ready, 1)

        @block.tensor
        def _(pe):
            mm, tr = nc.tensor.matmul, nc.tensor.transpose
            pe.wait_ge(consts_in, 16)

            def turn(call, s):
                i = tiles_of(call)[s][1]
                r = ROWS[i]
                pe.wait_ge(xn_ready, TILES * call + s + 1)
                for h in range(2):
                    back = 1 if call % 2 else 2
                    if s >= back:
                        pe.wait_ge(hT_ready, 10 * call + 2 * (s - back) + h + 1)
                    for k in range(4):
                        t = tr(psum[:, turn_bank(call, s, h), P * k:P * k + r],
                               xn_of(call)[0:r, i, P * (4 * h + k):P * (4 * h + k) + P], ident[0:r, 0:r])
                    t.then_inc(turned, 1)

            def stay_warm(times, bank=0):
                for _ in range(times):
                    mm(psum[:, bank, 0:C_SM], ident, cst[:, 0:C_SM], start=True, stop=True)

            for i in range(TILES):
                turn(0, i)
                stay_warm(1, 6)
            pe.wait_ge(hT_ready, 10)
            hT = hT_of(0)
            def sample_scores():
                pe.wait_ge(proj_kept, 17)
                pe.wait_ge(qbd_made, 24)
                for c in range(3):
                    pe.wait_ge(later_w[c], 16)
                for g in range(GROUPS):
                    for bb in range(2):
                        for r in range(2):
                            for q in range(4):
                                b = 2 * q + bb
                                mm(psum[32 * q:32 * q + 32, 6, KOFF[g]:KOFF[g] + KEYS[g]], qbd[:, g, r, b, :],
                                   kt_of(b)[:, r, KOFF[g]:KOFF[g] + KEYS[g]],
                                   start=bb + r == 0, stop=bb + r == 2, tile_position=(0, 32 * q))
                for g in range(GROUPS):
                    for bb in range(2):
                        for r in range(2):
                            for q in range(4):
                                t = mm(psum[32 * q:32 * q + 32, 7, 32 * g:32 * g + 32], qbd[:, g, r, 2 * q + bb, :],
                                       qkT[:, 6 + 2 * g + r, SEQ:TOK], start=bb + r == 0, stop=bb + r == 2,
                                       tile_position=(0, 32 * q))
                t.then_inc(ss_done, 1)

            for m in range(23):
                b = 2 * (m % 3)
                if m == 21:
                    sample_scores()
                chunk = 0 if m < 6 else 1 if m < 12 else 2 if m < 17 else 3
                if m in (0, 6, 12, 17):
                    pe.wait_ge(dense_w[chunk], 16)
                if m >= 3:
                    p = m - 3
                    pe.wait_ge(proj_kept, min(p + 1, 19) if p < 21 else p - 1)
                    if p in (19, 20):
                        pe.wait_ge(u_made, 3 * (p - 18))
                w = ring[:, chunk, :].rearrange("p (k c) -> p k c", k=KD)
                if m == 16:
                    for k in range(KD):
                        for q in range(4):
                            t = mm(psum[32 * q:32 * q + 32, b, 0:192], hT[:, k, SEQ:TOK],
                                   w[:, k, 192 * q:192 * q + 192], start=k == 0, stop=k == KD - 1,
                                   tile_position=(0, 32 * q))
                elif 12 <= m < 16:
                    i = m - 12
                    for h in range(2):
                        for k in range(KD):
                            t = mm(psum[0:ROWS[i], b + h, 0:384], hT[:, k, P * i:P * i + ROWS[i]],
                                   w[:, k, 384 * h:384 * h + 384], start=k == 0, stop=k == KD - 1)
                else:
                    c = m % 6 if m < 12 else (4, 5, 2, 3, 0, 1)[m - 17]
                    for h in range(2):
                        for k in range(KD):
                            t = mm(psum[:, b + h, 0:HALF], w[:, k, P * c:P * c + P],
                                   hT[:, k, HALF * h:HALF * h + HALF], start=k == 0, stop=k == KD - 1)
                t.then_inc(proj_done, 1)

            pe.wait_ge(proj_kept, 21)
            pe.wait_ge(u_made, 6)
            pe.wait_ge(ss_norm, 1)
            for t_, (rows_, _) in enumerate(VT):
                tr(psum[0:rows_, 2, P * t_:P * t_ + P], ps[:, P * t_:P * t_ + rows_], ident)
            for g in range(GROUPS):
                t = tr(psum[0:32, 3, P * g:P * g + P], ps[:, CACHED + 32 * g:CACHED + 32 * g + 32], ident)
            t.then_inc(ss_turned, 1)
            pe.wait_ge(ss_kept, 2)
            for bb in range(2):
                for s_, (rows_, g) in enumerate([(SAMPLES, g) for g in range(GROUPS)] + VT):
                    for q in range(4):
                        new = s_ < GROUPS
                        w = view((A_PTN if new else A_PTC) + P * (s_ if new else s_ - GROUPS) + 32 * q, 32, parts=rows_)
                        v = vS[0:SAMPLES, 4, 256 * g:256 * g + 256] if new else v_of(2 * q + bb)[0:rows_, s_ - GROUPS, :]
                        t = mm(psum[32 * q:32 * q + 32, 4 + bb, 0:256], w, v, start=s_ == 0,
                               stop=s_ == GROUPS + 3, tile_position=(0, 32 * q))
            t.then_inc(so_done, 1)
            pe.wait_ge(so_sum, 1)
            for c in range(4):
                t = tr(psum[:, 0, P * c:P * c + P], view(A_OS + P * c, P), ident)
            t.then_inc(so_turned, 1)

            def scores(n):
                i, h = n // 4, n % 4
                pe.wait_ge(qz_ready, n + 1)
                if n < 2:
                    pe.wait_ge(qz_zero, 2)
                if n == 0:
                    pe.wait_ge(masks_made, 6)
                    pe.wait_ge(so_kept, 8)
                if n:
                    pe.wait_ge(exp_done, n)
                at = 0
                for g in range(GROUPS):
                    lo = max(i - 1, 0) if g == 0 else 0
                    w = P * (i + 1 - lo)
                    mask_end = P + (2 * P if g == 0 else 2 * P + 4 * P * g)
                    done_ = 0
                    while done_ < w:
                        step = min(w - done_, 512 - at % 512)
                        out = psum[:, at // 512, at % 512:at % 512 + step]
                        mm(out, qz[h % 2][:, g, :], qkT[:, 6 + 2 * g + h // 2, P * lo + done_:P * lo + done_ + step],
                           start=True, stop=False)
                        o = mask_end - w + done_
                        t = mm(out, mb[:, 0:P], mb[:, o:o + step], start=False, stop=True)
                        at += step
                        done_ += step
                t.then_inc(s_done, 1)

            def weighted(n):
                h, hh = n % 4, n % 2
                pe.wait_ge(pt_kept, n + 1)
                if n >= 4:
                    pe.wait_ge(o_kept, n - 3)
                tiles = key_tiles(n)
                for t_, (g, j) in enumerate(tiles):
                    t = mm(psum[64 * hh:64 * hh + 64, 6 + (n // 2) % 2, 0:P],
                           vS[:, j, 256 * g + 64 * h:256 * g + 64 * h + 64], pT[n % 2][:, P * t_:P * t_ + P],
                           start=t_ == 0, stop=t_ == len(tiles) - 1)
                t.then_inc(o_done, 1)

            scores(0)
            for n in range(16):
                if n < 15:
                    scores(n + 1)
                pe.wait_ge(p_ready, n + 1)
                if n:
                    pe.wait_ge(pt_kept, n)
                w = len(key_tiles(n))
                sc = view(A_SC + 1280 * (n % 2), P * w)
                for t_ in range(w):
                    t = tr(psum[:, 3 + t_ // 4, P * (t_ % 4):P * (t_ % 4) + P], sc[:, P * t_:P * t_ + P], ident)
                t.then_inc(pt_done, 1)
                if n:
                    weighted(n - 1)
            weighted(15)

            def project(call, src, blocks, weights, done):
                for s, i in tiles_of(call):
                    r, b = ROWS[i], 2 * (s % 3)
                    if s >= 3:
                        pe.wait_ge(x_updated, TILES * (call - 1) + s - 2)
                    if s == 0:
                        for k in range(blocks):
                            if call == 3:
                                pe.wait_ge(swish_done, k + 1)
                            for q in range(4):
                                t = mm(psum[32 * q:32 * q + 32, b, 0:256], src[:, k, SEQ:TOK],
                                       weights(k, q // 2)[:, 256 * (q % 2):256 * (q % 2) + 256],
                                       start=k == 0, stop=k == blocks - 1, tile_position=(0, 32 * q))
                    for h in range(2 if s else 0):
                        for k in range(blocks):
                            t = mm(psum[0:r, b + h, :], src[:, k, P * i:P * i + r], weights(k, h),
                                   start=k == 0, stop=k == blocks - 1)
                    t.then_inc(done, 1)
                    if s:
                        turn(call, s - 1)
                turn(call, TILES - 1)
                pe.wait_ge(hT_ready, 10 * (call + 1))

            pe.wait_ge(wout_w, 16)
            pe.wait_ge(ya_made, 2)
            pe.wait_ge(so_kept, 8)
            pe.wait_ge(o_kept, 16)
            project(1, yT, 4, lambda k, h: ring[:, 3, D * k + 512 * h:D * k + 512 * h + 512], wo_done)

            def experts(n):
                hT = hT_of(2 * n + 1)
                for k in range(KD // 2):
                    for c in range(2):
                        for h in range(2):
                            o = V_RW + 64 * (KD * n + k + 4 * h)
                            t = mm(psum[64 * h:64 * h + 64, c, 0:HALF], sv[:, o:o + 64],
                                   hT[:, k + 4 * h, HALF * c:HALF * c + HALF], start=k == 0, stop=k == 3)
                t.then_inc(moe.routers, 1)
                pe.wait_ge(moe.routers_kept, n + 1)
                for i in range(TILES):
                    r = ROWS[i]
                    t = mm(psum[0:r, 4, 36 * i:36 * i + 36], view(M_R + P * i, r), cst[:, C_SEL:C_SEL + 36],
                           start=True, stop=True)
                t.then_inc(moe.logits, 1)
                pe.wait_ge(moe.picks, n + 1)
                mk = view(M_R + TOK + 180 + 40 + 4 * 160, 160)
                mm(psum[:, 5, 0:160], mean_of, mk, start=True, stop=True)
                mm(psum[:, 6, 0:160], cst[:, C_TRI:C_TRI + P], mk, start=True, stop=True).then_inc(moe.ranks, 1)
                stay_warm(12)
                pe.wait_ge(moe.places, n + 1)
                R = view(M_ROW, 10 * JOB, "p (i r) -> p i r", i=10)
                C = view(M_JOB, 480, "p (i j) -> p i j", i=10)
                for i in range(10):
                    r = ROWS[i // 2]
                    for h in range(2):
                        w = MORE if h else 2 * MORE
                        t = mm(psum[64 * h:64 * h + 64, 7, 0:w], R[0:r, i, :], C[0:r, i, 32 * h:32 * h + w],
                               start=i == 0, stop=i == 9)
                t.then_inc(moe.table, 1)
                stay_warm(7)
                pe.wait_ge(moe.jobs, n + 1)

                def turn_rows(it, v, first=False):
                    pe.wait_ge(moe.rows_in[v % 3], 16 * it + 16 * (n * len(range(v % 3, 16, 3)) + v // 3 + 1))
                    if not first:
                        pe.wait_ge(moe.rows_kept, MSLOTS * it + (2 * v + 32 * n))
                    rows_ = xg[v % 3].rearrange("t (d k) -> t k d", k=KD)
                    for k in range(KD):
                        o = P * (k % 4)
                        t = tr(psum[:, 3 + 4 * (k // 4), o:o + P], rows_[:, k, :], ident)
                    t.then_inc(moe.rows_turned, 1)

                def gate_up(it, u, first):
                    pe.wait_ge(moe.w_in[u], 16 * it + (16 * loads_before(n, u) + 16))
                    pe.wait_ge(moe.rows_kept, MSLOTS * it + (EXPERTS * n + 2 * (u // 2) + 2))
                    if not first or u >= 2:
                        pe.wait_ge(moe.act_ready, MSLOTS * it + (EXPERTS * n + u - 1))
                    w = slot(u)[:, 0:4096].rearrange("p (k f c) -> p k f c", k=KD, f=2)
                    for k in range(KD):
                        for f in range(2):
                            t = mm(psum[64 * f:64 * f + 64, u % 2, 0:2 * P],
                                   xt[:, k, 64 * (u % 2):64 * (u % 2) + 64], w[:, k, f, :],
                                   start=k == 0, stop=k == KD - 1)
                    t.then_inc(moe.gu_done, 1)

                def further(it, u, last):
                    def count(what):
                        return pe.value_load(jt[0:1, bass.ds(MSLOTS * it + (EXPERTS * what + u), 1)],
                                                min_val=0, max_val=MORE)

                    chunks = count(0)
                    w = slot(u)[:, 0:4096].rearrange("p (k f c) -> p k f c", k=KD, f=2)
                    with pe.If(chunks > 0):
                        before = count(1)
                        with pe.Fori(0, chunks) as c:
                            pe.wait_ge(moe.rows_kept, MSLOTS * it + (EXPERTS * n + 2 * min(u // 2 + 2, last)))
                            pe.wait_ge(ex[n].rows, 16 * (before + c) + 16)
                            pe.sem_inc(moe.seen, 1)
                            rows_ = xe.rearrange("t (d k) -> t k d", k=KD)
                            for k in range(KD):
                                t = tr(psum[:, 7, JOB * k:JOB * k + JOB], rows_[:, k, :], ident[0:JOB, 0:JOB])
                            t.then_inc(ex[n].turned, 1)
                            pe.wait_ge(ex[n].kept, before + c + 1)
                            pe.wait_ge(ex[n].turns_kept, before + c + 1)
                            for k in range(KD):
                                for f in range(2):
                                    t = mm(psum[64 * f:64 * f + 64, 6, 0:2 * P], xeT[:, k, :], w[:, k, f, :],
                                           start=k == 0, stop=k == KD - 1)
                            t.then_inc(ex[n].gu, 1)
                            pe.wait_ge(ex[n].act, before + c + 1)
                            tr(psum[:, 7, 0:P], ave, ident).then_inc(ex[n].at, 1)
                            pe.wait_ge(ex[n].atk, before + c + 1)
                            for k in range(2):
                                for h in range(2):
                                    o = 4096 + D * k + 512 * h
                                    t = mm(psum[64 * h:64 * h + 64, 6, :], aTe[:, 64 * k:64 * k + 64],
                                           slot(u)[:, o:o + 512], start=k == 0, stop=k == 1)
                            t.then_inc(ex[n].down, 1)

                def turn_act(it, u, first):
                    pe.wait_ge(moe.act_ready, MSLOTS * it + (EXPERTS * n + u + 1))
                    if not first or u:
                        pe.wait_ge(moe.at_kept, MSLOTS * it + (EXPERTS * n + u))
                    tr(psum[:, 2, 0:P], av[u % 2], ident).then_inc(moe.at_done, 1)

                def down(it, u, first):
                    pe.wait_ge(moe.at_kept, MSLOTS * it + (EXPERTS * n + u + 1))
                    if not first or u >= 2:
                        pe.wait_ge(moe.y_kept, MSLOTS * it + (EXPERTS * n + u - 1))
                    for k in range(2):
                        for h in range(2):
                            o = 4096 + D * k + 512 * h
                            t = mm(psum[64 * h:64 * h + 64, 4 + u % 2, :], aT[:, 64 * k:64 * k + 64],
                                   slot(u)[:, o:o + 512], start=k == 0, stop=k == 1)
                    t.then_inc(moe.down_done, 1)

                def body(it, first, jobs):
                    for u in range(jobs + 1):
                        if u < jobs:
                            gate_up(it, u, first)
                        if u % 2 and jobs == MSLOTS:
                            turn_rows(it, u // 2 + 1)
                        if u:
                            turn_act(it, u - 1, first)
                            further(it, u - 1, 4 if jobs == MSLOTS else 1)
                            down(it, u - 1, first)

                pe.sem_inc(ex[n].turned, 1)
                turn_rows(0, 0, True)
                over_experts(pe, body)

            experts(0)

            for i in range(TILES):
                turn(2, i)
                stay_warm(3, 6)
            pe.wait_ge(hT_ready, 30)
            hT2 = hT_of(2)

            def conv(n):
                c = PE_CONV[n]
                pe.wait_ge(u_ready, c + 1)
                pe.wait_ge(diag_made, CK * (n + 1))
                for j in range(CK):
                    t = mm(psum[:, 6 + n, :], diag(n, j), cu[:, c, j:j + SEQ], start=j == 0, stop=j == CK - 1)
                t.then_inc(pe_conv_done, 1)

            for m in range(2 * KD):
                if m == 12:
                    conv(0)
                c, gate = m // 2, m % 2 == 0
                b = 2 * (m % 3)
                if m % 4 == 0:
                    pe.wait_ge(dense_w[m // 4], 32)
                if m >= 3:
                    p = m - 3
                    if p % 2 == 0:
                        pe.wait_ge(sig_ready, p // 2 + 1)
                    else:
                        pe.wait_ge(u_ready, p // 2 + 1)
                w = ring[:, m // 4, 0:4096].rearrange("p (k c) -> p k c", k=KD)
                o = (256 if gate else 0) + P * (c % 2)
                for h in range(2):
                    for k in range(KD):
                        t = mm(psum[:, b + h, 0:HALF], w[:, k, o:o + P], hT2[:, k, HALF * h:HALF * h + HALF],
                               start=k == 0, stop=k == KD - 1)
                t.then_inc(z_done, 1)
            conv(1)
            pe.wait_ge(u_ready, KD)
            for k in range(KD):
                wait_conv(pe, k)
                for h in range(2):
                    t = mm(psum[:, 2 + h, 0:HALF], mean_of, cT[:, k, HALF * h:HALF * h + HALF], start=k == 0,
                           stop=k == KD - 1)
            t.then_inc(mean_done, 1)
            for k in range(KD):
                pe.wait_ge(squared, k + 1)
                for h in range(2):
                    t = mm(psum[:, 4 + h, 0:HALF], mean_of, hT2[:, k, HALF * h:HALF * h + HALF], start=k == 0,
                           stop=k == KD - 1)
            t.then_inc(var_done, 1)
            stay_warm(10, 6)
            for c in range(2):
                pe.wait_ge(later_w[c], 32)
            project(3, cT, KD, lambda k, h: ring[:, h, 512 * k:512 * k + 512], pw2_done)
            experts(1)


def constants():
    c = np.zeros((P, C_END), np.float32)
    p = np.arange(P)
    c[:, C_ID:C_ID + P] = np.eye(P)
    c[:, C_TRI:C_TRI + P] = p[:, None] < p[None, :]
    c[:, C_MEAN:C_MEAN + P] = 1.0 / D
    neg = np.float32(NEG)
    b, i = p // 16, p % 4
    cols = np.arange(CACHED)
    ok = np.zeros((P, CACHED + 96), bool)
    ok[:, 0:128] = cols[None, 0:128] >= i[:, None]
    ok[:, 128:384] = (cols[None, 0:256] % 4) == i[:, None]
    ok[:, 384:448] = (cols[None, 0:64] % 4) == i[:, None]
    new = np.arange(32)
    for g in range(3):
        mine = (new[None] // 4) == b[:, None]
        ok[:, CACHED + 32 * g:CACHED + 32 * g + 32] = mine & (
            (new[None] % 4 <= i[:, None]) if g == 0 else (new[None] % 4 == i[:, None]))
    c[:, C_SM:C_SM + 544] = np.where(ok, 0, neg)
    c[:, C_IOTAP:C_IOTAP + 32] = np.arange(32) + 100
    c[:, C_E64:C_E64 + 32] = 64 * np.arange(32)
    c[:, C_THR:C_THR + 8] = 64 * np.arange(1, 9)
    c[:, C_VALID:C_VALID + 5] = 1
    c[SAMPLES:, C_VALID + 4] = 0
    c[:, C_ROW:C_ROW + JOB] = np.arange(JOB)
    c[:, C_JOB:C_JOB + 48] = JOB * np.concatenate([np.arange(0, 32, 2), np.arange(32, 48), np.arange(1, 32, 2)])
    c[:, C_TOKEN:C_TOKEN + TILES] = p[:, None] + P * np.arange(TILES)
    for h in range(2):
        c[64 * h:64 * h + 36, C_SEL:C_SEL + 36] = np.eye(36)
    return c


def prompt_masks():
    p = np.arange(P)
    q, k = p[:, None], p[None, :]
    ok = [k >= q, k <= q]
    for dil in (4, 16):
        same = q % dil == k % dil
        ok += [same, same & (k <= q)]
    return np.concatenate([np.where(o, 0, NEG) for o in ok], 1).astype(np.float32)


def blocks_of(w):
    k, n = w.shape[0] // P, w.shape[1]
    return w.reshape(k, P, n).transpose(1, 0, 2).reshape(P, k * n)


def kernel(**inputs):
    import concourse.bacc as bacc
    from concourse.bass_utils import run_bass_kernel_spmd

    a = {k: np.asarray(v) for k, v in inputs.items()}
    cat, con = np.concatenate, np.ascontiguousarray
    arrays = {}
    arrays["x_in"] = cat([a["x_prompt"].reshape(SEQ, D), a["x_sample"].reshape(SAMPLES, D)])
    w = a["w_in"][0]
    arrays["w_mix0"] = np.stack([blocks_of(con(w[:, c:c + 768])) for c in (768, 1536, 2304, 0)])
    kv = np.zeros((3, P, SLOT), np.float32)
    caches = [a["cache_kv_w128"][0], a["cache_kv_w512"][0],
              a["cache_kv_w2048"][0].reshape(DEC_B, 16, 16, 2, 4, HD)[:, :, 0:4].reshape(DEC_B, 64, 2, 4, HD)]
    for b in range(DEC_B):
        o = KV * (b % 3)
        for g, c in enumerate(caches):
            kt = c[b, :, 0].reshape(KEYS[g], 2, P).transpose(2, 1, 0)
            img = kv[b // 3, :, o:o + 2 * CACHED].reshape(P, 2, CACHED)
            img[:, :, KOFF[g]:KOFF[g] + KEYS[g]] = kt
            kv[b // 3, :, o:o + 2 * CACHED] = img.reshape(P, 2 * CACHED)
        o += 2 * CACHED
        v = [c[b, :, 1].reshape(KEYS[g], 256) for g, c in enumerate(caches)]
        for t, part in enumerate((v[0], v[1][0:P], v[1][P:], v[2])):
            kv[b // 3, 0:len(part), o + 256 * t:o + 256 * t + 256] = part
    arrays["kv_in"] = kv
    arrays["w_out"] = blocks_of(a["w_out"][0])
    w = a["w_pw1"][0]
    arrays["w_pw1"] = np.stack([blocks_of(cat([w[:, 256 * c:256 * c + 256], w[:, D + 256 * c:D + 256 * c + 256]], 1))
                                for c in range(4)])
    arrays["w_pw2"] = np.stack([blocks_of(con(a["w_pw2"][0][:, 512 * c:512 * c + 512])) for c in range(2)])
    moe = np.empty((2, EXPERTS, P, SLOT), np.float32)
    gu = moe[..., 0:4096].reshape(2, EXPERTS, P, KD, 2, 2, P)
    gu[:, :, :, :, :, 0] = a["w_gate"].reshape(2, EXPERTS, P, KD, 2, P)
    gu[:, :, :, :, :, 1] = a["w_up"].reshape(2, EXPERTS, P, KD, 2, P)
    moe[..., 0:4096] = gu.reshape(2, EXPERTS, P, 4096)
    moe[..., 4096:] = a["w_down"].reshape(2, EXPERTS, 2, P, D).transpose(0, 1, 3, 2, 4).reshape(2, EXPERTS, P, 2 * D)
    arrays["w_moe"] = moe

    def col(v):
        return v.reshape(-1, P).T

    def spread(v):
        return np.broadcast_to(v.reshape(1, -1), (P, v.size))

    router = [cat([a["w_router_group"][n], a["w_router_expert"][n], np.zeros((D, 28), np.float32)], 1)
              for n in range(2)]
    arrays["smalls"] = con(cat(
        [col(a["g_mix"][0]), col(a["g_ffn"][0]), col(a["g_mix"][1]), col(a["g_ffn"][1]),
         a["g_ffn"][0].reshape(P, KD), a["g_ffn"][1].reshape(P, KD), col(a["b_pw1"][0]), col(a["dw_b"][0]),
         col(a["ln_g"][0]), col(a["ln_b"][0]),
         a["conv_a_w"][0].reshape(3, 2, P).transpose(2, 1, 0).reshape(P, 6),
         a["dw_w"][0].reshape(CK, KD, P).transpose(2, 1, 0).reshape(P, KD * CK)]
        + [spread(cat([a["b_router_group"][n], a["b_router_expert"][n]])) for n in range(2)]
        + [blocks_of(r) for r in router], 1))
    arrays["consts"] = constants()
    arrays["masks"] = prompt_masks()
    arrays["rows"] = np.stack([a["b_pw2"][0], a["g_final"]])
    arrays["st_a"] = con(a["state_shortconv"][0].reshape(DEC_B, 2, 2, P).transpose(3, 2, 0, 1))
    arrays["st_c"] = con(a["state_conformer"][0].reshape(DEC_B, CK - 1, KD, P).transpose(3, 2, 0, 1))
    outs = {"y": (TOK, D), "k": (P, 6, TOK), "v": (TOK, 768), "ua_p": (P, 2, 2), "ua_s": (P, 2, DEC_B, 2),
            "uc_p": (P, KD, CK - 1), "uc_s": (P, KD, DEC_B, CK - 1)}

    nc = bacc.Bacc("TRN2", target_bir_lowering=False, num_devices=1)
    args = [nc.dram_tensor(n, v.shape, F32, kind="ExternalInput").ap() for n, v in arrays.items()]
    args += [nc.dram_tensor("out_" + n, s, F32, kind="ExternalOutput").ap() for n, s in outs.items()]
    program(nc, *args)
    r = run_bass_kernel_spmd(nc, [arrays], core_ids=[0]).results[0]
    y, k, v, ua_p, ua_s, uc_p, uc_s = (np.asarray(r["out_" + n]) for n in outs)

    kv = np.stack([k.transpose(2, 1, 0).reshape(TOK, 3, 4, HD), v.reshape(TOK, 3, 4, HD)], 1)
    prompt, new = kv[0:SEQ], kv[SEQ:].reshape(DEC_B, DEC_T, 2, 3, 4, HD)
    p_kv = [con(prompt[SEQ - n:, :, g])[None, None] for g, n in enumerate((128, SEQ, SEQ))]
    s_kv = [con(new[:, :, :, g])[None] for g in range(3)]
    return (y[0:SEQ].reshape(1, SEQ, D), y[SEQ:].reshape(DEC_B, DEC_T, D),
            con(ua_p.transpose(2, 1, 0)).reshape(1, 1, 2, 256), *p_kv,
            con(uc_p.transpose(2, 1, 0)).reshape(1, 1, CK - 1, D),
            con(ua_s.transpose(2, 3, 1, 0)).reshape(1, DEC_B, 2, 256), *s_kv,
            con(uc_s.transpose(2, 3, 1, 0)).reshape(1, DEC_B, CK - 1, D))
```
